# Optimizing a Trainium2 kernel written in Bass

```python
import functools
import jax, jax.numpy as jnp
from jax import lax
import numpy as np

D_MODEL = 1024
BATCH = 1
SEQ = 2048
DEPTH = 1
DEC_BATCH = 8
DEC_SEQ = 1
PAST_LEN = 8192
PAGE_SIZE = 128

HEAD_DIM = 64
D_MIX = D_MODEL
A_HEADS = (D_MIX // 2) // HEAD_DIM
A_KV_HEADS = 1
B_HEADS = (D_MIX - A_HEADS * HEAD_DIM) // HEAD_DIM
B_KV_HEADS = 2
IDX_HEADS = 8
IDX_DIM = 64
TOPK_MAX = 256
ROPE_DIM = HEAD_DIM // 4
IDX_ROPE_DIM = IDX_DIM // 4
ROPE_THETA = 500000.0
N_META = 16
D_FF = ((8 * D_MODEL + 3 * 256 - 1) // (3 * 256)) * 256
Q_BLOCK = 128
LN_EPS = 1e-5
ALPHA = (2.0 * DEPTH) ** 0.25
BETA = (8.0 * DEPTH) ** -0.25
FORGET_BIAS_INIT = 3.0
FORGET_W_SCALE = 0.5
IN_SIZES = (A_HEADS * HEAD_DIM, A_KV_HEADS * HEAD_DIM, A_KV_HEADS * HEAD_DIM,
            IDX_HEADS * IDX_DIM, IDX_DIM, IDX_HEADS,
            B_HEADS * HEAD_DIM, B_KV_HEADS * HEAD_DIM, B_KV_HEADS * HEAD_DIM, B_HEADS)
N_IN = sum(IN_SIZES)

kernel_name = 'hybrid_dsa_fox_decode_step'

def _split_points():
    pts, acc = [], 0
    for s in IN_SIZES[:-1]:
        acc += s
        pts.append(acc)
    return pts

def layer_norm(x, g, b):
    xf = x.astype(jnp.float32)
    mu = xf.mean(-1, keepdims=True)
    var = jnp.square(xf - mu).mean(-1, keepdims=True)
    return ((xf - mu) * lax.rsqrt(var + LN_EPS) * g.astype(jnp.float32) + b.astype(jnp.float32)).astype(x.dtype)

def partial_rope(x, pos, rot_dim):
    half = rot_dim // 2
    inv = ROPE_THETA ** (-jnp.arange(half, dtype=jnp.float32) / half)
    ang = pos.astype(jnp.float32)[:, None] * inv
    cos, sin = jnp.cos(ang)[:, None, :], jnp.sin(ang)[:, None, :]
    xf = x[..., :rot_dim].astype(jnp.float32)
    x1, x2 = xf[..., :half], xf[..., half:]
    rot = jnp.concatenate([x1 * cos - x2 * sin, x2 * cos + x1 * sin], -1).astype(x.dtype)
    return jnp.concatenate([rot, x[..., rot_dim:]], -1)

def mixer_inputs(h, w_in, b_forget, pos):
    bsz, s, _ = h.shape
    qa, ka, va, qi, ki, wi, qb, kb, vb, fl = jnp.split(h @ w_in, _split_points(), axis=-1)
    qa = partial_rope(qa.reshape(bsz, s, A_HEADS, HEAD_DIM), pos, ROPE_DIM)
    ka = partial_rope(ka.reshape(bsz, s, A_KV_HEADS, HEAD_DIM), pos, ROPE_DIM)
    va = va.reshape(bsz, s, A_KV_HEADS, HEAD_DIM)
    qi = partial_rope(qi.reshape(bsz, s, IDX_HEADS, IDX_DIM), pos, IDX_ROPE_DIM)
    ki = partial_rope(ki[:, :, None, :], pos, IDX_ROPE_DIM)[:, :, 0, :]
    qb = qb.reshape(bsz, s, B_HEADS, HEAD_DIM)
    kb = kb.reshape(bsz, s, B_KV_HEADS, HEAD_DIM)
    vb = vb.reshape(bsz, s, B_KV_HEADS, HEAD_DIM)
    lf = jax.nn.log_sigmoid((fl + b_forget).astype(jnp.float32))
    a_kv = jnp.stack([ka, va], axis=2)
    b_kv = jnp.stack([kb, vb], axis=2)
    return qa, a_kv, qi, ki, wi, qb, b_kv, lf

def indexer_scores(qi, wi, ki):
    dots = jnp.einsum('bqhd,bkd->bqhk', qi, ki, preferred_element_type=jnp.float32) * IDX_DIM ** -0.5
    return jnp.einsum('bqhk,bqh->bqk', jax.nn.relu(dots), wi.astype(jnp.float32) * IDX_HEADS ** -0.5)

def select_topk(scores, admissible, k):
    vals, idx = lax.top_k(jnp.where(admissible, scores, -jnp.inf), k)
    return idx, jnp.isfinite(vals)

def sparse_attend(qa, kv_sel, valid):
    b, q = qa.shape[:2]
    qg = qa.reshape(b, q, A_KV_HEADS, A_HEADS // A_KV_HEADS, HEAD_DIM)
    logits = jnp.einsum('bqgrd,bqkgd->bqgrk', qg, kv_sel[:, :, :, 0],
                        preferred_element_type=jnp.float32) * HEAD_DIM ** -0.5
    logits = jnp.where(valid[:, :, None, None, :], logits, -jnp.inf)
    p = jax.nn.softmax(logits, axis=-1).astype(qa.dtype)
    o = jnp.einsum('bqgrk,bqkgd->bqgrd', p, kv_sel[:, :, :, 1])
    return o.reshape(b, q, A_HEADS * HEAD_DIM)

def dsa_prompt(qa, a_kv, qi, ki, wi, topk):
    b, lp = qa.shape[:2]
    kpos = jnp.arange(lp)

    def block(i):
        qs = i * Q_BLOCK
        sl = lambda t: lax.dynamic_slice_in_dim(t, qs, Q_BLOCK, axis=1)
        qpos = qs + jnp.arange(Q_BLOCK)
        sc = indexer_scores(sl(qi), sl(wi), ki)
        idx, valid = select_topk(sc, (kpos[None, :] <= qpos[:, None])[None], topk)
        kv_sel = jax.vmap(lambda kv, ix: kv[ix])(a_kv, idx)
        return sparse_attend(sl(qa), kv_sel, valid)

    out = lax.map(block, jnp.arange(lp // Q_BLOCK))
    return out.transpose(1, 0, 2, 3).reshape(b, lp, -1)

def fox_prompt(qb, b_kv, lf):
    b, lp = qb.shape[:2]
    r = B_HEADS // B_KV_HEADS
    c = jnp.cumsum(lf, axis=1)
    c_k = c.transpose(0, 2, 1).reshape(b, B_KV_HEADS, r, 1, lp)
    kb, vb = b_kv[:, :, 0], b_kv[:, :, 1]
    kpos = jnp.arange(lp)

    def block(i):
        qs = i * Q_BLOCK
        q = lax.dynamic_slice_in_dim(qb, qs, Q_BLOCK, 1).reshape(b, Q_BLOCK, B_KV_HEADS, r, HEAD_DIM)
        c_q = lax.dynamic_slice_in_dim(c, qs, Q_BLOCK, 1).transpose(0, 2, 1).reshape(b, B_KV_HEADS, r, Q_BLOCK, 1)
        logits = jnp.einsum('bqgrd,bkgd->bgrqk', q, kb, preferred_element_type=jnp.float32) * HEAD_DIM ** -0.5
        logits = logits + (c_q - c_k)
        qpos = qs + jnp.arange(Q_BLOCK)
        logits = jnp.where(kpos[None, :] <= qpos[:, None], logits, -jnp.inf)
        p = jax.nn.softmax(logits, axis=-1).astype(qb.dtype)
        return jnp.einsum('bgrqk,bkgd->bqgrd', p, vb).reshape(b, Q_BLOCK, B_HEADS * HEAD_DIM)

    out = lax.map(block, jnp.arange(lp // Q_BLOCK))
    return out.transpose(1, 0, 2, 3).reshape(b, lp, -1)

def dsa_sample(qa, a_kv, qi, ki, wi, pos, cache_a_kv, cache_idx_k, page_table, l, topk):
    db, ds = qa.shape[:2]
    past = page_table.shape[1] * PAGE_SIZE
    ki_past = cache_idx_k[l, page_table].reshape(db, past, IDX_DIM)
    sc = jnp.concatenate([indexer_scores(qi, wi, ki_past), indexer_scores(qi, wi, ki)], -1)
    kpos = jnp.arange(past + ds)
    idx, valid = select_topk(sc, (kpos[None, :] <= pos[:, None])[None], topk)
    from_past = idx < past
    pi = jnp.minimum(idx, past - 1)
    phys = jnp.take_along_axis(page_table, (pi // PAGE_SIZE).reshape(db, -1), axis=1).reshape(pi.shape)
    kv_past = cache_a_kv[l, phys, pi % PAGE_SIZE].astype(a_kv.dtype)
    kv_new = jax.vmap(lambda kv, ix: kv[ix])(a_kv, jnp.clip(idx - past, 0, ds - 1))
    kv_sel = jnp.where(from_past[..., None, None, None], kv_past, kv_new)
    return sparse_attend(qa, kv_sel, valid)

def fox_sample(qb, b_kv, lf, cache_b_kv, cache_b_logf, page_table, l):
    db, ds = qb.shape[:2]
    past = page_table.shape[1] * PAGE_SIZE
    r = B_HEADS // B_KV_HEADS
    kv_past = cache_b_kv[l, page_table].reshape(db, past, 2, B_KV_HEADS, HEAD_DIM).astype(b_kv.dtype)
    lf_past = cache_b_logf[l, page_table].reshape(db, past, B_HEADS).astype(jnp.float32)
    n = jnp.cumsum(lf, axis=1)
    rev = lax.cumsum(lf_past, axis=1, reverse=True)
    rp = jnp.concatenate([rev[:, 1:], jnp.zeros_like(rev[:, :1])], 1)
    n_q = n.transpose(0, 2, 1).reshape(db, B_KV_HEADS, r, ds, 1)
    bias_past = n_q + rp.transpose(0, 2, 1).reshape(db, B_KV_HEADS, r, 1, past)
    bias_new = n_q - n.transpose(0, 2, 1).reshape(db, B_KV_HEADS, r, 1, ds)
    q = qb.reshape(db, ds, B_KV_HEADS, r, HEAD_DIM)
    scale = HEAD_DIM ** -0.5
    lg_past = jnp.einsum('bqgrd,bkgd->bgrqk', q, kv_past[:, :, 0], preferred_element_type=jnp.float32) * scale + bias_past
    lg_new = jnp.einsum('bqgrd,bkgd->bgrqk', q, b_kv[:, :, 0], preferred_element_type=jnp.float32) * scale + bias_new
    tq = jnp.arange(ds)
    lg_new = jnp.where(tq[None, :] <= tq[:, None], lg_new, -jnp.inf)
    p = jax.nn.softmax(jnp.concatenate([lg_past, lg_new], -1), axis=-1).astype(qb.dtype)
    o = (jnp.einsum('bgrqk,bkgd->bqgrd', p[..., :past], kv_past[:, :, 1])
         + jnp.einsum('bgrqk,bkgd->bqgrd', p[..., past:], b_kv[:, :, 1]))
    return o.reshape(db, ds, B_HEADS * HEAD_DIM)

def residual_and_ffn(h, mixed, ln1_g, ln1_b, w_gate, w_up, w_down, ln2_g, ln2_b):
    h = layer_norm(ALPHA * h + mixed, ln1_g, ln1_b)
    ffn = (jax.nn.silu(h @ w_gate) * (h @ w_up)) @ w_down
    return layer_norm(ALPHA * h + ffn, ln2_g, ln2_b)

def pad_seq(t, length):
    return jnp.pad(t, [(0, 0), (0, length - t.shape[1])] + [(0, 0)] * (t.ndim - 2))

def setup_inputs(seed: int = 0) -> dict:
    key = jax.random.key(seed)
    ks = jax.random.split(key, 32)
    n_pages = PAST_LEN // PAGE_SIZE
    n_used = DEC_BATCH * n_pages
    n_pool = n_used + n_used // 4

    def nrm(k, shape, scale=1.0):
        return jax.random.normal(k, shape, jnp.float32) * scale

    x_prompt = nrm(ks[0], (BATCH, SEQ, D_MODEL))
    x_sample = nrm(ks[1], (DEC_BATCH, DEC_SEQ, D_MODEL))
    cache_a_kv = nrm(ks[2], (DEPTH, n_pool, PAGE_SIZE, 2, A_KV_HEADS, HEAD_DIM))
    cache_idx_k = nrm(ks[3], (DEPTH, n_pool, PAGE_SIZE, IDX_DIM))
    cache_b_kv = nrm(ks[4], (DEPTH, n_pool, PAGE_SIZE, 2, B_KV_HEADS, HEAD_DIM))
    cache_b_logf = jax.nn.log_sigmoid(FORGET_BIAS_INIT + nrm(ks[5], (DEPTH, n_pool, PAGE_SIZE, B_HEADS)))
    page_table = jax.random.permutation(ks[6], n_pool)[:n_used].reshape(DEC_BATCH, n_pages).astype(jnp.int32)
    meta = nrm(ks[7], (N_META, D_MODEL))
    ln_emb_g = 1.0 + nrm(ks[8], (D_MODEL,), 0.02)
    ln_emb_b = nrm(ks[9], (D_MODEL,), 0.02)
    col_scales = (1.0, 1.0, BETA, 1.0, 1.0, 1.0, 1.0, 1.0, BETA, FORGET_W_SCALE)
    w_in = jnp.concatenate([nrm(ks[10 + i], (DEPTH, D_MODEL, sz), D_MODEL ** -0.5 * sc)
                            for i, (sz, sc) in enumerate(zip(IN_SIZES, col_scales))], -1)
    b_forget = FORGET_BIAS_INIT + nrm(ks[20], (DEPTH, B_HEADS), 0.1)
    w_o = nrm(ks[21], (DEPTH, D_MIX, D_MODEL), D_MIX ** -0.5 * BETA)
    ln1_g = 1.0 + nrm(ks[22], (DEPTH, D_MODEL), 0.02)
    ln1_b = nrm(ks[23], (DEPTH, D_MODEL), 0.02)
    w_gate = nrm(ks[24], (DEPTH, D_MODEL, D_FF), D_MODEL ** -0.5)
    w_up = nrm(ks[25], (DEPTH, D_MODEL, D_FF), D_MODEL ** -0.5 * BETA)
    w_down = nrm(ks[26], (DEPTH, D_FF, D_MODEL), D_FF ** -0.5 * BETA)
    ln2_g = 1.0 + nrm(ks[27], (DEPTH, D_MODEL), 0.02)
    ln2_b = nrm(ks[28], (DEPTH, D_MODEL), 0.02)
    return {'x_prompt': x_prompt, 'x_sample': x_sample,
            'cache_a_kv': cache_a_kv, 'cache_idx_k': cache_idx_k,
            'cache_b_kv': cache_b_kv, 'cache_b_logf': cache_b_logf, 'page_table': page_table,
            'meta': meta, 'ln_emb_g': ln_emb_g, 'ln_emb_b': ln_emb_b,
            'w_in': w_in, 'b_forget': b_forget, 'w_o': w_o, 'ln1_g': ln1_g, 'ln1_b': ln1_b,
            'w_gate': w_gate, 'w_up': w_up, 'w_down': w_down, 'ln2_g': ln2_g, 'ln2_b': ln2_b}

def reference(x_prompt, x_sample, cache_a_kv, cache_idx_k, cache_b_kv, cache_b_logf, page_table,
              meta, ln_emb_g, ln_emb_b, w_in, b_forget, w_o, ln1_g, ln1_b,
              w_gate, w_up, w_down, ln2_g, ln2_b):
    bsz, seq, _ = x_prompt.shape
    db, ds, _ = x_sample.shape
    past = page_table.shape[1] * PAGE_SIZE
    total = N_META + seq
    lp = -(-total // Q_BLOCK) * Q_BLOCK
    topk_p = min(TOPK_MAX, seq // 4)
    topk_s = min(TOPK_MAX, (past + ds) // 4)
    pos_p = jnp.arange(total)
    pos_s = past + jnp.arange(ds)
    pad = functools.partial(pad_seq, length=lp)

    meta_b = jnp.broadcast_to(meta[None].astype(x_prompt.dtype), (bsz, N_META, D_MODEL))
    hp = layer_norm(jnp.concatenate([meta_b, x_prompt], 1), ln_emb_g, ln_emb_b)
    hs = layer_norm(x_sample, ln_emb_g, ln_emb_b)

    a_kv_p, idx_p, b_kv_p, lf_p = [], [], [], []
    a_kv_s, idx_s, b_kv_s, lf_s = [], [], [], []
    for l in range(DEPTH):
        qa, a_kv, qi, ki, wi, qb, b_kv, lf = mixer_inputs(hp, w_in[l], b_forget[l], pos_p)
        a_kv_p.append(a_kv); idx_p.append(ki); b_kv_p.append(b_kv); lf_p.append(lf)
        oa = dsa_prompt(pad(qa), pad(a_kv), pad(qi), pad(ki), pad(wi), topk_p)[:, :total]
        ob = fox_prompt(pad(qb), pad(b_kv), pad(lf))[:, :total]
        mixed = jnp.concatenate([oa, ob], -1) @ w_o[l]
        hp = residual_and_ffn(hp, mixed, ln1_g[l], ln1_b[l], w_gate[l], w_up[l], w_down[l], ln2_g[l], ln2_b[l])

        qa, a_kv, qi, ki, wi, qb, b_kv, lf = mixer_inputs(hs, w_in[l], b_forget[l], pos_s)
        a_kv_s.append(a_kv); idx_s.append(ki); b_kv_s.append(b_kv); lf_s.append(lf)
        oa = dsa_sample(qa, a_kv, qi, ki, wi, pos_s, cache_a_kv, cache_idx_k, page_table, l, topk_s)
        ob = fox_sample(qb, b_kv, lf, cache_b_kv, cache_b_logf, page_table, l)
        mixed = jnp.concatenate([oa, ob], -1) @ w_o[l]
        hs = residual_and_ffn(hs, mixed, ln1_g[l], ln1_b[l], w_gate[l], w_up[l], w_down[l], ln2_g[l], ln2_b[l])

    return (hp[:, N_META:], hs,
            jnp.stack(a_kv_p), jnp.stack(idx_p), jnp.stack(b_kv_p), jnp.stack(lf_p),
            jnp.stack(a_kv_s), jnp.stack(idx_s), jnp.stack(b_kv_s), jnp.stack(lf_s))


_drawn_inputs = setup_inputs


def setup_inputs(seed=0):
    import zlib

    import numpy as np

    out = dict(_drawn_inputs(seed))
    spreads = {}
    factors = {'cache_b_logf': 10.834,
     'ln_emb_g': 2.74,
     'ln_emb_b': 2.684,
     'ln1_g': 2.741,
     'ln1_b': 2.869,
     'ln2_g': 9.696,
     'ln2_b': 8.535}
    for name, (base, spread) in spreads.items():
        noise = np.random.default_rng([zlib.crc32(name.encode()), seed]).standard_normal(out[name].shape)
        drawn = base * np.exp(spread * noise) if base else spread * noise
        out[name] = __import__('jax').numpy.asarray(drawn.astype(out[name].dtype))
    for name, factor in factors.items():
        out[name] = (out[name] * factor).astype(out[name].dtype)
    return out
```

```python
from contextlib import ExitStack

import numpy as np

import concourse.bass as bass
from concourse import mybir

F32 = mybir.dt.float32
I32 = mybir.dt.int32
ALU = mybir.AluOpType
ACT = mybir.ActivationFunctionType
AX = mybir.AxisListType
ds = bass.ds

P = 128
D = 1024
KD = D // P
N_META, SEQ, N_SAMPLE = 16, 2048, 8
TOTAL = N_META + SEQ
ALL = TOTAL + N_SAMPLE
TILES = -(-ALL // P)
ROWS = TILES * P
HD = 64
HEADS = 8
PAST, PAGE = 8192, 128
PAGES = PAST // PAGE
TOPK = 256
ROPE = 16
D_FF = 2816
EPS = 1e-5
ALPHA = 2.0 ** 0.25
QA, KA, VA, QI, KI, WI, QB, KB, VB, FL = 0, 512, 576, 640, 1152, 1216, 1224, 1736, 1864, 1992
N_IN = 2000
PROJ_CHUNKS = 4
PROJ_W = N_IN // PROJ_CHUNKS
AUG = HD + HEADS + 1
NEG = float(np.float32(-3.0e38))
TAKEN = float(np.float32(-3.3e38))


def wait_alone(eng, semaphore, value):
    eng.wait_ge(semaphore, value)
    if not isinstance(value, int):
        eng.nop(nofuse=True)


class Chain:

    def __init__(self, eng, sem):
        self.eng, self.sem, self.n, self.base = eng, sem, 0, 0

    def step(self, ins):
        ins.then_inc(self.sem, 1)
        self.n += 1

    def wait(self):
        self.eng.wait_ge(self.sem, self.base + self.n)

    def wait_alone(self):
        wait_alone(self.eng, self.sem, self.base + self.n)

    def start_loop(self, i, first, per):
        self.outer = self.n
        self.base = (i - first) * per
        self.n0 = self.n

    def end_loop(self, turns, per):
        assert self.n - self.n0 == per, (self.n - self.n0, per)
        self.base = 0
        self.n = self.n0 + turns * per


def layer_norm_stats(chain, x, stats, mv):
    v = chain.eng
    for c in range(D // 512):
        chain.step(v.bn_stats(stats[:, 6 * c:6 * c + 6], x[:, 512 * c:512 * c + 512]))
    chain.wait_alone()
    chain.step(v.bn_aggr(mv, stats))
    chain.wait()


def project(nc, X, RT, W_IN, LN_G, LN_B, BF, CONST, PN, QTA, QTB, HN, keep):
    kaT, kiT, kbT, va1, vb1, ident, tri, ones = (keep[k] for k in ("kaT", "kiT", "kbT", "va1", "vb1", "ident", "tri", "ones"))
    with ExitStack() as ctx:
        def sb(name, shape, dt=F32):
            return ctx.enter_context(nc.sbuf_tensor(name, shape, dt))

        def sem(name):
            return ctx.enter_context(nc.semaphore(name))

        w_in = sb("w_in", [P, KD, N_IN])
        g_emb = sb("g_emb", [P, D])
        b_emb = sb("b_emb", [P, D])
        bf = sb("bf", [P, HEADS])
        x_in = [sb(f"x_in{p}", [P, D]) for p in range(2)]
        rt = [sb(f"rt{p}", [P, 2 * ROPE]) for p in range(2)]
        hT = [sb(f"hT{p}", [P, KD, P]) for p in range(2)]
        pn = [sb(f"pn{p}", [P, N_IN]) for p in range(2)]
        rope_a = sb("rope_a", [P, 2, 9, ROPE])
        rope_b = sb("rope_b", [P, 2, 9, ROPE])
        kdup = sb("kdup", [P, 2, 2, HD])
        q_aug = sb("q_aug", [P, HEADS, AUG])
        k_aug = sb("k_aug", [P, 2, AUG])
        qaiT = sb("qaiT", [P, 2, 4, P])
        qbT = sb("qbT", [AUG, 2, 4, P])
        lf_sum = sb("lf_sum", [P, HEADS])
        stats = sb("stats", [P, 12])
        mv = sb("mv", [P, 2])
        sd = sb("sd", [P, 1])
        rs = sb("rs", [P, 1])
        eps = sb("eps", [P, 1])
        z = sb("z", [P, HEADS])
        az = sb("az", [P, HEADS])
        sp_e = sb("sp_e", [P, HEADS])
        sp_l = sb("sp_l", [P, HEADS])
        pT = ctx.enter_context(nc.psum_tensor("pT", [P, 2, 512], F32))
        pP = ctx.enter_context(nc.psum_tensor("pP", [P, 4, 512], F32))
        pQ = ctx.enter_context(nc.psum_tensor("pQ", [P, 2, 512], F32))
        c_ps = pT[:, 0, 0:HEADS]

        w_here = sem("w_here")
        consts_here = sem("consts_here")
        x_here = [sem(f"x_here{p}") for p in range(2)]
        x_free = sem("x_free")
        var_done = sem("var_done")
        sd_done = sem("sd_done")
        h_done = sem("h_done")
        hT_ps = sem("hT_ps")
        hT_done = sem("hT_done")
        proj_ps = sem("proj_ps")
        pn_done = sem("pn_done")
        az_done = sem("az_done")
        spl_done = sem("spl_done")
        act_own = sem("act_own")
        lf_done = sem("lf_done")
        lf_sum_done = sem("lf_sum_done")
        c_sum_ps = sem("c_sum_ps")
        aug_done = sem("aug_done")
        q_ps = sem("q_ps")
        q_evac = sem("q_evac")
        pn_stored = [sem(f"pn_stored{p}") for p in range(2)]
        h_stored = [sem(f"h_stored{p}") for p in range(2)]
        q_stored = sem("q_stored")
        kdup_done = sem("kdup_done")
        pool_init = sem("pool_init")
        dve = sem("dve1")

        LAST = TILES - 1

        def tiles(eng, body, chain=None, per=0):
            body(0, 0, 0)
            body(1, 1, 0)
            with eng.Fori(1, TILES // 2) as i:
                if chain:
                    chain.start_loop(i, 1, per)
                body(2 * i, 0, i)
                body(2 * i + 1, 1, i)
                if chain:
                    chain.end_loop(TILES // 2 - 1, per)
            body(LAST, 0, TILES // 2)

        def is_first(t):
            return isinstance(t, int) and t == 0

        def is_last(t):
            return isinstance(t, int) and t == LAST

        block = ctx.enter_context(nc.Block())

        @block.sync
        def _(sp):
            sp.dma_start(g_emb[:], LN_G.unsqueeze(0).to_broadcast([P, D])).then_inc(consts_here, 16)
            sp.dma_start(b_emb[:], LN_B.unsqueeze(0).to_broadcast([P, D])).then_inc(consts_here, 16)
            sp.dma_start(bf[:], BF.to_broadcast([P, HEADS])).then_inc(consts_here, 16)
            sp.dma_start(ident[:], CONST[0]).then_inc(consts_here, 16)
            sp.dma_start(tri[:], CONST[1]).then_inc(consts_here, 16)
            sp.dma_start(ones[:], CONST[2]).then_inc(consts_here, 16)

            def load(t, p, i):
                if not (isinstance(t, int) and t < 2):
                    wait_alone(sp, x_free, t - 1)
                    wait_alone(sp, h_stored[p], 16 * i)
                sp.dma_start(x_in[p][:], X[ds(t * P, P), :]).then_inc(x_here[p], 16)
                sp.dma_start(rt[p][:], RT[ds(t * P, P), :]).then_inc(x_here[p], 16)
                if is_first(t):
                    for k in range(KD):
                        sp.dma_start(w_in[:, k, :], W_IN[k * P:(k + 1) * P, :]).then_inc(w_here, 16)

            tiles(sp, load)

        @block.gpsimd
        def _(pool):
            pool.memset(eps[:], EPS)
            pool.memset(lf_sum[:], 0.0)
            pool.memset(va1[:, :, HD:2 * HD], 1.0)
            pool.memset(vb1[:, :, :, HD:2 * HD], 1.0)
            pool.memset(k_aug[:, :, AUG - 1:AUG], 1.0)
            pool.memset(q_aug[:, :, HD:AUG], 0.0).then_inc(pool_init, 1)
            pool.wait_ge(pool_init, 1)
            for h in range(HEADS):
                pool.memset(q_aug[:, h, HD + h:HD + h + 1], 1.0).then_inc(pool_init, 1)

            def stage(t, p, i):
                wait_alone(pool, h_done, t + 1)
                pool.dma_start(HN[ds(t * P, P), :], x_in[p][:]).then_inc(h_stored[p], 16)
                wait_alone(pool, lf_done, t + 1)
                pool.dma_start(PN[ds(t * P, P), :], pn[p][:]).then_inc(pn_stored[p], 16)
                if not is_first(t):
                    wait_alone(pool, q_ps, t * 5)
                for c in range(2):
                    pool.tensor_copy(kdup[:, 0, c, :], pn[p][:, KA:KA + HD])
                    pool.tensor_copy(kdup[:, 1, c, :], pn[p][:, KI:KI + HD])
                pool.tensor_copy(va1[:, ds(t, 1), 0:HD].squeeze(1), pn[p][:, VA:VA + HD])
                for g in range(2):
                    pool.tensor_copy(vb1[:, ds(t, 1), g, 0:HD].squeeze(1), pn[p][:, VB + g * HD:VB + (g + 1) * HD])
                pool.tensor_copy(q_aug[:, :, 0:HD], pn[p][:, QB:QB + 512].rearrange("p (h d) -> p h d", d=HD))
                pool.tensor_copy(k_aug[:, :, 0:HD],
                                 pn[p][:, KB:KB + 128].rearrange("p (h d) -> p h d", d=HD)).then_inc(kdup_done, 1)
                if not is_first(t):
                    store_q(t - 1)

            def store_q(t):
                wait_alone(pool, q_evac, 5 * (t + 1))
                pool.dma_start(QTA[ds(t * P, P), :], qaiT[:].rearrange("p a b c -> p (a b c)")).then_inc(q_stored, 16)
                pool.dma_start(QTB[ds(t * AUG, AUG), :], qbT[:].rearrange("p a b c -> p (a b c)")).then_inc(q_stored, 16)

            tiles(pool, stage)
            store_q(LAST)
            pool.wait_ge(q_stored, 32 * TILES)
            for p in range(2):
                pool.wait_ge(h_stored[p], 16 * (TILES // 2 + 1 - p))
                pool.wait_ge(pn_stored[p], 16 * (TILES // 2 + 1 - p))

        @block.tensor
        def _(pe):
            def turn_h(t, p):
                pe.wait_ge(h_done, t + 1)
                if not is_first(t):
                    pe.wait_ge(hT_done, t)
                if not (isinstance(t, int) and t < 3):
                    pe.wait_ge(aug_done, t - 2)
                for k in range(KD):
                    ins = pe.transpose(pT[:, k // 4, (k % 4) * P:(k % 4 + 1) * P], x_in[p][:, k * P:(k + 1) * P], ident[:])
                ins.then_inc(hT_ps, 1)

            def turn_q(t, p):
                pe.wait_ge(kdup_done, t + 1)
                pe.wait_ge(aug_done, t + 1)
                for b in range(5):
                    if is_first(t) and b < 2:
                        pass
                    else:
                        pe.wait_ge(q_evac, t * 5 + max(b - 1, 0))
                    out = pQ[:, b % 2, :].rearrange("p (c n) -> p c n", c=4)
                    for c in range(4):
                        if b == 0:
                            ins = pe.transpose(out[:, c, :], pn[p][:, QA + c * P:QA + (c + 1) * P], ident[:])
                        elif b == 1:
                            ins = pe.transpose(out[:, c, :], pn[p][:, QI + c * P:QI + (c + 1) * P], ident[:])
                        elif b == 2 and c < 2:
                            ins = pe.transpose(out[:, c, :], kdup[:, c, :, :].rearrange("p a b -> p (a b)"), ident[:])
                        elif b == 2:
                            ins = pe.transpose(out[0:AUG, c, :], k_aug[:, c - 2, :], ident[:])
                        else:
                            ins = pe.transpose(out[0:AUG, c, :], q_aug[:, (b - 3) * 4 + c, :], ident[:])
                    ins.then_inc(q_ps, 1)

            def forget_sum(t, p):
                pe.wait_ge(lf_done, t + 1)
                pe.wait_ge(hT_done, TILES if is_last(t) or is_last(t + 1) else t + 3)
                pe.matmul(c_ps, tri[:], pn[p][:, FL:FL + HEADS], start=True, stop=False)
                pe.matmul(c_ps, ones[:], lf_sum[:], start=False, stop=True).then_inc(c_sum_ps, 1)

            def tile(t, p, i):
                if not is_last(t):
                    turn_h(t + 1, 1 - p)
                pe.wait_ge(hT_done, t + 1)
                for j in range(PROJ_CHUNKS):
                    if not is_first(t):
                        pe.wait_ge(pn_done, (t - 1) * PROJ_CHUNKS + j + 1)
                    for k in range(KD):
                        if is_first(t) and j == 0:
                            pe.wait_ge(w_here, 16 * KD)
                        ins = pe.matmul(pP[:, j, 0:PROJ_W], hT[p][:, k, :], w_in[:, k, j * PROJ_W:(j + 1) * PROJ_W],
                                        start=(k == 0), stop=(k == KD - 1))
                    ins.then_inc(proj_ps, 1)
                    if j == 0 and not is_first(t):
                        forget_sum(t - 1, 1 - p)
                if not is_first(t):
                    turn_q(t - 1, 1 - p)

            pe.wait_ge(consts_here, 96)
            pe.wait_ge(pool_init, 1 + HEADS)
            turn_h(0, 0)
            tiles(pe, tile)
            forget_sum(LAST, 0)
            turn_q(LAST, 0)

        @block.scalar
        def _(act):
            def tile(t, p, i):
                if not is_last(t):
                    head(t + 1, 1 - p)
                if not (isinstance(t, int) and t < 2):
                    act.wait_ge(pn_stored[p], 16 * i)
                    act.wait_ge(q_ps, 5 * (t - 1))
                    act.wait_ge(kdup_done, t - 1)
                for j in range(PROJ_CHUNKS):
                    act.wait_ge(proj_ps, t * PROJ_CHUNKS + j + 1)
                    act.activation(pn[p][:, j * PROJ_W:(j + 1) * PROJ_W], pP[:, j, 0:PROJ_W], ACT.Copy).then_inc(pn_done, 1)
                act.wait_ge(az_done, t + 1)
                act.activation(sp_e[:], az[:], ACT.Exp, scale=-1.0).then_inc(act_own, 1)
                act.wait_ge(act_own, t + 1)
                act.activation(sp_l[:], sp_e[:], ACT.Ln, bias=ones[:, 0:1]).then_inc(spl_done, 1)
                if not is_first(t):
                    copy_q(t - 1)

            def head(t, p):
                act.wait_ge(var_done, t + 1)
                act.activation(sd[:], mv[:, 1:2], ACT.Sqrt, bias=eps[:]).then_inc(sd_done, 1)
                act.wait_ge(hT_ps, t + 1)
                if not (isinstance(t, int) and t < 2):
                    act.wait_ge(proj_ps, (t - 1) * PROJ_CHUNKS)
                act.activation(hT[p][:].rearrange("p a b -> p (a b)"), pT[:].rearrange("p a b -> p (a b)"),
                               ACT.Copy).then_inc(hT_done, 1)

            def copy_q(t):
                if not is_first(t):
                    act.wait_ge(q_stored, 32 * t)
                for b in (0, 1, 3, 4):
                    act.wait_ge(q_ps, t * 5 + b + 1)
                    out, rows = (qaiT[:, b], P) if b < 2 else (qbT[:, b - 3], AUG)
                    if b == 3:
                        act.wait_ge(q_evac, t * 5 + 3)
                    act.activation(out.rearrange("p a b -> p (a b)"), pQ[0:rows, b % 2, :], ACT.Copy).then_inc(q_evac, 1)

            act.wait_ge(consts_here, 96)
            act.wait_ge(pool_init, 1 + HEADS)
            head(0, 0)
            tiles(act, tile)
            copy_q(LAST)

        @block.vector
        def _(v):
            ch = Chain(v, dve)

            def norm(t, p, turn):
                v.wait_ge(x_here[p], 32 * (turn + 1))
                layer_norm_stats(ch, x_in[p], stats[:], mv[:])
                v.sem_inc(var_done, 1)
                v.wait_ge(sd_done, t + 1)
                ch.step(v.reciprocal(rs[:], sd[:]))
                ch.wait()
                ch.step(v.tensor_scalar(x_in[p][:], x_in[p][:], mv[:, 0:1], rs[:], ALU.subtract, ALU.mult))
                ch.wait()
                ch.step(v.tensor_tensor(x_in[p][:], x_in[p][:], g_emb[:], ALU.mult))
                ch.wait()
                ch.step(v.tensor_tensor(x_in[p][:], x_in[p][:], b_emb[:], ALU.add))
                ch.wait()
                v.sem_inc(h_done, 1)

            def augment(t):
                v.wait_ge(c_sum_ps, t + 1)
                v.wait_ge(kdup_done, t + 1)
                for g in range(2):
                    ch.step(v.tensor_scalar(k_aug[:, g, HD:HD + HEADS], c_ps, -8.0, None, ALU.mult))
                ch.step(v.tensor_scalar(q_aug[:, :, AUG - 1], c_ps, 8.0, None, ALU.mult))
                ch.step(v.tensor_tensor(lf_sum[:], lf_sum[:], lf_of[t_par[0]], ALU.add))
                ch.wait()
                v.sem_inc(aug_done, 1)

            t_par = [0]
            lf_of = [pn[p][:, FL:FL + HEADS] for p in range(2)]

            def tile(t, p, i):
                if not is_last(t):
                    norm(t + 1, 1 - p, (i if p == 0 else i + 1))
                if not is_first(t):
                    t_par[0] = 1 - p
                    augment(t - 1)
                v.wait_ge(pn_done, PROJ_CHUNKS * (t + 1))
                ch.step(v.tensor_tensor(z[:], pn[p][:, FL:FL + HEADS], bf[:], ALU.add))
                ch.wait()
                ch.step(v.scalar_tensor_tensor(out=az[:], in0=z[:], scalar=-1.0, in1=z[:], op0=ALU.mult, op1=ALU.max))
                ch.wait()
                v.sem_inc(az_done, 1)
                x4 = [pn[p][:, s:s + 9 * HD].rearrange("p (h d) -> p h d", d=HD) for s in (QA, QI)]
                cos = rt[p][:, 0:ROPE].unsqueeze(1).to_broadcast([P, 9, ROPE])
                sin = rt[p][:, ROPE:2 * ROPE].unsqueeze(1).to_broadcast([P, 9, ROPE])
                for s in range(2):
                    ch.step(v.tensor_tensor(rope_a[:, s], x4[s][:, :, 0:ROPE], cos, ALU.mult))
                    ch.step(v.tensor_tensor(rope_b[:, s, :, 0:8], x4[s][:, :, 8:16], sin[:, :, 0:8], ALU.mult))
                    ch.step(v.tensor_tensor(rope_b[:, s, :, 8:16], x4[s][:, :, 0:8], sin[:, :, 8:16], ALU.mult))
                ch.wait()
                for s in range(2):
                    ch.step(v.tensor_tensor(x4[s][:, :, 0:ROPE], rope_a[:, s], rope_b[:, s], ALU.add))
                v.wait_ge(spl_done, t + 1)
                ch.step(v.scalar_tensor_tensor(out=pn[p][:, FL:FL + HEADS], in0=z[:], scalar=0.0, in1=sp_l[:],
                                               op0=ALU.min, op1=ALU.subtract))
                ch.wait()
                v.sem_inc(x_free, 1)
                v.sem_inc(lf_done, 1)
                if not is_first(t):
                    copy_k(t - 1)

            def copy_k(t):
                v.wait_ge(q_ps, t * 5 + 3)
                v.wait_ge(q_evac, t * 5 + 2)
                ch.step(v.tensor_copy(kaT[:, ds(t * P, P)], pQ[:, 0, 0:P]))
                ch.step(v.tensor_copy(kiT[:, ds(t * P, P)], pQ[:, 0, P:2 * P]))
                for g in range(2):
                    ch.step(v.tensor_copy(kbT[0:AUG, g, ds(t * P, P)], pQ[0:AUG, 0, (2 + g) * P:(3 + g) * P]))
                ch.wait()
                v.sem_inc(q_evac, 1)

            v.wait_ge(consts_here, 96)
            v.wait_ge(pool_init, 1 + HEADS)
            norm(0, 0, 0)
            per = 2 * (2 + 1 + 4 + 4 + 1 + 1 + 6 + 2 + 1 + 4)
            tiles(v, tile, ch, per)
            augment_last = LAST
            t_par[0] = 0
            augment(augment_last)
            copy_k(LAST)


SPAN = 1024


class Tally:

    def __init__(self, first=0):
        self.n, self.base, self.outer = first, 0, []

    def at(self, more=0):
        return self.base + (self.n + more)

    def add(self, k=1):
        self.n += k

    def enter(self, turn, per):
        self.outer.append((self.n, self.base))
        self.base = self.base + turn * per

    def leave(self, turns, per):
        mark, self.base = self.outer.pop()
        assert self.n - mark == per, (self.n - mark, per)
        self.n = mark + turns * per


def wait(eng, semaphore, value):
    if not isinstance(value, int) or value > 0:
        wait_alone(eng, semaphore, value)


def spans(width):
    return [(c, min(SPAN, width - c)) for c in range(0, width, SPAN)]


SEGMENTS = [
    (0, 1, 256, (0, 512), False),
    (2, 1, 512, (512, 1024), True),
    (4, 2, 1024, (1024, 1536), True),
    (8, 2, 1536, (1536, 2048), True),
    (12, 2, 2048, (2048, ROWS), True),
    (16, 1, ROWS, (0,), True),
]


def attend(nc, PN, QTA, QTB, MASK, MT, keep):
    kaT, kiT, kbT, va1, vb1, ident = (keep[k] for k in ("kaT", "kiT", "kbT", "va1", "vb1", "ident"))
    with ExitStack() as ctx:
        def sb(name, shape, dt=F32):
            return ctx.enter_context(nc.sbuf_tensor(name, shape, dt))

        def sem(name):
            return ctx.enter_context(nc.semaphore(name))

        qT = [sb(f"qT{p}", [P, 2, 4, P]) for p in range(2)]
        qbT = [sb(f"qbT{p}", [AUG, 2, 4, P]) for p in range(2)]
        wi = [sb(f"wi{p}", [P, HEADS]) for p in range(2)]
        mask = sb("mask", [P, ROWS])
        scores = sb("scores", [P, ROWS])
        work = sb("work", [P, ROWS])
        top8 = sb("top8", [P, 8])
        relu = sb("relu", [P, 2, SPAN])
        probs = sb("probs", [P, 2, 4, ROWS])
        nmax = sb("nmax", [P, 2 * HEADS])
        pT = sb("pT_sb", [P, 2, 4 * P])
        rsum = sb("rsum", [HD, 4, P])
        mixT = [sb(f"mixT{p}", [P, 8, P]) for p in range(2)]
        S = [ctx.enter_context(nc.psum_tensor(f"S{b}", [P, SPAN], F32)) for b in range(2)]
        tr = [ctx.enter_context(nc.psum_tensor(f"tr{b}", [P, 4, P], F32)) for b in range(2)]
        pv = [ctx.enter_context(nc.psum_tensor(f"pv{b}", [P, 4, P], F32)) for b in range(2)]

        q_here = [sem(f"q_here{p}") for p in range(2)]
        mask_here = sem("mask_here")
        s_full = sem("s_full")
        relu_done = sem("relu_done")
        acc_done = sem("acc_done")
        topk_step = sem("topk_step")
        ttr_done = sem("ttr_done")
        exp_done = sem("exp_done")
        tr_full = sem("tr_full")
        tr_copied = sem("tr_copied")
        pv_step = sem("pv_step")
        norm_step = sem("norm_step")
        mix_stored = [sem(f"mix_stored{p}") for p in range(2)]

        def per_tile(W, Wi, topk):
            nb = W // P
            return dict(full=8 * len(spans(Wi)) + 16 * len(spans(W)), relu=8 * len(spans(Wi)), acc=8 * len(spans(Wi)),
                        topk=(2 * TOPK // 8 + 1 if topk else 0), ttr=16 * len(spans(W)), exp=16,
                        tr=4 * nb, pvs=4 * nb, norm=12)

        def run(eng, body):
            counts = {k: Tally() for k in per_tile(P, 0, False)}
            for t0, turns, W, Wis, topk in SEGMENTS:
                per = [per_tile(W, Wi, topk) for Wi in Wis]
                total = {k: sum(x[k] for x in per) for k in counts}
                if turns == 1:
                    for j, Wi in enumerate(Wis):
                        body(t0 + j, j, (t0 + j) // 2, W, Wi, topk, counts)
                    continue
                with eng.Fori(0, turns) as i:
                    for k in counts:
                        counts[k].enter(i, total[k])
                    for j, Wi in enumerate(Wis):
                        body(i * 2 + (t0 + j), j, i + t0 // 2, W, Wi, topk, counts)
                for k in counts:
                    counts[k].leave(turns, total[k])
            return counts

        block = ctx.enter_context(nc.Block())

        @block.sync
        def _(sp):
            def load_q(t, p):
                sp.dma_start(qT[p][:].rearrange("p a b c -> p (a b c)"), QTA[ds(t * P, P), :]).then_inc(q_here[p], 16)
                sp.dma_start(qbT[p][:].rearrange("p a b c -> p (a b c)"), QTB[ds(t * AUG, AUG), :]).then_inc(q_here[p], 16)
                sp.dma_start(wi[p][:], PN[ds(t * P, P), WI:WI + HEADS]).then_inc(q_here[p], 16)

            def load_mask(t, W):
                sp.dma_start(mask[:, 0:W], MASK[:, ds(ROWS - t * P, W)]).then_inc(mask_here, 16)

            def store_mix(t, p):
                sp.dma_start(MT[ds(t * P, P), :], mixT[p][:].rearrange("p a b -> p (a b)")).then_inc(mix_stored[p], 16)

            before = [0]

            def tile(t, p, i, W, Wi, topk, n):
                last = isinstance(t, int) and t == TILES - 1
                if not last:
                    wait(sp, s_full, n["full"].at(-before[0]))
                    wait(sp, acc_done, n["acc"].at())
                    load_q(t + 1, 1 - p)
                    wait(sp, ttr_done, n["ttr"].at((8 if topk else 16) * len(spans(W))))
                    load_mask(t + 1, max(Wi, W))
                if not (isinstance(t, int) and t == 0):
                    wait(sp, norm_step, n["norm"].at())
                    store_mix(t - 1, 1 - p)
                for k, v in per_tile(W, Wi, topk).items():
                    n[k].add(v)
                before[0] = per_tile(W, Wi, topk)["relu"]

            load_q(0, 0)
            load_mask(0, 256)
            n = run(sp, tile)
            wait(sp, norm_step, n["norm"].at())
            store_mix(TILES - 1, 0)
            for p in range(2):
                sp.wait_ge(mix_stored[p], 16 * (TILES // 2 + 1 - p))

        @block.tensor
        def _(pe):
            state = dict(kind="ttr", run=0, bank=0, group=0, tb=0)

            def unit(kind, n, matmuls):
                if state["kind"] != kind:
                    state["before"], state["kind"], state["run"] = state["kind"], kind, 0
                sems = {"ttr": ttr_done, "relu": relu_done}
                if state["run"] < 2 and "before" in state:
                    wait(pe, sems[state["before"]], n[state["before"]].at(state["run"] - 1))
                else:
                    wait(pe, sems[kind], n[kind].at(-1))
                out = S[n["full"].n % 2]
                for k, (lo, w, lhsT, rhs) in enumerate(matmuls):
                    ins = pe.matmul(out[:, lo:lo + w], lhsT, rhs, start=True, stop=True)
                ins.then_inc(s_full, 1)
                n["full"].add()
                n[kind].add()
                state["run"] += 1

            def products(kind, n, W, lhsT, keys):
                for c, w in spans(W):
                    unit(kind, n, [(lo, min(512, w - lo), lhsT, keys[:, c + lo:c + min(w, lo + 512)]) for lo in range(0, w, 512)])

            def logits_b(p, g, W, n):
                for h in range(4):
                    products("ttr", n, W, qbT[p][:, g, h, :], kbT[0:AUG, g, :])

            def logits_a(p, g, W, n):
                for h in range(4 * g, 4 * g + 4):
                    half = slice(HD * (h % 2), HD * (h % 2) + HD)
                    products("ttr", n, W, qT[p][half, 0, h // 2, :], kaT[half, :])

            def indexer(p, W, n):
                for h in range(HEADS):
                    half = slice(HD * (h % 2), HD * (h % 2) + HD)
                    products("relu", n, W, qT[p][half, 1, h // 2, :], kiT[half, :])

            def weigh(W, n, values):
                nb = W // P
                grp, bank = state["group"] % 2, state["group"] % 2
                n["exp"].add(4)
                wait(pe, exp_done, n["exp"].at())
                wait(pe, norm_step, n["norm"].at(-3))
                for kb in range(nb + 1):
                    if kb < nb:
                        wait(pe, tr_copied, n["tr"].at(-1))
                        for h in range(4):
                            ins = pe.transpose(tr[state["tb"] % 2][:, h, :], probs[:, grp, h, kb * P:(kb + 1) * P], ident[:])
                        ins.then_inc(tr_full, 1)
                        n["tr"].add()
                        state["tb"] += 1
                    if kb > 0:
                        b = state["tb"] - (1 if kb == nb else 2)
                        wait(pe, tr_copied, n["tr"].at(0 if kb == nb else -1))
                        pe.matmul(pv[bank][:].rearrange("p a b -> p (a b)"), values(kb - 1), pT[:, b % 2, :],
                                  start=(kb == 1), stop=(kb == nb)).then_inc(pv_step, 1)
                n["norm"].add(3)
                state["group"] += 1

            def tile(t, p, i, W, Wi, topk, n):
                pe.wait_ge(q_here[p], 48 * (i + 1))
                for g in range(2):
                    logits_b(p, g, W, n)
                for g in range(2):
                    weigh(W, n, lambda kb, g=g: vb1[:, kb, g, :])
                for g in range(2):
                    logits_a(p, g, W, n)
                if Wi:
                    pe.wait_ge(q_here[1 - p], 48 * (i + 1 + p))
                    indexer(1 - p, Wi, n)
                for g in range(2):
                    weigh(W, n, lambda kb: va1[:, kb, :])
                n["acc"].add(per_tile(W, Wi, topk)["acc"])
                n["topk"].add(per_tile(W, Wi, topk)["topk"])
                n["pvs"].add(per_tile(W, Wi, topk)["pvs"])

            run(pe, tile)

        @block.scalar
        def _(act):
            state = dict(group=0, tb=0)

            def softmax(W, n, g):
                for h in range(4):
                    k = len(spans(W))
                    n["ttr"].add(k)
                    n["full"].add(k)
                    wait(act, ttr_done, n["ttr"].at())
                    slot = 4 * (state["group"] % 4) + h
                    row = probs[:, state["group"] % 2, h, 0:W]
                    act.activation(row, row, ACT.Exp, bias=nmax[:, slot:slot + 1], scale=-1.0).then_inc(exp_done, 1)
                    n["exp"].add()
                state["group"] += 1

            def copies(W, n):
                for kb in range(W // P):
                    n["tr"].add()
                    wait(act, tr_full, n["tr"].at())
                    wait(act, pv_step, n["pvs"].at(-1))
                    b = state["tb"] % 2
                    act.activation(pT[:, b, :], tr[b][:].rearrange("p a b -> p (a b)"), ACT.Copy).then_inc(tr_copied, 1)
                    n["pvs"].add()
                    state["tb"] += 1

            def relus(W, n):
                for h in range(HEADS):
                    for c, w in spans(W):
                        b = n["full"].n % 2
                        n["full"].add()
                        wait(act, s_full, n["full"].at())
                        wait(act, acc_done, n["acc"].at(-1))
                        act.activation(relu[:, b, 0:w], S[b][:, 0:w], ACT.Relu, scale=HD ** -0.5 * HEADS ** -0.5).then_inc(relu_done, 1)
                        n["relu"].add()
                        n["acc"].add()

            def tile(t, p, i, W, Wi, topk, n):
                for g in range(2):
                    softmax(W, n, g)
                for g in range(2):
                    copies(W, n)
                for g in range(2):
                    softmax(W, n, g)
                if Wi:
                    relus(Wi, n)
                for g in range(2):
                    copies(W, n)
                n["norm"].add(12)
                n["topk"].add(per_tile(W, Wi, topk)["topk"])

            run(act, tile)

        @block.vector
        def _(v):
            state = dict(group=0, out=0, nb=0)

            def logits(W, n, bias, h):
                grp = state["group"] % 2
                if h == 0:
                    wait(v, tr_full, n["tr"].at(-(W // P) if state["group"] % 4 else -state["nb"]))
                slot = 4 * (state["group"] % 4) + h
                for k, (c, w) in enumerate(spans(W)):
                    b = n["full"].n % 2
                    n["full"].add()
                    wait(v, s_full, n["full"].at())
                    if k:
                        wait(v, ttr_done, n["ttr"].at())
                    v.tensor_tensor_reduce(probs[:, grp, h, c:c + w], S[b][:, 0:w], bias[:, c:c + w], -HD ** -0.5,
                                           nmax[:, slot:slot + 1] if k else 3.4e38, ALU.add, ALU.min,
                                           nmax[:, slot:slot + 1]).then_inc(ttr_done, 1)
                    n["ttr"].add()
                if h == 3:
                    state["group"] += 1
                    n["tr"].add(W // P)

            def normalise(p, first, nb, n, pvs):
                wait(v, pv_step, pvs)
                wait(v, norm_step, n["norm"].at())
                o = pv[state["out"] % 2]
                v.reciprocal(rsum[:], o[HD:P]).then_inc(norm_step, 1)
                n["norm"].add()
                wait(v, norm_step, n["norm"].at())
                for k in range(2):
                    v.tensor_tensor(mixT[p][k * HD:(k + 1) * HD, first:first + 2, :], o[0:HD, k::2, :], rsum[:, k::2, :],
                                    ALU.mult).then_inc(norm_step, 1)
                    n["norm"].add()
                state["out"] += 1

            def index_scores(t, p, W, n):
                for h in range(HEADS):
                    for k, (c, w) in enumerate(spans(W)):
                        b = n["full"].n % 2
                        n["full"].add()
                        n["relu"].add()
                        wait(v, relu_done, n["relu"].at())
                        if h:
                            wait(v, acc_done, n["acc"].at(1 - len(spans(W))))
                        v.scalar_tensor_tensor(out=scores[:, c:c + w], in0=relu[:, b, 0:w], scalar=wi[p][:, h:h + 1],
                                               in1=(scores if h else mask)[:, c:c + w], op0=ALU.mult, op1=ALU.add)\
                            .then_inc(acc_done, 1)
                        n["acc"].add()

            def take8(W, n, first):
                src = (scores if first else work)[:, 0:W]
                wait(v, topk_step, n["topk"].at())
                v.max(top8[:], src).then_inc(topk_step, 1)
                n["topk"].add()
                wait(v, topk_step, n["topk"].at())
                v.match_replace(work[:, 0:W], top8[:], src, TAKEN).then_inc(topk_step, 1)
                n["topk"].add()

            def tile(t, p, i, W, Wi, topk, n):
                nb = W // P
                first_tile = isinstance(t, int) and t == 0
                if topk:
                    wait(v, acc_done, n["acc"].at())
                v.wait_ge(mask_here, t * 16 + 16)
                v.wait_ge(q_here[p], 48 * (i + 1))
                pvs0 = n["pvs"].n
                for h in range(HEADS):
                    if topk:
                        for r in range(TOPK // 8 // HEADS):
                            take8(W, n, h == 0 and r == 0)
                    if h == 4 and not first_tile:
                        for g in range(2):
                            normalise(1 - p, 2 * g, None, n, n["pvs"].at(-state["nb"] if g == 0 else 0))
                    logits(W, n, mask, h % 4)
                if not (isinstance(t, int) and t < 2):
                    v.wait_ge(mix_stored[p], 16 * i)
                for g in range(2):
                    n["pvs"].add(nb)
                    normalise(p, 4 + 2 * g, nb, n, n["pvs"].at())
                bias = mask
                if topk:
                    wait(v, topk_step, n["topk"].at())
                    v.tensor_scalar(work[:, 0:W], work[:, 0:W], TAKEN, NEG, ALU.not_equal, ALU.mult).then_inc(topk_step, 1)
                    n["topk"].add()
                    wait(v, topk_step, n["topk"].at())
                    bias = work
                state["nb"] = nb
                for h in range(HEADS):
                    logits(W, n, bias, h % 4)
                if Wi:
                    v.wait_ge(mask_here, t * 16 + 32)
                    v.wait_ge(q_here[1 - p], 48 * (i + 1 + p))
                    index_scores(t, 1 - p, Wi, n)
                for g in range(2):
                    n["pvs"].add(nb)
                n["exp"].add(16)

            n = run(v, tile)
            for g in range(2):
                normalise(0, 2 * g, None, n, n["pvs"].at(-state["nb"] if g == 0 else 0))


GROUPS = 3
GCOLS = 692
HALF = GCOLS // 2
FC = D_FF // P
BLOCKS = -(-GCOLS // P)


def mix_out(nc, MT, HN, W_O, LN_G, LN_B, H1T, keep):
    ident = keep["ident"]
    with ExitStack() as ctx:
        def sb(name, shape, dt=F32):
            return ctx.enter_context(nc.sbuf_tensor(name, shape, dt))

        def sem(name):
            return ctx.enter_context(nc.semaphore(name))

        w_o = sb("w_o", [P, KD, D])
        g1 = sb("g1", [P, D])
        b1 = sb("b1", [P, D])
        mixT = [sb(f"mo_mixT{p}", [P, KD, P]) for p in range(2)]
        hn = [sb(f"mo_h{p}", [P, D]) for p in range(2)]
        z = [sb(f"mo_z{p}", [P, D]) for p in range(2)]
        h1T = [sb(f"mo_h1T{p}", [P, KD, P]) for p in range(2)]
        stats = sb("mo_stats", [P, 12])
        mv = sb("mo_mv", [P, 2])
        sd = sb("mo_sd", [P, 1])
        rs = sb("mo_rs", [P, 1])
        eps = sb("mo_eps", [P, 1])
        po = [ctx.enter_context(nc.psum_tensor(f"mo_po{p}", [P, D], F32)) for p in range(2)]
        pt = [ctx.enter_context(nc.psum_tensor(f"mo_pt{p}", [P, D], F32)) for p in range(2)]

        w_here = sem("mo_w_here")
        in_here = [sem(f"mo_in_here{p}") for p in range(2)]
        eps_set = sem("mo_eps_set")
        o_ps = sem("mo_o_ps")
        z_done = sem("mo_z_done")
        var_done = sem("mo_var_done")
        sd_done = sem("mo_sd_done")
        ln_step = sem("mo_ln_step")
        h1_done = sem("mo_h1_done")
        t_ps = sem("mo_t_ps")
        t_copied = sem("mo_t_copied")
        stored = [sem(f"mo_stored{p}") for p in range(2)]

        LN_STEPS = 5

        def run(eng, body):
            ln = Tally()
            for t in (0, 1):
                body(t, t, 0, ln)
                ln.add(LN_STEPS)
            with eng.Fori(0, TILES // 2 - 1) as i:
                ln.enter(i, 2 * LN_STEPS)
                for p in range(2):
                    body(2 * i + (2 + p), p, i + 1, ln)
                    ln.add(LN_STEPS)
                ln.leave(TILES // 2 - 1, 2 * LN_STEPS)
            body(TILES - 1, 0, TILES // 2, ln)

        block = ctx.enter_context(nc.Block())

        @block.sync
        def _(sp):
            for k in range(KD):
                sp.dma_start(w_o[:, k, :], W_O[k * P:(k + 1) * P, :]).then_inc(w_here, 16)
            sp.dma_start(g1[:], LN_G.unsqueeze(0).to_broadcast([P, D])).then_inc(w_here, 16)
            sp.dma_start(b1[:], LN_B.unsqueeze(0).to_broadcast([P, D])).then_inc(w_here, 16)

            def tile(t, p, i, ln):
                if not (isinstance(t, int) and t < 2):
                    wait_alone(sp, o_ps, t - 1)
                    wait_alone(sp, z_done, 2 * t - 2)
                sp.dma_start(mixT[p][:].rearrange("p a b -> p (a b)"), MT[ds(t * P, P), :]).then_inc(in_here[p], 16)
                sp.dma_start(hn[p][:], HN[ds(t * P, P), :]).then_inc(in_here[p], 16)

            run(sp, tile)

        @block.gpsimd
        def _(pool):
            pool.memset(eps[:], EPS).then_inc(eps_set, 1)

            def tile(t, p, i, ln):
                wait_alone(pool, t_copied, t + 1)
                pool.dma_start(H1T.rearrange("(k p) n -> p k n", p=P)[:, :, ds(t * P, P)], h1T[p][:]).then_inc(stored[p], 16)

            run(pool, tile)
            for p in range(2):
                wait_alone(pool, stored[p], 16 * (TILES // 2 + 1 - p))

        @block.tensor
        def _(pe):
            def turn(t, p):
                wait_alone(pe, h1_done, t + 1)
                if not (isinstance(t, int) and t < 2):
                    wait_alone(pe, t_copied, t - 1)
                for k in range(KD):
                    ins = pe.transpose(pt[p][:, k * P:(k + 1) * P], z[p][:, k * P:(k + 1) * P], ident[:])
                ins.then_inc(t_ps, 1)

            def tile(t, p, i, ln):
                wait_alone(pe, in_here[p], 32 * (i + 1))
                if not (isinstance(t, int) and t < 2):
                    wait_alone(pe, z_done, 2 * t - 2)
                for j in range(2):
                    for k in range(KD):
                        ins = pe.matmul(po[p][:, j * 512:(j + 1) * 512], mixT[p][:, k, :], w_o[:, k, j * 512:(j + 1) * 512],
                                        start=(k == 0), stop=(k == KD - 1))
                ins.then_inc(o_ps, 1)
                if not (isinstance(t, int) and t == 0):
                    turn(t - 1, 1 - p)

            wait_alone(pe, w_here, 16 * (KD + 2))
            run(pe, tile)
            turn(TILES - 1, 0)

        @block.scalar
        def _(act):
            def copy(t, p, i):
                act.wait_ge(t_ps, t + 1)
                if not (isinstance(t, int) and t < 2):
                    act.wait_ge(stored[p], 16 * i)
                act.activation(h1T[p][:].rearrange("p a b -> p (a b)"), pt[p][:], ACT.Copy).then_inc(t_copied, 1)

            def tile(t, p, i, ln):
                act.wait_ge(var_done, t + 1)
                act.activation(sd[:], mv[:, 1:2], ACT.Sqrt, bias=eps[:]).then_inc(sd_done, 1)
                if not (isinstance(t, int) and t == 0):
                    copy(t - 1, 1 - p, i if p else i - 1)

            act.wait_ge(eps_set, 1)
            run(act, tile)
            copy(TILES - 1, 0, TILES // 2)

        @block.vector
        def _(v):
            def tile(t, p, i, ln):
                v.wait_ge(in_here[p], 32 * (i + 1))
                v.wait_ge(o_ps, t + 1)
                if not (isinstance(t, int) and t < 2):
                    v.wait_ge(t_ps, t - 1)
                for j in range(2):
                    c = slice(j * 512, (j + 1) * 512)
                    v.scalar_tensor_tensor(out=z[p][:, c], in0=hn[p][:, c], scalar=ALPHA, in1=po[p][:, c],
                                           op0=ALU.mult, op1=ALU.add).then_inc(z_done, 1)
                v.wait_ge(z_done, 2 * t + 2)
                for j in range(2):
                    v.bn_stats(stats[:, 6 * j:6 * j + 6], z[p][:, j * 512:(j + 1) * 512]).then_inc(ln_step, 1)
                wait_alone(v, ln_step, ln.at(2))
                v.bn_aggr(mv[:], stats[:]).then_inc(var_done, 1)
                v.wait_ge(sd_done, t + 1)
                v.wait_ge(var_done, t + 1)
                v.reciprocal(rs[:], sd[:]).then_inc(ln_step, 1)
                v.wait_ge(ln_step, ln.at(3))
                v.tensor_scalar(z[p][:], z[p][:], mv[:, 0:1], rs[:], ALU.subtract, ALU.mult).then_inc(ln_step, 1)
                v.wait_ge(ln_step, ln.at(4))
                v.tensor_tensor(z[p][:], z[p][:], g1[:], ALU.mult).then_inc(ln_step, 1)
                v.wait_ge(ln_step, ln.at(5))
                v.tensor_tensor(z[p][:], z[p][:], b1[:], ALU.add).then_inc(h1_done, 1)

            v.wait_ge(w_here, 16 * (KD + 2))
            run(v, tile)


def feed_forward(nc, H1T, W_GATE, W_UP, W_DOWN, LN_G, LN_B, Y, keep):
    ident = keep["ident"]
    with ExitStack() as ctx:
        def sb(name, shape, dt=F32):
            return ctx.enter_context(nc.sbuf_tensor(name, shape, dt))

        def sem(name):
            return ctx.enter_context(nc.semaphore(name))

        h1T = sb("ff_h1T", [P, KD, GCOLS])
        hid = sb("ff_hid", [P, FC, GCOLS])
        silu = sb("ff_silu", [P, 2, 2, HALF])
        wg = [sb(f"ff_wg{p}", [P, KD, P]) for p in range(2)]
        wu = [sb(f"ff_wu{p}", [P, KD, P]) for p in range(2)]
        wd = [sb(f"ff_wd{p}", [P, FC, P]) for p in range(2)]
        zT = sb("ff_zT", [P, KD, GCOLS])
        g2 = sb("ff_g2", [P, D])
        b2 = sb("ff_b2", [P, D])
        y = [sb(f"ff_y{p}", [P, D]) for p in range(2)]
        stats = sb("ff_stats", [P, 12])
        mv = sb("ff_mv", [P, 2])
        sd = sb("ff_sd", [P, 1])
        rs = sb("ff_rs", [P, 1])
        eps = sb("ff_eps", [P, 1])
        ps = [ctx.enter_context(nc.psum_tensor(f"ff_ps{p}", [P, 4, 512], F32)) for p in range(2)]

        consts = sem("ff_consts")
        eps_set = sem("ff_eps_set")
        h_here = sem("ff_h_here")
        w_here = [sem(f"ff_w_here{p}") for p in range(2)]
        wd_here = [sem(f"ff_wd_here{p}") for p in range(2)]
        gu_ps = sem("ff_gu_ps")
        silu_done = sem("ff_silu_done")
        hid_done = sem("ff_hid_done")
        down_ps = sem("ff_down_ps")
        z_done = sem("ff_z_done")
        t_ps = sem("ff_t_ps")
        ln_step = sem("ff_ln_step")
        var_done = sem("ff_var_done")
        sd_done = sem("ff_sd_done")
        y_done = sem("ff_y_done")
        y_stored = [sem(f"ff_y_stored{p}") for p in range(2)]

        HIDDEN = dict(gu=2, silu=2, hid=2)
        DOWN = dict(down=2, z=4)
        AHEAD = dict(gu=1, hid=1, down=1, z=2)
        BLOCK = dict(t=1, ln=5, var=1, sd=1, y=1)

        def run(eng, start, hidden, down, rows):
            n = {k: Tally(AHEAD.get(k, 0)) for k in (*HIDDEN, *DOWN, *BLOCK)}
            group = dict({k: v * FC // 2 for k, v in HIDDEN.items()}, **{k: v * KD // 2 for k, v in DOWN.items()},
                         **{k: v * BLOCKS for k, v in BLOCK.items()})
            with eng.Fori(0, GROUPS) as g:
                for k in n:
                    n[k].enter(g, group[k])
                start(g, n)
                if hidden:
                    with eng.Fori(0, FC // 2) as i:
                        for k, per in HIDDEN.items():
                            n[k].enter(i, per)
                        for p in range(2):
                            hidden(g, 2 * i + p, p, n)
                            for k, per in HIDDEN.items():
                                n[k].add(per // 2)
                        for k, per in HIDDEN.items():
                            n[k].leave(FC // 2, per)
                else:
                    for k, per in HIDDEN.items():
                        n[k].add(per * FC // 2)
                if down:
                    with eng.Fori(0, KD // 2) as i:
                        for k, per in DOWN.items():
                            n[k].enter(i, per)
                        for p in range(2):
                            down(g, 2 * i + p, p, n)
                            for k, per in DOWN.items():
                                n[k].add(per // 2)
                        for k, per in DOWN.items():
                            n[k].leave(KD // 2, per)
                else:
                    for k, per in DOWN.items():
                        n[k].add(per * KD // 2)
                for r in range(BLOCKS):
                    if rows:
                        rows(g, r, min(P, GCOLS - r * P), n)
                    for k, per in BLOCK.items():
                        n[k].add(per)
                for k in n:
                    n[k].leave(GROUPS, group[k])
            return n

        block = ctx.enter_context(nc.Block())

        @block.sync
        def _(sp):
            sp.dma_start(g2[:], LN_G.unsqueeze(0).to_broadcast([P, D])).then_inc(consts, 16)
            sp.dma_start(b2[:], LN_B.unsqueeze(0).to_broadcast([P, D])).then_inc(consts, 16)

            def start(g, n):
                wait_alone(sp, z_done, n["z"].at())
                sp.dma_start(h1T[:], H1T.rearrange("(k p) n -> p k n", p=P)[:, :, ds(g * GCOLS, GCOLS)]).then_inc(h_here, 16)

            def hidden(g, f, p, n):
                wait_alone(sp, gu_ps, n["gu"].at(-1))
                for w, src in ((wg[p], W_GATE), (wu[p], W_UP)):
                    sp.dma_start(w[:], src.rearrange("(k p) n -> p k n", p=P)[:, :, ds(f * P, P)]).then_inc(w_here[p], 16)

            def down(g, d, p, n):
                wait_alone(sp, down_ps, n["down"].at(-1))
                sp.dma_start(wd[p][:], W_DOWN.rearrange("(f p) n -> p f n", p=P)[:, :, ds(d * P, P)]).then_inc(wd_here[p], 16)

            run(sp, start, hidden, down, None)

        @block.gpsimd
        def _(pool):
            pool.memset(eps[:], EPS).then_inc(eps_set, 1)

            def rows(g, r, m, n):
                wait_alone(pool, y_done, n["y"].at(1))
                pool.dma_start(Y[ds(g * GCOLS + r * P, m), :], y[r % 2][0:m, :]).then_inc(y_stored[r % 2], 16)

            run(pool, lambda g, n: None, None, None, rows)
            for p in range(2):
                wait_alone(pool, y_stored[p], 16 * GROUPS * BLOCKS // 2)

        @block.tensor
        def _(pe):
            def start(g, n):
                wait_alone(pe, h_here, g * 16 + 16)
                wait_alone(pe, y_done, n["y"].at())

            def hidden(g, f, p, n):
                wait_alone(pe, w_here[p], (n["gu"].at(-1) - p) * 16 + 32)
                wait_alone(pe, hid_done, n["hid"].at(-1))
                for m, w in enumerate((wg[p], wu[p])):
                    for k in range(KD):
                        for c in range(2):
                            ins = pe.matmul(ps[p][:, 2 * m + c, 0:HALF], w[:, k, :], h1T[:, k, c * HALF:(c + 1) * HALF],
                                            start=(k == 0), stop=(k == KD - 1))
                ins.then_inc(gu_ps, 1)

            def down(g, d, p, n):
                wait_alone(pe, wd_here[p], (n["down"].at(-1) - p) * 8 + 16)
                wait_alone(pe, hid_done, n["hid"].at())
                wait_alone(pe, z_done, n["z"].at(-2))
                for f in range(FC):
                    for c in range(2):
                        ins = pe.matmul(ps[p][:, c, 0:HALF], wd[p][:, f, :], hid[:, f, c * HALF:(c + 1) * HALF],
                                        start=(f == 0), stop=(f == FC - 1))
                ins.then_inc(down_ps, 1)

            def rows(g, r, m, n):
                if r == 0:
                    wait_alone(pe, z_done, n["z"].at())
                if r >= 2:
                    wait_alone(pe, y_done, n["y"].at(-1))
                for k in range(KD):
                    ins = pe.transpose(ps[r % 2][0:m, 2 + k // 4, (k % 4) * P:(k % 4 + 1) * P], zT[:, k, r * P:r * P + m],
                                       ident[:])
                ins.then_inc(t_ps, 1)

            pe.sem_inc(gu_ps, AHEAD["gu"])
            pe.sem_inc(down_ps, AHEAD["down"])
            run(pe, start, hidden, down, rows)

        @block.scalar
        def _(act):
            def hidden(g, f, p, n):
                act.wait_ge(gu_ps, n["gu"].at(1))
                act.wait_ge(hid_done, n["hid"].at(-1))
                act.activation(silu[:, p], ps[p][:, 0:2, 0:HALF], ACT.Silu).then_inc(silu_done, 1)

            def rows(g, r, m, n):
                act.wait_ge(var_done, n["var"].at(1))
                act.activation(sd[0:m], mv[0:m, 1:2], ACT.Sqrt, bias=eps[0:m]).then_inc(sd_done, 1)

            act.wait_ge(eps_set, 1)
            run(act, lambda g, n: None, hidden, None, rows)

        @block.vector
        def _(v):
            def hidden(g, f, p, n):
                v.wait_ge(silu_done, n["silu"].at(1))
                v.tensor_tensor(hid[:, ds(f, 1), :].rearrange("p a (c n) -> p (a c) n", c=2), silu[:, p],
                                ps[p][:, 2:4, 0:HALF], ALU.mult).then_inc(hid_done, 1)

            def down(g, d, p, n):
                v.wait_ge(down_ps, n["down"].at(1))
                for c in range(2):
                    cols = slice(c * HALF, (c + 1) * HALF)
                    v.scalar_tensor_tensor(out=zT[:, ds(d, 1), cols].squeeze(1), in0=h1T[:, ds(d, 1), cols].squeeze(1),
                                           scalar=ALPHA, in1=ps[p][:, c, 0:HALF], op0=ALU.mult, op1=ALU.add)\
                        .then_inc(z_done, 1)

            def rows(g, r, m, n):
                x = ps[r % 2][0:m, 2:4, :].rearrange("p a b -> p (a b)")
                out = y[r % 2][0:m, :]
                ln = n["ln"].at
                v.wait_ge(t_ps, n["t"].at(1))
                for j in range(2):
                    v.bn_stats(stats[0:m, 6 * j:6 * j + 6], x[:, j * 512:(j + 1) * 512]).then_inc(ln_step, 1)
                wait_alone(v, ln_step, ln(2))
                v.bn_aggr(mv[0:m], stats[0:m]).then_inc(var_done, 1)
                v.wait_ge(sd_done, n["sd"].at(1))
                v.wait_ge(var_done, n["var"].at(1))
                v.reciprocal(rs[0:m], sd[0:m]).then_inc(ln_step, 1)
                v.wait_ge(ln_step, ln(3))
                v.wait_ge(y_stored[r % 2], (g * (BLOCKS // 2) + r // 2) * 16)
                v.tensor_scalar(out, x, mv[0:m, 0:1], rs[0:m], ALU.subtract, ALU.mult).then_inc(ln_step, 1)
                v.wait_ge(ln_step, ln(4))
                v.tensor_tensor(out, out, g2[0:m], ALU.mult).then_inc(ln_step, 1)
                v.wait_ge(ln_step, ln(5))
                v.tensor_tensor(out, out, b2[0:m], ALU.add).then_inc(y_done, 1)

            v.sem_inc(hid_done, AHEAD["hid"])
            v.sem_inc(z_done, AHEAD["z"])
            v.wait_ge(consts, 32)
            run(v, lambda g, n: None, hidden, down, rows)


NB = N_SAMPLE
BH = NB * HEADS
RUN = 4
CHUNK = P * RUN
CHUNKS = PAST // CHUNK
UNITS = PAGE // RUN
SROW = TOTAL
FAR = -1.0e30


def decode(nc, PN, PAGE_TABLE, CACHE_A, CACHE_I, CACHE_B, CACHE_LF, CONST, PMOD, EXPAND, OS, MT, keep):
    ident, ones = keep["ident"], keep["ones"]
    with ExitStack() as ctx:
        def sb(name, shape, dt=F32):
            return ctx.enter_context(nc.sbuf_tensor(name, shape, dt))

        def sem(name):
            return ctx.enter_context(nc.semaphore(name))

        after = sb("after", [P, P])
        expand = sb("expand", [P, BH])
        pmod = sb("pmod", [P, 1])
        pages = sb("pages", [P, NB, CHUNKS], I32)
        runs = sb("runs", [P, NB, CHUNKS], I32)
        run_now = [sb(f"run_now{p}", [P, NB], I32) for p in range(2)]
        q_b = sb("q_b", [P, NB * (BH + HEADS)])
        q_a = sb("q_a", [P, NB * (BH + HEADS)])
        q_i = sb("q_i", [P, NB * (P + HEADS)])
        kn_b = sb("kn_b", [P, NB])
        kn_a = sb("kn_a", [HD, NB])
        kn_i = sb("kn_i", [HD, NB])
        w_sel = sb("w_sel", [P, 2, NB])
        scores = sb("d_scores", [NB, PAST + 8])
        work = sb("d_work", [P, PAST + 8])
        top8 = sb("d_top8", [NB, 8])
        kv = sb("kv", [P, 2, NB, RUN * 256])
        lf = sb("d_lf", [P, 2, NB, RUN * HEADS])
        lf_r = sb("lf_r", [P, RUN, BH])
        lf_later = sb("lf_later", [P, BH])
        kT = sb("kT_d", [P, 2, CHUNK])
        relu = sb("d_relu", [P, CHUNK // 2])
        prob = sb("prob", [BH, CHUNK])
        pT = sb("d_pT", [P, RUN, NB * (BH + HEADS)])
        m_old = sb("m_old", [BH, 1])
        m_new = sb("m_new", [BH, 1])
        neg_m = sb("neg_m", [BH, 1])
        shrink = sb("shrink", [BH, 1])
        den = sb("den", [BH, 1])
        den_c = sb("den_c", [BH, 1])
        rden = sb("rden", [BH, 1])
        o = sb("o_d", [BH, P])

        tr = [ctx.enter_context(nc.psum_tensor(f"d_tr{b}", [P, 512], F32)) for b in range(2)]
        S = [ctx.enter_context(nc.psum_tensor(f"d_S{b}", [P, 512], F32)) for b in range(2)]
        pw = ctx.enter_context(nc.psum_tensor("d_pw", [P, 512], F32))
        pt = ctx.enter_context(nc.psum_tensor("d_pt", [P, 512], F32))
        po = ctx.enter_context(nc.psum_tensor("d_po", [P, 512], F32))

        in_dma = sem("d_in_dma")
        pages_here = sem("d_pages")
        zeroed = sem("d_zeroed")
        prep = sem("d_prep")
        topk_step = sem("d_topk_step")

        def own(q, b_cols):
            return q.rearrange("p (b x) -> p b x", x=BH + HEADS)[:, :, b_cols]

        with nc.Block() as block:
            @block.sync
            def _(sp):
                sp.dma_start(after[:], CONST[3]).then_inc(in_dma, 16)
                sp.dma_start(expand[:], EXPAND).then_inc(in_dma, 16)
                sp.dma_start(pmod[:], PMOD).then_inc(in_dma, 16)
                with nc.allow_non_contiguous_dma(reason="the page table once per partition"):
                    for q in range(P // UNITS):
                        sp.dma_start(pages[q * UNITS:(q + 1) * UNITS].rearrange("p b c -> p (b c)"),
                                     PAGE_TABLE.rearrange("b (c q) -> q (b c)", q=RUN)[q:q + 1, :].to_broadcast([UNITS, NB * CHUNKS]))\
                            .then_inc(pages_here, 16)
                wait_alone(sp, zeroed, 5)
                rows = PN[SROW:SROW + NB, :]
                with nc.allow_non_contiguous_dma(reason="a few thousand elements"):
                    for g in range(2):
                        half = slice(g * HD, (g + 1) * HD)
                        for b in range(NB):
                            row = PN[SROW + b:SROW + b + 1, :]
                            sp.dma_start(own(q_b[half], slice(4 * g, 4 * g + 4))[:, b, :],
                                         row[:, QB + g * 256:QB + (g + 1) * 256].rearrange("o (h d) -> d (o h)", d=HD)).then_inc(in_dma, 16)
                            sp.dma_start(own(q_a[half], slice(0, HEADS))[:, b, :],
                                         row[:, QA:QA + 512].rearrange("o (h d) -> d (o h)", d=HD)).then_inc(in_dma, 16)
                            at = b * (P + HEADS) + g * HD
                            sp.dma_start(q_i[half, at:at + HEADS],
                                         row[:, QI:QI + 512].rearrange("o (h d) -> d (o h)", d=HD)).then_inc(in_dma, 16)
                    sp.dma_start(kn_b[:], rows[:, KB:KB + P].rearrange("b n -> n b")).then_inc(in_dma, 16)
                    sp.dma_start(kn_a[:], rows[:, KA:KA + HD].rearrange("b n -> n b")).then_inc(in_dma, 16)
                    sp.dma_start(kn_i[:], rows[:, KI:KI + HD].rearrange("b n -> n b")).then_inc(in_dma, 16)
                    for b in range(NB):
                        for g in range(2):
                            at = g * BH + b * HEADS
                            sp.dma_start(w_sel[at:at + HEADS, g, b:b + 1],
                                         rows[b:b + 1, WI:WI + HEADS].rearrange("o h -> h o")).then_inc(in_dma, 16)
                        sp.dma_start(lf_later[0:1, b * HEADS:(b + 1) * HEADS], rows[b:b + 1, FL:FL + HEADS]).then_inc(in_dma, 16)
                wait_alone(sp, in_dma, 16 * (3 + 6 * NB + 3 + 3 * NB))

            @block.gpsimd
            def _(pool):
                pool.memset(q_b[:], 0.0).then_inc(zeroed, 1)
                pool.memset(q_a[:], 0.0).then_inc(zeroed, 1)
                pool.memset(q_i[:], 0.0).then_inc(zeroed, 1)
                pool.memset(w_sel[:], 0.0).then_inc(zeroed, 1)
                pool.memset(lf_later[:], 0.0).then_inc(zeroed, 1)
                pool.memset(pT[:], 0.0)
                pool.memset(work[:], 0.0)
                pool.memset(lf_r[:], 0.0)

            @block.vector
            def _(v):
                v.wait_ge(pages_here, 16 * (P // UNITS))
                v.wait_ge(in_dma, 16 * (3 + 6 * NB + 3 + 3 * NB))
                v.tensor_scalar(runs[:], pages[:], float(UNITS), pmod[:], ALU.mult, ALU.add).then_inc(prep, 1)
                for q in (q_b, q_a):
                    v.tensor_scalar(q[:], q[:], HD ** -0.5, None, ALU.mult).then_inc(prep, 1)

        def heads_of(q, rows, b, width=BH):
            return q[rows, b * width:b * width + BH]

        def walk(kind):
            width = {"i": HD, "a": 2 * HD, "b": 4 * HD}[kind]
            pool_rows = {"i": CACHE_I, "a": CACHE_A, "b": CACHE_B}[kind]
            vcol, vw = {"i": (0, 0), "a": (HD, HD), "b": (P, P)}[kind]
            q = {"i": q_i, "a": q_a, "b": q_b}[kind]
            knew = {"i": kn_i, "a": kn_a, "b": kn_b}[kind]
            kd = P if kind == "b" else HD
            nblk = RUN // 2 if kind == "i" else RUN
            with ExitStack() as sub:
                def ksem(name):
                    return sub.enter_context(nc.semaphore(f"{kind}_{name}"))

                kv_here = [ksem(f"kv_here{p}") for p in range(2)]
                v0_here = ksem("v0_here")
                idx_done = ksem("idx_done")
                turned = ksem("turned")
                kt_copied = ksem("kt_copied")
                qk = ksem("qk")
                s_full = ksem("s_full")
                s_read = ksem("s_read")
                lf_step = ksem("lf_step")
                w_ps = ksem("w_ps")
                w_read = ksem("w_read")
                mx = ksem("mx")
                shrunk = ksem("shrunk")
                pt_ps = ksem("pt_ps")
                pt_copied = ksem("pt_copied")
                pv_ps = ksem("pv_ps")
                upd = ksem("upd")
                stored = ksem("stored")
                PER = dict(seq=NB, chunk=1, mx=4, upd=2, lf=5)

                def run(eng, body):
                    n = {k: Tally() for k in PER}
                    with eng.Fori(0, CHUNKS // 2) as i:
                        for k, per in PER.items():
                            n[k].enter(i, 2 * per)
                        for p in range(2):
                            body(i * -2 + (CHUNKS - 1 - p), p, i, n)
                            for k, per in PER.items():
                                n[k].add(per)
                        for k, per in PER.items():
                            n[k].leave(CHUNKS // 2, 2 * per)
                    return n

                attn = kind != "i"
                block = sub.enter_context(nc.Block())

                @block.sync
                def _(sp):
                    if not attn:
                        return
                    base = {"a": VA, "b": VB}[kind]
                    for b in range(NB):
                        sp.dma_start(o[b * HEADS:(b + 1) * HEADS, 0:vw],
                                     PN[SROW + b:SROW + b + 1, base:base + vw].to_broadcast([HEADS, vw])).then_inc(v0_here, 16)
                    wait_alone(sp, upd, 2 * CHUNKS + 2)
                    out = OS[kind == "b"]
                    sp.dma_start(out[:, 0:vw], o[:, 0:vw]).then_inc(stored, 16)
                    wait_alone(sp, stored, 16)
                    tile0 = (TILES - 1) * P
                    with nc.allow_non_contiguous_dma(reason="a few thousand elements"):
                        for h in range(HEADS):
                            c = h // 2 + (4 if kind == "b" else 0)
                            v0 = (h // 4) * HD if kind == "b" else 0
                            row = tile0 + (h % 2) * HD
                            sp.dma_start(MT[row:row + HD, c * P + N_META:c * P + N_META + NB],
                                         out.rearrange("(b h) n -> h n b", h=HEADS)[h, v0:v0 + HD, :]).then_inc(stored, 16)
                    wait_alone(sp, stored, 16 * (1 + HEADS))

                @block.gpsimd
                def _(pool):
                    def chunk(c, p, i, n):
                        if attn:
                            wait_alone(pool, pv_ps, n["chunk"].at())
                        else:
                            wait_alone(pool, turned, n["seq"].at())
                        pool.tensor_copy(run_now[p][:], runs[:, :, ds(c, 1)].rearrange("p b o -> p (b o)")).then_inc(idx_done, 1)
                        wait_alone(pool, idx_done, n["chunk"].at(1))
                        for b in range(NB):
                            at = bass.IndirectOffsetOnAxis(ap=run_now[p][:, b:b + 1], axis=0)
                            pool.indirect_dma_start(kv[:, p, b, 0:RUN * width], None, pool_rows, at).then_inc(kv_here[p], 16)
                            if kind == "b":
                                pool.indirect_dma_start(lf[:, p, b, :], None, CACHE_LF, at).then_inc(kv_here[p], 16)

                    run(pool, chunk)

                @block.tensor
                def _(pe):
                    pe.sem_inc(turned, NB)
                    if attn:
                        pe.sem_inc(pv_ps, 1)
                    for b in range(NB):
                        ins = pe.matmul(S[1][0:BH, 0:1], heads_of(q, slice(0, kd), b, BH if attn else P), knew[0:kd, b:b + 1], start=(b == 0),
                                        stop=(b == NB - 1 and kind != "a"))
                    ins.then_inc(qk, 1)
                    if kind == "a":
                        pe.matmul(S[1][0:BH, 0:1], expand[:], work[:, PAST:PAST + 1], start=False, stop=True).then_inc(s_full, 1)
                    if kind == "i":
                        wait_alone(pe, s_read, 1)
                        pe.matmul(pw[0:NB, 0:1], w_sel[0:BH, 0], relu[0:BH, 0:1], start=True, stop=True).then_inc(w_ps, 1)

                    def turn_keys(p, b, n):
                        wait_alone(pe, kt_copied, n["seq"].at(b))
                        keys = kv[:, p, b, 0:RUN * width]
                        for r in range(nblk):
                            at = r * max(width, P)
                            ins = pe.transpose(tr[b % 2][:, r * P:(r + 1) * P], keys[:, at:at + P], ident[:])
                        ins.then_inc(turned, 1)

                    def products(p, b, n):
                        wait_alone(pe, kt_copied, n["seq"].at(b + 2))
                        out = S[p][0:BH, :]
                        if attn:
                            ins = pe.matmul(out, heads_of(q, slice(0, kd), b), kT[0:kd, b % 2, :], start=(b == 0), stop=False)
                        else:
                            ins = pe.matmul(S[p][:, 0:2 * P], q_i[:, b * P:(b + 1) * P], kT[:, b % 2, 0:2 * P], start=(b == 0),
                                            stop=(b == NB - 1))
                        ins.then_inc(qk, 1)

                    def chunk(c, p, i, n):
                        out = S[p][0:BH, :]
                        wait_alone(pe, kv_here[p], (i + 1) * (16 * NB * (2 if kind == "b" else 1)))
                        turn_keys(p, 0, n)
                        for b in range(NB):
                            if b + 1 < NB:
                                turn_keys(p, b + 1, n)
                            if b == 0:
                                wait_alone(pe, s_read, n["chunk"].at())
                            products(p, b, n)
                        if kind == "b":
                            wait_alone(pe, lf_step, n["lf"].at(5))
                            for r in range(RUN - 1):
                                pe.matmul(out[:, r * P:(r + 1) * P], lf_r[:, r, :], ident[:], start=False, stop=False)
                            pe.matmul(out, lf_r[:, RUN - 1, :], after[:].unsqueeze(1).to_broadcast([P, RUN, P]), start=False, stop=False)
                            pe.matmul(out, lf_later[:], ones[:].unsqueeze(1).to_broadcast([P, RUN, P]), start=False, stop=True).then_inc(s_full, 1)
                        elif kind == "a":
                            pe.matmul(out, expand[:], work[:, ds(c * CHUNK, CHUNK)].rearrange("p (n r) -> p r n", r=RUN),
                                      start=False, stop=True).then_inc(s_full, 1)
                        else:
                            wait_alone(pe, s_read, n["chunk"].at(2))
                            wait_alone(pe, w_read, n["chunk"].at(1))
                            for g in range(2):
                                ins = pe.matmul(pw[0:NB, g * 2 * P:(g + 1) * 2 * P], w_sel[:, g], relu[:], start=True, stop=True)
                            ins.then_inc(w_ps, 1)
                        if attn:
                            wait_alone(pe, s_read, n["chunk"].at(2))
                            wait_alone(pe, pt_copied, n["chunk"].at())
                            for r in range(RUN):
                                ins = pe.transpose(pt[:, r * BH:(r + 1) * BH], prob[:, r * P:(r + 1) * P], ident[0:BH, 0:BH])
                            ins.then_inc(pt_ps, 1)
                            wait_alone(pe, pt_copied, n["chunk"].at(1))
                            wait_alone(pe, upd, n["upd"].at())
                            for b in range(NB):
                                for r in range(RUN):
                                    at = r * width + vcol
                                    ins = pe.matmul(po[0:BH, 0:vw], heads_of(pT[:, r, :], slice(0, P), b), kv[:, p, b, at:at + vw],
                                                    start=(b == 0 and r == 0), stop=(b == NB - 1 and r == RUN - 1))
                            ins.then_inc(pv_ps, 1)

                    run(pe, chunk)

                @block.scalar
                def _(act):
                    act.sem_inc(kt_copied, 1)
                    if kind == "i":
                        act.wait_ge(qk, 1)
                        act.activation(relu[0:BH, 0:1], S[1][0:BH, 0:1], ACT.Relu, scale=HD ** -0.5 * HEADS ** -0.5).then_inc(s_read, 1)

                    def chunk(c, p, i, n):
                        for b in range(NB):
                            act.wait_ge(turned, n["seq"].at(b + 1 + NB))
                            act.wait_ge(qk, n["seq"].at(b))
                            rows = slice(0, HD if kind == "a" else P)
                            act.activation(kT[rows, b % 2, 0:nblk * P], tr[b % 2][rows, 0:nblk * P], ACT.Copy).then_inc(kt_copied, 1)
                        if kind == "i":
                            act.wait_ge(qk, n["seq"].at(NB + 1))
                            act.wait_ge(w_ps, n["chunk"].at(1))
                            act.activation(relu[:], S[p][:, 0:2 * P], ACT.Relu, scale=HD ** -0.5 * HEADS ** -0.5).then_inc(s_read, 1)
                            return
                        act.wait_ge(mx, n["mx"].at(3 + 1))
                        act.wait_ge(upd, n["upd"].at())
                        act.activation(shrink[:], m_old[:], ACT.Exp, bias=neg_m[:]).then_inc(shrunk, 1)
                        act.wait_ge(pt_ps, n["chunk"].at())
                        act.activation(prob[:], S[p][0:BH, :], ACT.Exp, bias=neg_m[:], accum_out=den_c[:]).then_inc(s_read, 1)
                        act.wait_ge(pt_ps, n["chunk"].at(1))
                        act.wait_ge(pv_ps, n["chunk"].at(1))
                        act.activation(pT[:].rearrange("p r (b x) -> p r b x", x=BH + HEADS)[:, :, :, 0:HEADS],
                                       pt[:, 0:RUN * BH].rearrange("p (r b h) -> p r b h", r=RUN, b=NB), ACT.Copy).then_inc(pt_copied, 1)

                    run(act, chunk)

                @block.vector
                def _(v):
                    if kind == "i":
                        v.wait_ge(w_ps, 1)
                        v.tensor_copy(scores[:, PAST:PAST + 1], pw[0:NB, 0:1]).then_inc(w_read, 1)
                    else:
                        v.memset(den[:], 1.0).then_inc(mx, 1)
                        v.wait_ge(s_full if kind == "a" else qk, 1)
                        v.tensor_copy(m_old[:], S[1][0:BH, 0:1]).then_inc(s_read, 1)
                        v.wait_ge(v0_here, 16 * NB)

                    full = {"a": 2, "b": 1, "i": 0}[kind]

                    def chunk(c, p, i, n):
                        if kind == "i":
                            v.wait_ge(w_ps, n["chunk"].at(2))
                            v.tensor_copy(scores[:, ds(c * CHUNK, CHUNK)].rearrange("p (n j g) -> p g j n", j=2, g=2),
                                          pw[0:NB, :].rearrange("p (g j n) -> p g j n", g=2, j=2)).then_inc(w_read, 1)
                            return
                        if kind == "b":
                            v.wait_ge(kv_here[p], (i + 1) * (32 * NB))
                            v.wait_ge(s_full, n["chunk"].at())
                            v.wait_ge(lf_step, n["lf"].at())
                            v.tensor_tensor(lf_later[:], lf_later[:], lf_r[:, RUN - 1, :], ALU.add).then_inc(lf_step, 1)
                            mine = lf[:, p].rearrange("p b (r h) -> p r b h", r=RUN)
                            sums = lf_r[:].rearrange("p r (b h) -> p r b h", b=NB)
                            v.wait_ge(lf_step, n["lf"].at(1))
                            v.tensor_copy(sums[:, 2], mine[:, 3]).then_inc(lf_step, 1)
                            for k, (to, frm) in enumerate(((1, 2), (0, 1), (3, 0))):
                                v.wait_ge(lf_step, n["lf"].at(2 + k))
                                v.tensor_tensor(sums[:, to], sums[:, frm], mine[:, frm], ALU.add).then_inc(lf_step, 1)
                        v.wait_ge(s_full, n["chunk"].at(full))
                        v.reduce_max(m_new[:], S[p][0:BH, :], AX.X).then_inc(mx, 1)
                        v.wait_ge(s_read, n["chunk"].at(1))
                        v.wait_ge(mx, n["mx"].at(2))
                        v.tensor_tensor(m_new[:], m_new[:], m_old[:], ALU.max).then_inc(mx, 1)
                        v.wait_ge(mx, n["mx"].at(3))
                        v.tensor_scalar(neg_m[:], m_new[:], -1.0, None, ALU.mult).then_inc(mx, 1)
                        v.wait_ge(shrunk, n["chunk"].at(1))
                        v.tensor_copy(m_old[:], m_new[:]).then_inc(mx, 1)
                        v.wait_ge(s_read, n["chunk"].at(2))
                        v.wait_ge(upd, n["upd"].at())
                        v.wait_ge(mx, n["mx"].at(5))
                        v.scalar_tensor_tensor(out=den[:], in0=den[:], scalar=shrink[:], in1=den_c[:], op0=ALU.mult, op1=ALU.add)\
                            .then_inc(upd, 1)
                        v.wait_ge(pv_ps, n["chunk"].at(2))
                        v.scalar_tensor_tensor(out=o[:, 0:vw], in0=o[:, 0:vw], scalar=shrink[:], in1=po[0:BH, 0:vw],
                                               op0=ALU.mult, op1=ALU.add).then_inc(upd, 1)

                    run(v, chunk)
                    if attn:
                        v.wait_ge(upd, 2 * CHUNKS)
                        v.reciprocal(rden[:], den[:]).then_inc(upd, 1)
                        v.wait_ge(upd, 2 * CHUNKS + 1)
                        v.tensor_scalar(o[:, 0:vw], o[:, 0:vw], rden[:], None, ALU.mult).then_inc(upd, 1)

        walk("i")

        with nc.Block() as block:
            @block.vector
            def _(v):
                keys = slice(0, PAST + 1)
                mine = work[0:NB, keys]
                with v.Fori(0, TOPK // 8) as i:
                    wait_alone(v, topk_step, i * 2 + 1)
                    v.max(top8[:], mine).then_inc(topk_step, 1)
                    wait_alone(v, topk_step, i * 2 + 2)
                    v.match_replace(mine, top8[:], mine, TAKEN).then_inc(topk_step, 1)
                v.wait_ge(topk_step, TOPK // 4 + 1)
                v.tensor_scalar(mine, mine, TAKEN, FAR, ALU.not_equal, ALU.mult)

            @block.gpsimd
            def _(pool):
                pool.tensor_copy(work[0:NB, 0:PAST + 1], scores[:, 0:PAST + 1]).then_inc(topk_step, 1)

        walk("a")
        walk("b")


def build_program(nc, a, o):
    def scratch(name, shape):
        return nc.dram_tensor(f"dram_{name}", shape, F32, kind="Internal").ap()

    QTA = scratch("QTA", [ROWS, 8 * P])
    QTB = scratch("QTB", [TILES * AUG, 8 * P])
    HN = scratch("HN", [ROWS, D])
    MT = scratch("MT", [ROWS, D])
    H1T = scratch("H1T", [D, ROWS])
    OS = [scratch(f"OS{k}", [BH, P]) for k in range(2)]
    PN, Y = o["PN"], o["Y"]
    with ExitStack() as consts:
        ident = consts.enter_context(nc.sbuf_tensor("ident", [P, P], F32))
        ones = consts.enter_context(nc.sbuf_tensor("ones", [P, P], F32))
        with ExitStack() as prompt:
            def sb(name, shape):
                return prompt.enter_context(nc.sbuf_tensor(name, shape, F32))

            keep = dict(ident=ident, ones=ones, tri=sb("tri", [P, P]), kaT=sb("kaT", [P, ROWS]), kiT=sb("kiT", [P, ROWS]),
                        kbT=sb("kbT", [P, 2, ROWS]), va1=sb("va1", [P, TILES, P]), vb1=sb("vb1", [P, TILES, 2, P]))
            project(nc, a["x_rows"], a["rope"], a["w_in"], a["ln_emb_g"], a["ln_emb_b"], a["b_forget"], a["matrices"],
                    PN, QTA, QTB, HN, keep)
            attend(nc, PN, QTA, QTB, a["mask"], MT, keep)
        keep = dict(ident=ident, ones=ones)
        decode(nc, PN, a["page_table"], a["cache_a"], a["cache_i"], a["cache_b"], a["cache_lf"], a["matrices"], a["pmod"],
               a["expand"], OS, MT, keep)
        mix_out(nc, MT, HN, a["w_o"], a["ln1_g"], a["ln1_b"], H1T, keep)
        feed_forward(nc, H1T, a["w_gate"], a["w_up"], a["w_down"], a["ln2_g"], a["ln2_b"], Y, keep)


def shape_constants():
    pos = np.zeros(ROWS, np.float32)
    pos[:TOTAL] = np.arange(TOTAL)
    pos[TOTAL:ALL] = PAST
    half = ROPE // 2
    inv = (np.float32(500000.0) ** (-np.arange(half, dtype=np.float32) / np.float32(half))).astype(np.float32)
    angle = (pos[:, None] * inv).astype(np.float32).astype(np.float64)
    cos, sin = np.cos(angle).astype(np.float32), np.sin(angle).astype(np.float32)
    square = np.ones((P, P), np.float32)
    expand = np.zeros((P, BH), np.float32)
    for b in range(NB):
        expand[b, b * HEADS:(b + 1) * HEADS] = 1.0
    behind = np.arange(2 * ROWS)[None, :] - ROWS > np.arange(P)[:, None]
    return dict(
        rope=np.concatenate([cos, cos, -sin, sin], 1),
        matrices=np.stack([np.eye(P, dtype=np.float32), np.triu(square), square, np.tril(square, -1)]),
        mask=np.where(behind, np.float32(NEG), np.float32(0.0)).astype(np.float32),
        pmod=(np.arange(P) % UNITS).astype(np.float32)[:, None].copy(),
        expand=expand,
    )


def kernel(x_prompt, x_sample, cache_a_kv, cache_idx_k, cache_b_kv, cache_b_logf, page_table, meta, ln_emb_g, ln_emb_b,
           w_in, b_forget, w_o, ln1_g, ln1_b, w_gate, w_up, w_down, ln2_g, ln2_b):
    import concourse.bacc as bacc
    from concourse.bass_utils import run_bass_kernel_spmd

    def arr(x):
        return np.ascontiguousarray(x)

    pad = np.zeros((ROWS - ALL, D), np.float32)
    arrays = dict(
        x_rows=np.concatenate([arr(meta), arr(x_prompt)[0], arr(x_sample)[:, 0], pad], 0),
        cache_a=arr(cache_a_kv).reshape(-1, RUN * 2 * HD), cache_i=arr(cache_idx_k).reshape(-1, RUN * HD),
        cache_b=arr(cache_b_kv).reshape(-1, RUN * 4 * HD), cache_lf=arr(cache_b_logf).reshape(-1, RUN * HEADS),
        page_table=arr(page_table), ln_emb_g=arr(ln_emb_g), ln_emb_b=arr(ln_emb_b), w_in=arr(w_in)[0], b_forget=arr(b_forget),
        w_o=arr(w_o)[0], ln1_g=arr(ln1_g)[0], ln1_b=arr(ln1_b)[0], w_gate=arr(w_gate)[0], w_up=arr(w_up)[0],
        w_down=arr(w_down)[0], ln2_g=arr(ln2_g)[0], ln2_b=arr(ln2_b)[0], **shape_constants())

    nc = bacc.Bacc("TRN2", target_bir_lowering=False, num_devices=1)
    arrays = {f"in_{n}": x for n, x in arrays.items()}
    ins = {n[3:]: nc.dram_tensor(n, x.shape, mybir.dt.from_np(x.dtype), kind="ExternalInput").ap() for n, x in arrays.items()}
    outs = {n: nc.dram_tensor(f"out_{n}", shape, F32, kind="ExternalOutput").ap() for n, shape in (("PN", (ROWS, N_IN)), ("Y", (ROWS, D)))}
    build_program(nc, ins, outs)
    got = run_bass_kernel_spmd(nc, [arrays], core_ids=[0]).results[0]
    pn, y = got["out_PN"], got["out_Y"]

    def rows(first, last, c0, c1, *shape):
        return np.ascontiguousarray(pn[first:last, c0:c1]).reshape(shape)

    n = N_SAMPLE
    return (y[N_META:TOTAL][None], y[TOTAL:ALL][:, None],
            rows(0, TOTAL, KA, KA + 2 * HD, 1, 1, TOTAL, 2, 1, HD), rows(0, TOTAL, KI, KI + HD, 1, 1, TOTAL, HD),
            rows(0, TOTAL, KB, KB + 4 * HD, 1, 1, TOTAL, 2, 2, HD), rows(0, TOTAL, FL, FL + HEADS, 1, 1, TOTAL, HEADS),
            rows(TOTAL, ALL, KA, KA + 2 * HD, 1, n, 1, 2, 1, HD), rows(TOTAL, ALL, KI, KI + HD, 1, n, 1, HD),
            rows(TOTAL, ALL, KB, KB + 4 * HD, 1, n, 1, 2, 2, HD), rows(TOTAL, ALL, FL, FL + HEADS, 1, n, 1, HEADS))
```

```python
from contextlib import ExitStack

import numpy as np

import concourse.bass as bass
from concourse import mybir

F32 = mybir.dt.float32
F32R = mybir.dt.float32r
I32 = mybir.dt.int32
ALU = mybir.AluOpType
ACT = mybir.ActivationFunctionType
AX = mybir.AxisListType
ds = bass.ds

P = 128
D = 1024
KD = D // P
N_META, SEQ, N_SAMPLE = 16, 2048, 8
TOTAL = N_META + SEQ
ALL = TOTAL + N_SAMPLE
TILES = -(-ALL // P)
ROWS = TILES * P
HD = 64
HEADS = 8
PAST, PAGE = 8192, 128
PAGES = PAST // PAGE
TOPK = 256
ROPE = 16
D_FF = 2816
EPS = 1e-5
ALPHA = 2.0 ** 0.25
QA, KA, VA, QI, KI, WI, QB, KB, VB, FL = 0, 512, 576, 640, 1152, 1216, 1224, 1736, 1864, 1992
N_IN = 2000
PROJ_CHUNKS = 4
PROJ_W = N_IN // PROJ_CHUNKS
AUG = HD + HEADS + 1
NEG = float(np.float32(-3.0e38))
TAKEN = float(np.float32(-3.3e38))


def wait_alone(eng, semaphore, value):
    eng.wait_ge(semaphore, value)
    if not isinstance(value, int):
        eng.nop(nofuse=True)


class Chain:

    def __init__(self, eng, sem):
        self.eng, self.sem, self.n, self.base = eng, sem, 0, 0

    def step(self, ins):
        ins.then_inc(self.sem, 1)
        self.n += 1

    def wait(self):
        self.eng.wait_ge(self.sem, self.base + self.n)

    def wait_alone(self):
        wait_alone(self.eng, self.sem, self.base + self.n)

    def start_loop(self, i, first, per):
        self.outer = self.n
        self.base = (i - first) * per
        self.n0 = self.n

    def end_loop(self, turns, per):
        assert self.n - self.n0 == per, (self.n - self.n0, per)
        self.base = 0
        self.n = self.n0 + turns * per


def layer_norm_stats(chain, x, stats, mv):
    v = chain.eng
    for c in range(D // 512):
        chain.step(v.bn_stats(stats[:, 6 * c:6 * c + 6], x[:, 512 * c:512 * c + 512]))
    chain.wait_alone()
    chain.step(v.bn_aggr(mv, stats))
    chain.wait()


def project(nc, X, RT, W_IN, LN_G, LN_B, BF, CONST, PN, QTA, QTB, HN, keep):
    ka_high, ka_low, ki_high, ki_low = (keep[k] for k in ("ka_high", "ka_low", "ki_high", "ki_low"))
    kbT, va1, vb1, ident, tri, ones = (keep[k] for k in ("kbT", "va1", "vb1", "ident", "tri", "ones"))
    with ExitStack() as ctx:
        def sb(name, shape, dt=F32):
            return ctx.enter_context(nc.sbuf_tensor(name, shape, dt))

        def sem(name):
            return ctx.enter_context(nc.semaphore(name))

        w_in = sb("w_in", [P, KD, N_IN])
        g_emb = sb("g_emb", [P, D])
        b_emb = sb("b_emb", [P, D])
        bf = sb("bf", [P, HEADS])
        x_in = [sb(f"x_in{p}", [P, D]) for p in range(2)]
        rt = [sb(f"rt{p}", [P, 2 * ROPE]) for p in range(2)]
        hT = [sb(f"hT{p}", [P, KD, P]) for p in range(2)]
        pn = [sb(f"pn{p}", [P, N_IN]) for p in range(2)]
        rope_a = sb("rope_a", [P, 2, 9, ROPE])
        rope_b = sb("rope_b", [P, 2, 9, ROPE])
        kdup = sb("kdup", [P, 2, 2, HD])
        q_aug = sb("q_aug", [P, HEADS, AUG])
        k_aug = sb("k_aug", [P, 2, AUG])
        qaiT = sb("qaiT", [P, 2, 4, P])
        qbT = sb("qbT", [AUG, 2, 4, P])
        lf_sum = sb("lf_sum", [P, HEADS])
        stats = sb("stats", [P, 12])
        mv = sb("mv", [P, 2])
        sd = sb("sd", [P, 1])
        rs = sb("rs", [P, 1])
        eps = sb("eps", [P, 1])
        z = sb("z", [P, HEADS])
        az = sb("az", [P, HEADS])
        sp_e = sb("sp_e", [P, HEADS])
        sp_l = sb("sp_l", [P, HEADS])
        pT = ctx.enter_context(nc.psum_tensor("pT", [P, 2, 512], F32))
        pP = ctx.enter_context(nc.psum_tensor("pP", [P, 4, 512], F32))
        pQ = ctx.enter_context(nc.psum_tensor("pQ", [P, 2, 512], F32))
        c_ps = pT[:, 0, 0:HEADS]

        w_here = sem("w_here")
        consts_here = sem("consts_here")
        x_here = [sem(f"x_here{p}") for p in range(2)]
        x_free = sem("x_free")
        var_done = sem("var_done")
        sd_done = sem("sd_done")
        h_done = sem("h_done")
        hT_ps = sem("hT_ps")
        hT_done = sem("hT_done")
        proj_ps = sem("proj_ps")
        pn_done = sem("pn_done")
        az_done = sem("az_done")
        spl_done = sem("spl_done")
        act_own = sem("act_own")
        lf_done = sem("lf_done")
        lf_sum_done = sem("lf_sum_done")
        c_sum_ps = sem("c_sum_ps")
        aug_done = sem("aug_done")
        q_ps = sem("q_ps")
        q_evac = sem("q_evac")
        pn_stored = [sem(f"pn_stored{p}") for p in range(2)]
        h_stored = [sem(f"h_stored{p}") for p in range(2)]
        q_stored = sem("q_stored")
        kdup_done = sem("kdup_done")
        pool_init = sem("pool_init")
        dve = sem("dve1")

        LAST = TILES - 1

        def tiles(eng, body, chain=None, per=0):
            body(0, 0, 0)
            body(1, 1, 0)
            with eng.Fori(1, TILES // 2) as i:
                if chain:
                    chain.start_loop(i, 1, per)
                body(2 * i, 0, i)
                body(2 * i + 1, 1, i)
                if chain:
                    chain.end_loop(TILES // 2 - 1, per)
            body(LAST, 0, TILES // 2)

        def is_first(t):
            return isinstance(t, int) and t == 0

        def is_last(t):
            return isinstance(t, int) and t == LAST

        block = ctx.enter_context(nc.Block())

        @block.sync
        def _(sp):
            sp.dma_start(g_emb[:], LN_G.unsqueeze(0).to_broadcast([P, D])).then_inc(consts_here, 16)
            sp.dma_start(b_emb[:], LN_B.unsqueeze(0).to_broadcast([P, D])).then_inc(consts_here, 16)
            sp.dma_start(bf[:], BF.to_broadcast([P, HEADS])).then_inc(consts_here, 16)
            sp.dma_start(ident[:], CONST[0]).then_inc(consts_here, 16)
            sp.dma_start(tri[:], CONST[1]).then_inc(consts_here, 16)
            sp.dma_start(ones[:], CONST[2]).then_inc(consts_here, 16)

            def load(t, p, i):
                if not (isinstance(t, int) and t < 2):
                    wait_alone(sp, x_free, t - 1)
                    wait_alone(sp, h_stored[p], 16 * i)
                sp.dma_start(x_in[p][:], X[ds(t * P, P), :]).then_inc(x_here[p], 16)
                sp.dma_start(rt[p][:], RT[ds(t * P, P), :]).then_inc(x_here[p], 16)
                if is_first(t):
                    for k in range(KD):
                        sp.dma_start(w_in[:, k, :], W_IN[k * P:(k + 1) * P, :]).then_inc(w_here, 16)

            tiles(sp, load)

        @block.gpsimd
        def _(pool):
            pool.memset(eps[:], EPS)
            pool.memset(lf_sum[:], 0.0)
            pool.memset(va1[:, :, HD:2 * HD], 1.0)
            pool.memset(vb1[:, :, :, HD:2 * HD], 1.0)
            pool.memset(k_aug[:, :, AUG - 1:AUG], 1.0)
            pool.memset(q_aug[:, :, HD:AUG], 0.0).then_inc(pool_init, 1)
            pool.wait_ge(pool_init, 1)
            for h in range(HEADS):
                pool.memset(q_aug[:, h, HD + h:HD + h + 1], 1.0).then_inc(pool_init, 1)

            def stage(t, p, i):
                wait_alone(pool, h_done, t + 1)
                pool.dma_start(HN[ds(t * P, P), :], x_in[p][:]).then_inc(h_stored[p], 16)
                wait_alone(pool, lf_done, t + 1)
                pool.dma_start(PN[ds(t * P, P), :], pn[p][:]).then_inc(pn_stored[p], 16)
                if not is_first(t):
                    wait_alone(pool, q_ps, t * 5)
                for c in range(2):
                    pool.tensor_copy(kdup[:, 0, c, :], pn[p][:, KA:KA + HD])
                    pool.tensor_copy(kdup[:, 1, c, :], pn[p][:, KI:KI + HD])
                pool.tensor_copy(va1[:, ds(t, 1), 0:HD].squeeze(1), pn[p][:, VA:VA + HD])
                for g in range(2):
                    pool.tensor_copy(vb1[:, ds(t, 1), g, 0:HD].squeeze(1), pn[p][:, VB + g * HD:VB + (g + 1) * HD])
                pool.tensor_copy(q_aug[:, :, 0:HD], pn[p][:, QB:QB + 512].rearrange("p (h d) -> p h d", d=HD))
                pool.tensor_copy(k_aug[:, :, 0:HD],
                                 pn[p][:, KB:KB + 128].rearrange("p (h d) -> p h d", d=HD)).then_inc(kdup_done, 1)
                if not is_first(t):
                    store_q(t - 1)

            def store_q(t):
                wait_alone(pool, q_evac, 5 * (t + 1))
                pool.dma_start(QTA[ds(t * P, P), :], qaiT[:].rearrange("p a b c -> p (a b c)")).then_inc(q_stored, 16)
                pool.dma_start(QTB[ds(t * AUG, AUG), :], qbT[:].rearrange("p a b c -> p (a b c)")).then_inc(q_stored, 16)

            tiles(pool, stage)
            store_q(LAST)
            pool.wait_ge(q_stored, 32 * TILES)
            for p in range(2):
                pool.wait_ge(h_stored[p], 16 * (TILES // 2 + 1 - p))
                pool.wait_ge(pn_stored[p], 16 * (TILES // 2 + 1 - p))

        @block.tensor
        def _(pe):
            def turn_h(t, p):
                pe.wait_ge(h_done, t + 1)
                if not is_first(t):
                    pe.wait_ge(hT_done, t)
                if not (isinstance(t, int) and t < 3):
                    pe.wait_ge(aug_done, t - 2)
                for k in range(KD):
                    ins = pe.transpose(pT[:, k // 4, (k % 4) * P:(k % 4 + 1) * P], x_in[p][:, k * P:(k + 1) * P], ident[:])
                ins.then_inc(hT_ps, 1)

            def turn_q(t, p):
                pe.wait_ge(kdup_done, t + 1)
                pe.wait_ge(aug_done, t + 1)
                for b in range(5):
                    if is_first(t) and b < 2:
                        pass
                    else:
                        pe.wait_ge(q_evac, t * 5 + max(b - 1, 0))
                    out = pQ[:, b % 2, :].rearrange("p (c n) -> p c n", c=4)
                    for c in range(4):
                        if b == 0:
                            ins = pe.transpose(out[:, c, :], pn[p][:, QA + c * P:QA + (c + 1) * P], ident[:])
                        elif b == 1:
                            ins = pe.transpose(out[:, c, :], pn[p][:, QI + c * P:QI + (c + 1) * P], ident[:])
                        elif b == 2 and c < 2:
                            ins = pe.transpose(out[:, c, :], kdup[:, c, :, :].rearrange("p a b -> p (a b)"), ident[:])
                        elif b == 2:
                            ins = pe.transpose(out[0:AUG, c, :], k_aug[:, c - 2, :], ident[:])
                        else:
                            ins = pe.transpose(out[0:AUG, c, :], q_aug[:, (b - 3) * 4 + c, :], ident[:])
                    ins.then_inc(q_ps, 1)

            def forget_sum(t, p):
                pe.wait_ge(lf_done, t + 1)
                pe.wait_ge(hT_done, TILES if is_last(t) or is_last(t + 1) else t + 3)
                pe.matmul(c_ps, tri[:], pn[p][:, FL:FL + HEADS], start=True, stop=False)
                pe.matmul(c_ps, ones[:], lf_sum[:], start=False, stop=True).then_inc(c_sum_ps, 1)

            def tile(t, p, i):
                if not is_last(t):
                    turn_h(t + 1, 1 - p)
                pe.wait_ge(hT_done, t + 1)
                for j in range(PROJ_CHUNKS):
                    if not is_first(t):
                        pe.wait_ge(pn_done, (t - 1) * PROJ_CHUNKS + j + 1)
                    for k in range(KD):
                        if is_first(t) and j == 0:
                            pe.wait_ge(w_here, 16 * KD)
                        ins = pe.matmul(pP[:, j, 0:PROJ_W], hT[p][:, k, :], w_in[:, k, j * PROJ_W:(j + 1) * PROJ_W],
                                        start=(k == 0), stop=(k == KD - 1))
                    ins.then_inc(proj_ps, 1)
                    if j == 0 and not is_first(t):
                        forget_sum(t - 1, 1 - p)
                if not is_first(t):
                    turn_q(t - 1, 1 - p)

            pe.wait_ge(consts_here, 96)
            pe.wait_ge(pool_init, 1 + HEADS)
            turn_h(0, 0)
            tiles(pe, tile)
            forget_sum(LAST, 0)
            turn_q(LAST, 0)

        @block.scalar
        def _(act):
            def tile(t, p, i):
                if not is_last(t):
                    head(t + 1, 1 - p)
                if not (isinstance(t, int) and t < 2):
                    act.wait_ge(pn_stored[p], 16 * i)
                    act.wait_ge(q_ps, 5 * (t - 1))
                    act.wait_ge(kdup_done, t - 1)
                for j in range(PROJ_CHUNKS):
                    act.wait_ge(proj_ps, t * PROJ_CHUNKS + j + 1)
                    act.activation(pn[p][:, j * PROJ_W:(j + 1) * PROJ_W], pP[:, j, 0:PROJ_W], ACT.Copy).then_inc(pn_done, 1)
                act.wait_ge(az_done, t + 1)
                act.activation(sp_e[:], az[:], ACT.Exp, scale=-1.0).then_inc(act_own, 1)
                act.wait_ge(act_own, t + 1)
                act.activation(sp_l[:], sp_e[:], ACT.Ln, bias=ones[:, 0:1]).then_inc(spl_done, 1)
                if not is_first(t):
                    copy_q(t - 1)

            def head(t, p):
                act.wait_ge(var_done, t + 1)
                act.activation(sd[:], mv[:, 1:2], ACT.Sqrt, bias=eps[:]).then_inc(sd_done, 1)
                act.wait_ge(hT_ps, t + 1)
                if not (isinstance(t, int) and t < 2):
                    act.wait_ge(proj_ps, (t - 1) * PROJ_CHUNKS)
                act.activation(hT[p][:].rearrange("p a b -> p (a b)"), pT[:].rearrange("p a b -> p (a b)"),
                               ACT.Copy).then_inc(hT_done, 1)

            def copy_q(t):
                if not is_first(t):
                    act.wait_ge(q_stored, 32 * t)
                for b in (0, 1, 3, 4):
                    act.wait_ge(q_ps, t * 5 + b + 1)
                    out, rows = (qaiT[:, b], P) if b < 2 else (qbT[:, b - 3], AUG)
                    if b == 3:
                        act.wait_ge(q_evac, t * 5 + 3)
                    act.activation(out.rearrange("p a b -> p (a b)"), pQ[0:rows, b % 2, :], ACT.Copy).then_inc(q_evac, 1)

            act.wait_ge(consts_here, 96)
            act.wait_ge(pool_init, 1 + HEADS)
            head(0, 0)
            tiles(act, tile)
            copy_q(LAST)

        @block.vector
        def _(v):
            ch = Chain(v, dve)

            def norm(t, p, turn):
                v.wait_ge(x_here[p], 32 * (turn + 1))
                layer_norm_stats(ch, x_in[p], stats[:], mv[:])
                v.sem_inc(var_done, 1)
                v.wait_ge(sd_done, t + 1)
                ch.step(v.reciprocal(rs[:], sd[:]))
                ch.wait()
                ch.step(v.tensor_scalar(x_in[p][:], x_in[p][:], mv[:, 0:1], rs[:], ALU.subtract, ALU.mult))
                ch.wait()
                ch.step(v.tensor_tensor(x_in[p][:], x_in[p][:], g_emb[:], ALU.mult))
                ch.wait()
                ch.step(v.tensor_tensor(x_in[p][:], x_in[p][:], b_emb[:], ALU.add))
                ch.wait()
                v.sem_inc(h_done, 1)

            def augment(t):
                v.wait_ge(c_sum_ps, t + 1)
                v.wait_ge(kdup_done, t + 1)
                for g in range(2):
                    ch.step(v.tensor_scalar(k_aug[:, g, HD:HD + HEADS], c_ps, -8.0, None, ALU.mult))
                ch.step(v.tensor_scalar(q_aug[:, :, AUG - 1], c_ps, 8.0, None, ALU.mult))
                ch.step(v.tensor_tensor(lf_sum[:], lf_sum[:], lf_of[t_par[0]], ALU.add))
                ch.wait()
                v.sem_inc(aug_done, 1)

            t_par = [0]
            lf_of = [pn[p][:, FL:FL + HEADS] for p in range(2)]

            def tile(t, p, i):
                if not is_last(t):
                    norm(t + 1, 1 - p, (i if p == 0 else i + 1))
                if not is_first(t):
                    t_par[0] = 1 - p
                    augment(t - 1)
                v.wait_ge(pn_done, PROJ_CHUNKS * (t + 1))
                ch.step(v.tensor_tensor(z[:], pn[p][:, FL:FL + HEADS], bf[:], ALU.add))
                ch.wait()
                ch.step(v.scalar_tensor_tensor(out=az[:], in0=z[:], scalar=-1.0, in1=z[:], op0=ALU.mult, op1=ALU.max))
                ch.wait()
                v.sem_inc(az_done, 1)
                x4 = [pn[p][:, s:s + 9 * HD].rearrange("p (h d) -> p h d", d=HD) for s in (QA, QI)]
                cos = rt[p][:, 0:ROPE].unsqueeze(1).to_broadcast([P, 9, ROPE])
                sin = rt[p][:, ROPE:2 * ROPE].unsqueeze(1).to_broadcast([P, 9, ROPE])
                for s in range(2):
                    ch.step(v.tensor_tensor(rope_a[:, s], x4[s][:, :, 0:ROPE], cos, ALU.mult))
                    ch.step(v.tensor_tensor(rope_b[:, s, :, 0:8], x4[s][:, :, 8:16], sin[:, :, 0:8], ALU.mult))
                    ch.step(v.tensor_tensor(rope_b[:, s, :, 8:16], x4[s][:, :, 0:8], sin[:, :, 8:16], ALU.mult))
                ch.wait()
                for s in range(2):
                    ch.step(v.tensor_tensor(x4[s][:, :, 0:ROPE], rope_a[:, s], rope_b[:, s], ALU.add))
                v.wait_ge(spl_done, t + 1)
                ch.step(v.scalar_tensor_tensor(out=pn[p][:, FL:FL + HEADS], in0=z[:], scalar=0.0, in1=sp_l[:],
                                               op0=ALU.min, op1=ALU.subtract))
                ch.wait()
                v.sem_inc(x_free, 1)
                v.sem_inc(lf_done, 1)
                if not is_first(t):
                    copy_k(t - 1)

            def copy_k(t):
                v.wait_ge(q_ps, t * 5 + 3)
                v.wait_ge(q_evac, t * 5 + 2)
                for k, (high, low) in enumerate(((ka_high, ka_low), (ki_high, ki_low))):
                    ch.step(v.tensor_copy(high[:, ds(t * P, P)], pQ[:, 0, k * P:(k + 1) * P]))
                ch.wait()
                for k, (high, low) in enumerate(((ka_high, ka_low), (ki_high, ki_low))):
                    ch.step(v.tensor_tensor(low[:, ds(t * P, P)], pQ[:, 0, k * P:(k + 1) * P],
                                            high[:, ds(t * P, P)].bitcast(F32), ALU.subtract))
                for g in range(2):
                    ch.step(v.tensor_copy(kbT[0:AUG, g, ds(t * P, P)], pQ[0:AUG, 0, (2 + g) * P:(3 + g) * P]))
                ch.wait()
                v.sem_inc(q_evac, 1)

            v.wait_ge(consts_here, 96)
            v.wait_ge(pool_init, 1 + HEADS)
            norm(0, 0, 0)
            per = 2 * (2 + 1 + 4 + 4 + 1 + 1 + 6 + 2 + 1 + 6)
            tiles(v, tile, ch, per)
            augment_last = LAST
            t_par[0] = 0
            augment(augment_last)
            copy_k(LAST)


BITS = 32


def count_at_least(v, out, x, cand, cnt):
    return v.tensor_scalar(out, x, cand.bitcast(F32), 0.0, ALU.is_ge, ALU.add, accum_out=cnt)


def judge(v, step, cnt, miss):
    if step == 0:
        return v.tensor_scalar(miss, cnt, float(TOPK), -1.0, ALU.is_lt, ALU.mult)
    return v.tensor_scalar(miss, cnt, float(TOPK), float(1 << (BITS - 1 - step)), ALU.is_lt, ALU.mult)


def next_candidate(v, step, miss, cand):
    if step == 0:
        return v.tensor_scalar(cand, miss, 1 << (BITS - 2), None, ALU.bitwise_xor)
    if step == BITS - 1:
        return v.tensor_tensor(cand, miss, cand, ALU.bitwise_xor)
    return v.scalar_tensor_tensor(out=cand, in0=miss, scalar=1 << (BITS - 2 - step), in1=cand, op0=ALU.bitwise_or, op1=ALU.bitwise_xor)


def choose(v, out, x, ties, cand, cnt, low):
    least = cand.bitcast(F32)
    yield v.tensor_scalar(out, x, least, 0.0, ALU.is_gt, ALU.add, accum_out=cnt)
    yield v.tensor_scalar(cnt, cnt, -1.0, float(TOPK), ALU.mult, ALU.add)
    yield v.tensor_scalar(out, x, least, None, ALU.is_equal)
    yield v.tensor_tensor_scan(ties, out, out, 0.0, ALU.add, ALU.max)
    yield v.scalar_tensor_tensor(out=ties, in0=ties, scalar=cnt, in1=out, op0=ALU.is_gt, op1=ALU.mult)
    yield v.scalar_tensor_tensor(out=out, in0=x, scalar=least, in1=ties, op0=ALU.is_lt, op1=ALU.add)
    yield v.tensor_scalar(out, out, low, None, ALU.mult)


SPAN = 1024


class Tally:

    def __init__(self, first=0):
        self.n, self.base, self.outer = first, 0, []

    def at(self, more=0):
        return self.base + (self.n + more)

    def add(self, k=1):
        self.n += k

    def enter(self, turn, per):
        self.outer.append((self.n, self.base))
        self.base = self.base + turn * per

    def leave(self, turns, per):
        mark, self.base = self.outer.pop()
        assert self.n - mark == per, (self.n - mark, per)
        self.n = mark + turns * per


def wait(eng, semaphore, value):
    if not isinstance(value, int) or value > 0:
        wait_alone(eng, semaphore, value)


def spans(width):
    return [(c, min(SPAN, width - c)) for c in range(0, width, SPAN)]


SEGMENTS = [
    (0, 1, 256, (0, 512), False),
    (2, 1, 512, (512, 1024), True),
    (4, 2, 1024, (1024, 1536), True),
    (8, 2, 1536, (1536, 2048), True),
    (12, 2, 2048, (2048, ROWS), True),
    (16, 1, ROWS, (0,), True),
]


def attend(nc, PN, QTA, QTB, MASK, MT, keep):
    ka_high, ka_low, ki_high, ki_low = (keep[k] for k in ("ka_high", "ka_low", "ki_high", "ki_low"))
    kbT, va1, vb1, ident = (keep[k] for k in ("kbT", "va1", "vb1", "ident"))
    with ExitStack() as ctx:
        def sb(name, shape, dt=F32):
            return ctx.enter_context(nc.sbuf_tensor("at_" + name, shape, dt))

        def sem(name):
            return ctx.enter_context(nc.semaphore(name))

        q_raw = sb("q_raw", [P, HEADS, P])
        q_a = sb("q_a", [P, HEADS, P], F32R)
        q_i = sb("q_i", [P, HEADS, P], F32R)
        qbT = sb("queries_b", [AUG, 2, 4, P])
        wi = [sb(f"wi{p}", [P, HEADS]) for p in range(2)]
        mask = sb("mask", [P, ROWS])
        scores = sb("scores", [P, ROWS])
        work = sb("work", [P, ROWS])
        cand = sb("cand", [P, 1], I32)
        miss = sb("miss", [P, 1], I32)
        count = sb("count", [P, 1])
        relu = sb("relu", [P, 2, ROWS // 2])
        ties = relu[:].rearrange("p a b -> p (a b)")
        probs = sb("probs", [P, 2, 4, ROWS])
        nmax = sb("nmax", [P, 2 * HEADS])
        pT = sb("pT_sb", [P, 2, 4 * P])
        rsum = sb("rsum", [HD, 4, P])
        mixT = sb("mixT", [P, 8, P])
        S = [ctx.enter_context(nc.psum_tensor(f"S{b}", [P, SPAN], F32)) for b in range(2)]
        tr = [ctx.enter_context(nc.psum_tensor(f"tr{b}", [P, 4, P], F32)) for b in range(2)]
        pv = [ctx.enter_context(nc.psum_tensor(f"pv{b}", [P, 4, P], F32)) for b in range(2)]

        raw_here = sem("raw_here")
        q_split = sem("q_split")
        qb_here = sem("qb_here")
        wi_here = sem("wi_here")
        mask_here = sem("mask_here")
        s_full = sem("s_full")
        relu_done = sem("relu_done")
        acc_done = sem("acc_done")
        topk_step = sem("topk_step")
        ttr_done = sem("ttr_done")
        exp_done = sem("exp_done")
        tr_full = sem("tr_full")
        tr_copied = sem("tr_copied")
        pv_step = sem("pv_step")
        norm_step = sem("norm_step")
        mix_stored = sem("mix_stored")

        def per_tile(W, Wi, topk):
            nb = W // P
            return dict(full=8 * len(spans(Wi)) + 16 * len(spans(W)), relu=8 * len(spans(Wi)), acc=8 * len(spans(Wi)),
                        topk=(3 * BITS + 8 if topk else 0), ttr=16 * len(spans(W)), exp=16,
                        tr=4 * nb, pvs=4 * nb, norm=12)

        def run(eng, body):
            counts = {k: Tally() for k in per_tile(P, 0, False)}
            for t0, turns, W, Wis, topk in SEGMENTS:
                per = [per_tile(W, Wi, topk) for Wi in Wis]
                total = {k: sum(x[k] for x in per) for k in counts}
                if turns == 1:
                    for j, Wi in enumerate(Wis):
                        body(t0 + j, j, (t0 + j) // 2, W, Wi, topk, counts)
                    continue
                with eng.Fori(0, turns) as i:
                    for k in counts:
                        counts[k].enter(i, total[k])
                    for j, Wi in enumerate(Wis):
                        body(i * 2 + (t0 + j), j, i + t0 // 2, W, Wi, topk, counts)
                for k in counts:
                    counts[k].leave(turns, total[k])
            return counts

        def share(nb, j, parts):
            return range(nb * j // parts, nb * (j + 1) // parts)

        block = ctx.enter_context(nc.Block())

        @block.sync
        def _(sp):
            def load_raw(t, a):
                for half in range(2):
                    for e in range(2):
                        to = q_raw[half * HD:(half + 1) * HD].rearrange("p (c e) n -> p e c n", e=2)[:, e]
                        sp.dma_start(to, QTA[ds(t * P + e * HD, HD), a * 512:(a + 1) * 512].rearrange("p (c n) -> p c n", c=4))\
                            .then_inc(raw_here, 16)

            def load_b(t):
                sp.dma_start(qbT[:].rearrange("p a b c -> p (a b c)"), QTB[ds(t * AUG, AUG), :]).then_inc(qb_here, 16)

            def load_wi(t, p):
                sp.dma_start(wi[p][:], PN[ds(t * P, P), WI:WI + HEADS]).then_inc(wi_here, 16)

            def load_mask(t, W):
                sp.dma_start(mask[:, 0:W], MASK[:, ds(ROWS - t * P, W)]).then_inc(mask_here, 16)

            def store_mix(t):
                sp.dma_start(MT[ds(t * P, P), :], mixT[:].rearrange("p a b -> p (a b)")).then_inc(mix_stored, 16)

            def tile(t, p, i, W, Wi, topk, n):
                last = isinstance(t, int) and t == TILES - 1
                if not last:
                    wait(sp, q_split, t * 4 + 2)
                    load_raw(t + 1, 1)
                    wait(sp, acc_done, n["acc"].at())
                    load_wi(t + 1, 1 - p)
                if not (isinstance(t, int) and t == 0):
                    wait(sp, norm_step, n["norm"].at())
                    store_mix(t - 1)
                if not last:
                    wait(sp, q_split, t * 4 + 4)
                    load_raw(t + 1, 0)
                    wait(sp, s_full, n["full"].at(8 * len(spans(W))))
                    load_b(t + 1)
                    wait(sp, ttr_done, n["ttr"].at((8 if topk else 16) * len(spans(W))))
                    load_mask(t + 1, max(Wi, W))
                for k, v in per_tile(W, Wi, topk).items():
                    n[k].add(v)

            load_raw(0, 0)
            load_b(0)
            load_wi(0, 0)
            load_mask(0, 256)
            n = run(sp, tile)
            wait(sp, norm_step, n["norm"].at())
            store_mix(TILES - 1)
            sp.wait_ge(mix_stored, 16 * TILES)

        @block.gpsimd
        def _(pool):
            def split(q, turn):
                wait(pool, raw_here, turn * 64 + 64)
                pool.tensor_copy(q[:], q_raw[:]).then_inc(q_split, 1)
                wait(pool, q_split, turn * 2 + 1)
                low = slice(HD, P)
                pool.tensor_tensor(q[low], q_raw[low], q[low].bitcast(F32), ALU.subtract).then_inc(q_split, 1)

            def tile(t, p, i, W, Wi, topk, n):
                if not (isinstance(t, int) and t == TILES - 1):
                    wait(pool, s_full, n["full"].at())
                    split(q_i, t * 2 + 1)
                    wait(pool, s_full, n["full"].at(16 * len(spans(W))))
                    split(q_a, t * 2 + 2)
                for k, v in per_tile(W, Wi, topk).items():
                    n[k].add(v)

            split(q_a, 0)
            run(pool, tile)

        @block.tensor
        def _(pe):
            state = dict(kind="ttr", run=0, bank=0, group=0, tb=0)

            def unit(kind, n, matmuls):
                if state["kind"] != kind:
                    state["before"], state["kind"], state["run"] = state["kind"], kind, 0
                sems = {"ttr": ttr_done, "relu": relu_done}
                if state["run"] < 2 and "before" in state:
                    wait(pe, sems[state["before"]], n[state["before"]].at(state["run"] - 1))
                else:
                    wait(pe, sems[kind], n[kind].at(-1))
                out = S[n["full"].n % 2]
                for lo, w, passes in matmuls:
                    for k, (lhsT, rhs) in enumerate(passes):
                        ins = pe.matmul(out[:, lo:lo + w], lhsT, rhs, start=(k == 0), stop=(k == len(passes) - 1))
                ins.then_inc(s_full, 1)
                n["full"].add()
                n[kind].add()
                state["run"] += 1

            def logits_b(g, h, W, n):
                for c, w in spans(W):
                    unit("ttr", n, [(lo, min(512, w - lo), [(qbT[:, g, h, :], kbT[0:AUG, g, c + lo:c + min(w, lo + 512)])])
                                    for lo in range(0, w, 512)])

            def split_products(kind, q, high, low, W, n):
                for c, w in spans(W):
                    unit(kind, n, [(lo, min(512, w - lo), [(q, keys[:, c + lo:c + min(w, lo + 512)]) for keys in (high, low)])
                                   for lo in range(0, w, 512)])

            def weigh(blocks, W, n, values):
                nb = W // P
                grp, bank = state["group"] % 2, state["group"] % 2
                for kb in blocks:
                    if kb == 0:
                        n["exp"].add(4)
                        wait(pe, exp_done, n["exp"].at())
                        wait(pe, norm_step, n["norm"].at(-3))
                    wait(pe, tr_copied, n["tr"].at(-1))
                    for h in range(4):
                        ins = pe.transpose(tr[state["tb"] % 2][:, h, :], probs[:, grp, h, kb * P:(kb + 1) * P], ident[:])
                    ins.then_inc(tr_full, 1)
                    n["tr"].add()
                    state["tb"] += 1
                    for late in ([kb - 1] if kb > 0 else []) + ([kb] if kb == nb - 1 else []):
                        wait(pe, tr_copied, n["tr"].at(late - kb))
                        pe.matmul(pv[bank][:].rearrange("p a b -> p (a b)"), values(late), pT[:, (state["tb"] - 1 + late - kb) % 2, :],
                                  start=(late == 0), stop=(late == nb - 1)).then_inc(pv_step, 1)
                    if kb == nb - 1:
                        n["norm"].add(3)
                        state["group"] += 1

            def tile(t, p, i, W, Wi, topk, n):
                nb = W // P
                wait(pe, qb_here, t * 16 + 16)
                for h in range(4):
                    logits_b(0, h, W, n)
                for h in range(4):
                    logits_b(1, h, W, n)
                    weigh(share(nb, h, 4), W, n, lambda kb: vb1[:, kb, 0, :])
                wait(pe, q_split, t * 4 + 2)
                for g in range(2):
                    for h in range(4):
                        split_products("ttr", q_a[:, 4 * g + h, :], ka_high, ka_low, W, n)
                        weigh(share(nb, h, 4), W, n, (lambda kb: va1[:, kb, :]) if g else (lambda kb: vb1[:, kb, 1, :]))
                if Wi:
                    wait(pe, q_split, t * 4 + 4)
                for h in range(HEADS):
                    split_products("relu", q_i[:, h, :], ki_high, ki_low, Wi, n)
                    weigh(share(nb, h, HEADS), W, n, lambda kb: va1[:, kb, :])
                for k in ("acc", "topk", "pvs"):
                    n[k].add(per_tile(W, Wi, topk)[k])

            run(pe, tile)

        @block.scalar
        def _(act):
            state = dict(group=0, tb=0)

            def softmax(W, n, h):
                k = len(spans(W))
                n["ttr"].add(k)
                n["full"].add(k)
                wait(act, ttr_done, n["ttr"].at())
                slot = 4 * (state["group"] % 4) + h
                row = probs[:, state["group"] % 2, h, 0:W]
                act.activation(row, row, ACT.Exp, bias=nmax[:, slot:slot + 1], scale=-1.0).then_inc(exp_done, 1)
                n["exp"].add()
                if h == 3:
                    state["group"] += 1

            def copies(blocks, n):
                for kb in blocks:
                    n["tr"].add()
                    wait(act, tr_full, n["tr"].at())
                    wait(act, pv_step, n["pvs"].at(-1))
                    b = state["tb"] % 2
                    act.activation(pT[:, b, :], tr[b][:].rearrange("p a b -> p (a b)"), ACT.Copy).then_inc(tr_copied, 1)
                    n["pvs"].add()
                    state["tb"] += 1

            def relus(W, n):
                for c, w in spans(W):
                    b = n["full"].n % 2
                    n["full"].add()
                    wait(act, s_full, n["full"].at())
                    wait(act, acc_done, n["acc"].at(-1))
                    act.activation(relu[:, b, 0:w], S[b][:, 0:w], ACT.Relu, scale=HD ** -0.5 * HEADS ** -0.5).then_inc(relu_done, 1)
                    n["relu"].add()
                    n["acc"].add()

            def tile(t, p, i, W, Wi, topk, n):
                nb = W // P
                for g in range(4):
                    for h in range(4):
                        if g > 0:
                            copies(share(nb, h, 4), n)
                        softmax(W, n, h)
                for h in range(HEADS):
                    relus(Wi, n)
                    copies(share(nb, h, HEADS), n)
                n["norm"].add(12)
                n["topk"].add(per_tile(W, Wi, topk)["topk"])

            run(act, tile)

        @block.vector
        def _(v):
            state = dict(group=0, out=0)

            def logits(W, n, bias, h, read):
                grp = state["group"] % 2
                if h == 0:
                    wait(v, tr_full, n["tr"].at(read))
                slot = 4 * (state["group"] % 4) + h
                for k, (c, w) in enumerate(spans(W)):
                    b = n["full"].n % 2
                    n["full"].add()
                    wait(v, s_full, n["full"].at())
                    if k:
                        wait(v, ttr_done, n["ttr"].at())
                    v.tensor_tensor_reduce(probs[:, grp, h, c:c + w], S[b][:, 0:w], bias[:, c:c + w], -HD ** -0.5,
                                           nmax[:, slot:slot + 1] if k else 3.4e38, ALU.add, ALU.min,
                                           nmax[:, slot:slot + 1]).then_inc(ttr_done, 1)
                    n["ttr"].add()
                if h == 3:
                    state["group"] += 1

            def normalise(first, n, pvs):
                wait(v, pv_step, pvs)
                wait(v, norm_step, n["norm"].at())
                o = pv[state["out"] % 2]
                v.reciprocal(rsum[:], o[HD:P]).then_inc(norm_step, 1)
                n["norm"].add()
                wait(v, norm_step, n["norm"].at())
                for k in range(2):
                    v.tensor_tensor(mixT[k * HD:(k + 1) * HD, first:first + 2, :], o[0:HD, k::2, :], rsum[:, k::2, :],
                                    ALU.mult).then_inc(norm_step, 1)
                    n["norm"].add()
                state["out"] += 1

            def index_scores(p, W, n, h):
                for c, w in spans(W):
                    b = n["full"].n % 2
                    n["full"].add()
                    n["relu"].add()
                    wait(v, relu_done, n["relu"].at())
                    if h:
                        wait(v, acc_done, n["acc"].at(1 - len(spans(W))))
                    v.scalar_tensor_tensor(out=scores[:, c:c + w], in0=relu[:, b, 0:w], scalar=wi[p][:, h:h + 1],
                                           in1=(scores if h else mask)[:, c:c + w], op0=ALU.mult, op1=ALU.add)\
                        .then_inc(acc_done, 1)
                    n["acc"].add()

            def chained(n, ins):
                ins.then_inc(topk_step, 1)
                n["topk"].add()
                wait(v, topk_step, n["topk"].at())

            def search(W, n, step):
                if step == 0:
                    chained(n, v.memset(cand[:], 0))
                chained(n, count_at_least(v, work[:, 0:W], scores[:, 0:W], cand[:], count[:]))
                chained(n, judge(v, step, count[:], miss[:]))
                chained(n, next_candidate(v, step, miss[:], cand[:]))

            def tile(t, p, i, W, Wi, topk, n):
                nb = W // P
                first_tile = isinstance(t, int) and t == 0
                if topk:
                    wait(v, acc_done, n["acc"].at())
                wait(v, mask_here, t * 16 + 16)
                for h in range(HEADS):
                    if topk:
                        for r in range(BITS // HEADS):
                            search(W, n, h * (BITS // HEADS) + r)
                    if h == 2 and not first_tile:
                        normalise(2, n, n["pvs"].at())
                    logits(W, n, mask, h % 4, 0)
                bias = mask
                if topk:
                    s, w = scores[:, 0:W], work[:, 0:W]
                    for ins in choose(v, w, s, ties[:, 0:W], cand[:], count[:], NEG):
                        chained(n, ins)
                    bias = work
                for g in range(2):
                    for h in range(4):
                        if h == 2:
                            if g == 0 and not first_tile:
                                wait(v, mix_stored, t * 16)
                            normalise(4 + 2 * g, n, n["pvs"].at((g + 1) * nb))
                        logits(W, n, bias, h, (g + 1) * nb)
                if Wi:
                    wait(v, mask_here, t * 16 + 32)
                    wait(v, wi_here, t * 16 + 32)
                for h in range(HEADS):
                    if h == 4:
                        normalise(0, n, n["pvs"].at(3 * nb))
                    index_scores(1 - p, Wi, n, h)
                n["pvs"].add(4 * nb)
                n["tr"].add(4 * nb)
                n["exp"].add(16)

            n = run(v, tile)
            normalise(2, n, n["pvs"].at())


GROUPS = 5
GCOLS = -(-ALL // (2 * GROUPS)) * 2
FC = D_FF // P
BLOCKS = -(-GCOLS // P)


def mix_out(nc, MT, HN, W_O, LN_G, LN_B, H1T, keep):
    ident = keep["ident"]
    with ExitStack() as ctx:
        def sb(name, shape, dt=F32):
            return ctx.enter_context(nc.sbuf_tensor(name, shape, dt))

        def sem(name):
            return ctx.enter_context(nc.semaphore(name))

        w_o = sb("w_o", [P, KD, D])
        g1 = sb("g1", [P, D])
        b1 = sb("b1", [P, D])
        mixT = [sb(f"mo_mixT{p}", [P, KD, P]) for p in range(2)]
        hn = [sb(f"mo_h{p}", [P, D]) for p in range(2)]
        z = [sb(f"mo_z{p}", [P, D]) for p in range(2)]
        h1T = [sb(f"mo_h1T{p}", [P, KD, P]) for p in range(2)]
        stats = sb("mo_stats", [P, 12])
        mv = sb("mo_mv", [P, 2])
        sd = sb("mo_sd", [P, 1])
        rs = sb("mo_rs", [P, 1])
        eps = sb("mo_eps", [P, 1])
        po = [ctx.enter_context(nc.psum_tensor(f"mo_po{p}", [P, D], F32)) for p in range(2)]
        pt = [ctx.enter_context(nc.psum_tensor(f"mo_pt{p}", [P, D], F32)) for p in range(2)]

        w_here = sem("mo_w_here")
        in_here = [sem(f"mo_in_here{p}") for p in range(2)]
        eps_set = sem("mo_eps_set")
        o_ps = sem("mo_o_ps")
        z_done = sem("mo_z_done")
        var_done = sem("mo_var_done")
        sd_done = sem("mo_sd_done")
        ln_step = sem("mo_ln_step")
        h1_done = sem("mo_h1_done")
        t_ps = sem("mo_t_ps")
        t_copied = sem("mo_t_copied")
        stored = [sem(f"mo_stored{p}") for p in range(2)]

        LN_STEPS = 5

        def run(eng, body):
            ln = Tally()
            for t in range(3):
                body(t, t % 2, t // 2, ln)
                ln.add(LN_STEPS)
            turns = (TILES - 3) // 2
            with eng.Fori(0, turns) as i:
                ln.enter(i, 2 * LN_STEPS)
                for t in (3, 4):
                    body(2 * i + t, t % 2, i + t // 2, ln)
                    ln.add(LN_STEPS)
                ln.leave(turns, 2 * LN_STEPS)

        block = ctx.enter_context(nc.Block())

        @block.sync
        def _(sp):
            for k in range(KD):
                sp.dma_start(w_o[:, k, :], W_O[k * P:(k + 1) * P, :]).then_inc(w_here, 16)
            sp.dma_start(g1[:], LN_G.unsqueeze(0).to_broadcast([P, D])).then_inc(w_here, 16)
            sp.dma_start(b1[:], LN_B.unsqueeze(0).to_broadcast([P, D])).then_inc(w_here, 16)

            def tile(t, p, i, ln):
                if not (isinstance(t, int) and t < 2):
                    wait_alone(sp, o_ps, t - 1)
                    wait_alone(sp, z_done, 2 * t - 2)
                sp.dma_start(mixT[p][:].rearrange("p a b -> p (a b)"), MT[ds(t * P, P), :]).then_inc(in_here[p], 16)
                sp.dma_start(hn[p][:], HN[ds(t * P, P), :]).then_inc(in_here[p], 16)

            run(sp, tile)

        @block.gpsimd
        def _(pool):
            pool.memset(eps[:], EPS).then_inc(eps_set, 1)

            def tile(t, p, i, ln):
                wait_alone(pool, t_copied, t + 1)
                pool.dma_start(H1T.rearrange("(k p) n -> p k n", p=P)[:, :, ds(t * P, P)], h1T[p][:]).then_inc(stored[p], 16)

            run(pool, tile)
            for p in range(2):
                wait_alone(pool, stored[p], 16 * (TILES // 2 + 1 - p))

        @block.tensor
        def _(pe):
            def turn(t, p):
                wait_alone(pe, h1_done, t + 1)
                if not (isinstance(t, int) and t < 2):
                    wait_alone(pe, t_copied, t - 1)
                for k in range(KD):
                    ins = pe.transpose(pt[p][:, k * P:(k + 1) * P], z[p][:, k * P:(k + 1) * P], ident[:])
                ins.then_inc(t_ps, 1)

            def tile(t, p, i, ln):
                wait_alone(pe, in_here[p], 32 * (i + 1))
                if not (isinstance(t, int) and t < 2):
                    wait_alone(pe, z_done, 2 * t - 2)
                for j in range(2):
                    for k in range(KD):
                        ins = pe.matmul(po[p][:, j * 512:(j + 1) * 512], mixT[p][:, k, :], w_o[:, k, j * 512:(j + 1) * 512],
                                        start=(k == 0), stop=(k == KD - 1))
                ins.then_inc(o_ps, 1)
                if not (isinstance(t, int) and t == 0):
                    turn(t - 1, 1 - p)

            wait_alone(pe, w_here, 16 * (KD + 2))
            run(pe, tile)
            turn(TILES - 1, 0)

        @block.scalar
        def _(act):
            def copy(t, p, i):
                act.wait_ge(t_ps, t + 1)
                if not (isinstance(t, int) and t < 2):
                    act.wait_ge(stored[p], 16 * i)
                act.activation(h1T[p][:].rearrange("p a b -> p (a b)"), pt[p][:], ACT.Copy).then_inc(t_copied, 1)

            def tile(t, p, i, ln):
                act.wait_ge(var_done, t + 1)
                act.activation(sd[:], mv[:, 1:2], ACT.Sqrt, bias=eps[:]).then_inc(sd_done, 1)
                if not (isinstance(t, int) and t == 0):
                    copy(t - 1, 1 - p, i if p else i - 1)

            act.wait_ge(eps_set, 1)
            run(act, tile)
            copy(TILES - 1, 0, TILES // 2)

        @block.vector
        def _(v):
            def tile(t, p, i, ln):
                v.wait_ge(in_here[p], 32 * (i + 1))
                v.wait_ge(o_ps, t + 1)
                if not (isinstance(t, int) and t < 2):
                    v.wait_ge(t_ps, t - 1)
                for j in range(2):
                    c = slice(j * 512, (j + 1) * 512)
                    v.scalar_tensor_tensor(out=z[p][:, c], in0=hn[p][:, c], scalar=ALPHA, in1=po[p][:, c],
                                           op0=ALU.mult, op1=ALU.add).then_inc(z_done, 1)
                v.wait_ge(z_done, 2 * t + 2)
                for j in range(2):
                    v.bn_stats(stats[:, 6 * j:6 * j + 6], z[p][:, j * 512:(j + 1) * 512]).then_inc(ln_step, 1)
                wait_alone(v, ln_step, ln.at(2))
                v.bn_aggr(mv[:], stats[:]).then_inc(var_done, 1)
                v.wait_ge(sd_done, t + 1)
                v.wait_ge(var_done, t + 1)
                v.reciprocal(rs[:], sd[:]).then_inc(ln_step, 1)
                v.wait_ge(ln_step, ln.at(3))
                v.tensor_scalar(z[p][:], z[p][:], mv[:, 0:1], rs[:], ALU.subtract, ALU.mult).then_inc(ln_step, 1)
                v.wait_ge(ln_step, ln.at(4))
                v.tensor_tensor(z[p][:], z[p][:], g1[:], ALU.mult).then_inc(ln_step, 1)
                v.wait_ge(ln_step, ln.at(5))
                v.tensor_tensor(z[p][:], z[p][:], b1[:], ALU.add).then_inc(h1_done, 1)

            v.wait_ge(w_here, 16 * (KD + 2))
            run(v, tile)


def feed_forward(nc, H1T, W_GATE, W_UP, W_DOWN, LN_G, LN_B, Y, keep):
    ident = keep["ident"]
    with ExitStack() as ctx:
        def sb(name, shape, dt=F32):
            return ctx.enter_context(nc.sbuf_tensor("ff_" + name, shape, dt))

        def sem(name):
            return ctx.enter_context(nc.semaphore("ff_" + name))

        zT = sb("zT", [P, KD, GCOLS])
        h_high = sb("h_high", [P, KD, GCOLS], F32R)
        h_low = sb("h_low", [P, KD, GCOLS], F32R)
        silu = sb("silu", [P, 2, GCOLS])
        hid = sb("hid", [P, 2, GCOLS])
        hid_high = sb("hid_high", [P, FC, GCOLS], F32R)
        hid_low = sb("hid_low", [P, FC, GCOLS], F32R)
        w_raw = [sb(f"w_raw{p}", [P, FC * P]) for p in range(2)]
        w_high = [sb(f"w_high{p}", [P, FC * P], F32R) for p in range(2)]
        w_low = [sb(f"w_low{p}", [P, FC * P], F32R) for p in range(2)]
        g2 = sb("g2", [P, D])
        b2 = sb("b2", [P, D])
        y = [sb(f"y{p}", [P, D]) for p in range(2)]
        stats = sb("stats", [P, 12])
        mv = sb("mv", [P, 2])
        sd = sb("sd", [P, 1])
        rs = sb("rs", [P, 1])
        eps = sb("eps", [P, 1])
        ps = [ctx.enter_context(nc.psum_tensor(f"ff_ps{p}", [P, 4, 512], F32)) for p in range(2)]

        consts = sem("consts")
        eps_set = sem("eps_set")
        h_here = sem("h_here")
        h_high_done = sem("h_high_done")
        h_low_done = sem("h_low_done")
        w_here = [sem(f"w_here{p}") for p in range(2)]
        w_high_done = sem("w_high_done")
        w_low_done = sem("w_low_done")
        products = sem("products")
        silu_done = sem("silu_done")
        hid_done = sem("hid_done")
        hid_high_done = sem("hid_high_done")
        hid_low_done = sem("hid_low_done")
        z_done = sem("z_done")
        t_ps = sem("t_ps")
        ln_step = sem("ln_step")
        var_done = sem("var_done")
        sd_done = sem("sd_done")
        y_done = sem("y_done")
        y_free = sem("y_free")
        y_stored = [sem(f"y_stored{p}") for p in range(2)]

        HIDDEN = dict(w=2, hid=2)
        DOWN = dict(w=2, z=2)
        AHEAD = dict(w=2, hid=2, z=2, y=1, t=1)
        BLOCK = dict(t=1, ln=5, var=1, y=1)
        hidden_cols, down_cols = 2 * KD * P, FC * P

        def run(eng, start, hidden, down, rows):
            n = {k: Tally(AHEAD.get(k, 0)) for k in (*HIDDEN, *DOWN, *BLOCK)}
            group = {k: (HIDDEN.get(k, 0) * FC + DOWN.get(k, 0) * KD) // 2 + BLOCK.get(k, 0) * BLOCKS for k in n}

            def pairs(g, part, grows, count, cols, last_cols):
                def pair(at, cols_behind):
                    for p in range(2):
                        if part:
                            part(g, at + p, p, n, cols_behind if p else cols)
                        for k, per in grows.items():
                            n[k].add(per // 2)

                with eng.Fori(0, count // 2 - 1) as i:
                    for k, per in grows.items():
                        n[k].enter(i, per)
                    pair(2 * i, cols)
                    for k, per in grows.items():
                        n[k].leave(count // 2 - 1, per)
                pair(count - 2, last_cols)

            with eng.Fori(0, GROUPS) as g:
                for k in n:
                    n[k].enter(g, group[k])
                start(g, n)
                pairs(g, hidden, HIDDEN, FC, hidden_cols, down_cols)
                pairs(g, down, DOWN, KD, down_cols, 0)
                for r in range(BLOCKS):
                    if rows:
                        rows(g, r, min(P, GCOLS - r * P), n)
                    for k, per in BLOCK.items():
                        n[k].add(per)
                for k in n:
                    n[k].leave(GROUPS, group[k])

        def block_bank(r):
            first = 2 if r < 2 else 0
            return ps[r % 2][:, first:first + 2, :].rearrange("p a b -> p (a b)")

        block = ctx.enter_context(nc.Block())

        @block.sync
        def _(sp):
            sp.dma_start(g2[:], LN_G.unsqueeze(0).to_broadcast([P, D])).then_inc(consts, 16)
            sp.dma_start(b2[:], LN_B.unsqueeze(0).to_broadcast([P, D])).then_inc(consts, 16)

            def start(g, n):
                wait_alone(sp, t_ps, n["t"].at())
                sp.dma_start(zT[:], H1T.rearrange("(k p) n -> p k n", p=P)[:, :, ds(g * GCOLS, GCOLS)]).then_inc(h_here, 16)

            def hidden(g, f, p, n, cols_next):
                wait_alone(sp, w_low_done, n["w"].at(-1))
                for m, src in enumerate((W_GATE, W_UP)):
                    to = w_raw[p][:, m * KD * P:(m + 1) * KD * P].rearrange("p (k n) -> p k n", n=P)
                    sp.dma_start(to, src.rearrange("(k p) n -> p k n", p=P)[:, :, ds(f * P, P)]).then_inc(w_here[p], 16)

            def down(g, d, p, n, cols_next):
                wait_alone(sp, w_low_done, n["w"].at(-1))
                for m in range(2):
                    part = slice(m * FC // 2, (m + 1) * FC // 2)
                    sp.dma_start(w_raw[p][:].rearrange("p (f n) -> p f n", n=P)[:, part],
                                 W_DOWN.rearrange("(f p) n -> p f n", p=P)[:, part, ds(d * P, P)]).then_inc(w_here[p], 16)

            run(sp, start, hidden, down, None)

        @block.gpsimd
        def _(pool):
            pool.memset(eps[:], EPS).then_inc(eps_set, 1)

            def rows(g, r, m, n):
                wait_alone(pool, y_done, n["y"].at(1))
                pool.dma_start(Y[ds(g * GCOLS + r * P, m), :], y[r % 2][0:m, :]).then_inc(y_stored[r % 2], 16)
                if r == BLOCKS - 1:
                    for p in range(2):
                        wait_alone(pool, y_stored[p], (g + 1) * (16 * BLOCKS // 2))
                    pool.sem_inc(y_free, 1)

            pool.sem_inc(y_free, 1)
            run(pool, lambda g, n: None, None, None, rows)

        @block.tensor
        def _(pe):
            def three(out, at, high, low, p, first, last):
                w = slice(at * P, (at + 1) * P)
                pe.matmul(out, w_high[p][:, w], high, start=first, stop=False)
                pe.matmul(out, w_high[p][:, w], low, start=False, stop=False)
                return pe.matmul(out, w_low[p][:, w], high, start=False, stop=last)

            def start(g, n):
                wait_alone(pe, h_low_done, g + 1)
                wait_alone(pe, y_done, n["y"].at())

            def hidden(g, f, p, n, cols_next):
                wait_alone(pe, w_low_done, n["w"].at(1))
                wait_alone(pe, hid_done, n["hid"].at(-1))
                for m in range(2):
                    for k in range(KD):
                        ins = three(ps[p][:, m, 0:GCOLS], m * KD + k, h_high[:, k, :], h_low[:, k, :], p, k == 0, k == KD - 1)
                ins.then_inc(products, 1)

            def down(g, d, p, n, cols_next):
                wait_alone(pe, w_low_done, n["w"].at(1))
                wait_alone(pe, hid_low_done, n["hid"].at())
                wait_alone(pe, z_done, n["z"].at(-1))
                for f in range(FC):
                    ins = three(ps[p][:, 0, 0:GCOLS], f, hid_high[:, f, :], hid_low[:, f, :], p, f == 0, f == FC - 1)
                ins.then_inc(products, 1)

            def rows(g, r, m, n):
                if r == 0:
                    wait_alone(pe, z_done, n["z"].at())
                for k in range(KD):
                    ins = pe.transpose(block_bank(r)[0:m, k * P:(k + 1) * P], zT[:, k, r * P:r * P + m], ident[:])
                ins.then_inc(t_ps, 1)

            pe.sem_inc(products, AHEAD["w"])
            pe.sem_inc(t_ps, AHEAD["t"])
            run(pe, start, hidden, down, rows)

        @block.scalar
        def _(act):
            def split(p, n, more, cols):
                act.wait_ge(w_here[p], (n["w"].at(more - AHEAD["w"]) - p) * 16 + 32)
                act.wait_ge(products, n["w"].at(more - 1))
                act.activation(w_high[p][:, 0:cols], w_raw[p][:, 0:cols], ACT.Copy).then_inc(w_high_done, 1)

            def start(g, n):
                act.wait_ge(h_here, g * 16 + 16)
                act.wait_ge(products, n["w"].at())
                act.activation(h_high[:], zT[:], ACT.Copy).then_inc(h_high_done, 1)
                split(0, n, 0, hidden_cols)

            def hidden(g, f, p, n, cols_next):
                split(1 - p, n, 1, cols_next)
                act.wait_ge(products, n["w"].at(1))
                act.wait_ge(hid_done, n["hid"].at(-1))
                act.activation(silu[:, p], ps[p][:, 0, 0:GCOLS], ACT.Silu).then_inc(silu_done, 1)
                act.wait_ge(hid_done, n["hid"].at(1))
                act.activation(hid_high[:, ds(f, 1), :].squeeze(1), hid[:, p], ACT.Copy).then_inc(hid_high_done, 1)

            def down(g, d, p, n, cols_next):
                if cols_next:
                    split(1 - p, n, 1, cols_next)

            def rows(g, r, m, n):
                act.wait_ge(var_done, n["var"].at(1))
                act.activation(sd[0:m], mv[0:m, 1:2], ACT.Sqrt, bias=eps[0:m]).then_inc(sd_done, 1)

            act.wait_ge(eps_set, 1)
            act.sem_inc(w_high_done, AHEAD["w"])
            act.sem_inc(hid_high_done, AHEAD["hid"])
            act.sem_inc(silu_done, AHEAD["hid"])
            run(act, start, hidden, down, rows)

        @block.vector
        def _(v):
            def split(p, n, more, cols):
                v.wait_ge(w_high_done, n["w"].at(more + 1))
                v.tensor_tensor(w_low[p][:, 0:cols], w_raw[p][:, 0:cols], w_high[p][:, 0:cols].bitcast(F32),
                                ALU.subtract).then_inc(w_low_done, 1)

            def start(g, n):
                v.wait_ge(h_high_done, g + 1)
                v.tensor_tensor(h_low[:], zT[:], h_high[:].bitcast(F32), ALU.subtract).then_inc(h_low_done, 1)
                split(0, n, 0, hidden_cols)

            def hidden(g, f, p, n, cols_next):
                split(1 - p, n, 1, cols_next)
                v.wait_ge(silu_done, n["hid"].at(1))
                v.wait_ge(hid_low_done, n["hid"].at(-1))
                v.tensor_tensor(hid[:, p], silu[:, p], ps[p][:, 1, 0:GCOLS], ALU.mult).then_inc(hid_done, 1)
                v.wait_ge(hid_high_done, n["hid"].at(1))
                v.tensor_tensor(hid_low[:, ds(f, 1), :].squeeze(1), hid[:, p], hid_high[:, ds(f, 1), :].squeeze(1).bitcast(F32),
                                ALU.subtract).then_inc(hid_low_done, 1)

            def down(g, d, p, n, cols_next):
                if cols_next:
                    split(1 - p, n, 1, cols_next)
                v.wait_ge(products, n["w"].at(1))
                v.scalar_tensor_tensor(out=zT[:, ds(d, 1), :].squeeze(1), in0=zT[:, ds(d, 1), :].squeeze(1), scalar=ALPHA,
                                       in1=ps[p][:, 0, 0:GCOLS], op0=ALU.mult, op1=ALU.add).then_inc(z_done, 1)

            def rows(g, r, m, n):
                x = block_bank(r)[0:m]
                out = y[r % 2][0:m, :]
                ln = n["ln"].at
                v.wait_ge(t_ps, n["t"].at(1))
                for j in range(2):
                    v.bn_stats(stats[0:m, 6 * j:6 * j + 6], x[:, j * 512:(j + 1) * 512]).then_inc(ln_step, 1)
                wait_alone(v, ln_step, ln(2))
                v.bn_aggr(mv[0:m], stats[0:m]).then_inc(var_done, 1)
                v.wait_ge(sd_done, n["var"].at(1))
                v.wait_ge(var_done, n["var"].at(1))
                v.reciprocal(rs[0:m], sd[0:m]).then_inc(ln_step, 1)
                v.wait_ge(ln_step, ln(3))
                if r < 2:
                    v.wait_ge(y_free, g + 1)
                else:
                    v.wait_ge(y_stored[r % 2], (g * (BLOCKS // 2) + r // 2) * 16)
                v.tensor_scalar(out, x, mv[0:m, 0:1], rs[0:m], ALU.subtract, ALU.mult).then_inc(ln_step, 1)
                v.wait_ge(ln_step, ln(4))
                v.tensor_tensor(out, out, g2[0:m], ALU.mult).then_inc(ln_step, 1)
                v.wait_ge(ln_step, ln(5))
                v.tensor_tensor(out, out, b2[0:m], ALU.add).then_inc(y_done, 1)

            for semaphore, first in ((w_low_done, "w"), (hid_done, "hid"), (hid_low_done, "hid"), (z_done, "z"), (y_done, "y")):
                v.sem_inc(semaphore, AHEAD[first])
            v.wait_ge(consts, 32)
            run(v, start, hidden, down, rows)


NB = N_SAMPLE
BH = NB * HEADS
RUN = 4
CHUNK = P * RUN
CHUNKS = PAST // CHUNK
UNITS = PAGE // RUN
SROW = TOTAL
FAR = -1.0e30
CHUNK_W = CHUNK + 1
NEW = CHUNKS * CHUNK_W - 1


def decode(nc, PN, PAGE_TABLE, CACHE_A, CACHE_I, CACHE_B, CACHE_LF, CONST, PMOD, EXPAND, SEQS, SC, OS, MT, keep):
    ident, ones = keep["ident"], keep["ones"]
    with ExitStack() as ctx:
        def sb(name, shape, dt=F32):
            return ctx.enter_context(nc.sbuf_tensor("de_" + name, shape, dt))

        def sem(name):
            return ctx.enter_context(nc.semaphore(name))

        after = sb("after", [P, P])
        expand = sb("expand", [P, BH])
        pmod = sb("pmod", [P, 1])
        pages = sb("pages", [P, NB, CHUNKS], I32)
        runs = sb("runs", [P, NB, CHUNKS], I32)
        run_now = [sb(f"run_now{p}", [P, NB], I32) for p in range(2)]
        q_b = sb("q_b", [P, NB * (BH + HEADS)])
        q_a = sb("q_a", [P, NB * (BH + HEADS)])
        q_i = sb("q_i", [P, NB * (P + HEADS)])
        kn_b = sb("kn_b", [P, NB])
        kn_a = sb("kn_a", [HD, NB])
        kn_i = sb("kn_i", [HD, NB])
        w_sel = sb("w_sel", [P, 2, NB])
        scores = sb("d_scores", [NB, CHUNKS * CHUNK_W])
        work = sb("d_work", [P, CHUNKS * CHUNK_W])
        spread = sb("spread", [P, CHUNK_W])
        chosen = sb("chosen", [P, CHUNK_W])
        ties = sb("d_ties", [P, CHUNK_W])
        same = sb("same", [P, P])
        sooner = sb("sooner", [P, P])
        cand = sb("d_cand", [P, 1], I32)
        miss = sb("d_miss", [P, 1], I32)
        count = sb("d_count", [P, 1])
        left = sb("d_left", [P, 1])
        kv = sb("kv", [P, 2, NB, RUN * 256])
        lf = sb("d_lf", [P, 2, NB, RUN * HEADS])
        lf_r = sb("lf_r", [P, RUN, BH])
        lf_later = sb("lf_later", [P, BH])
        kT = sb("kT_d", [P, 2, CHUNK])
        relu = sb("d_relu", [P, CHUNK // 2])
        prob = sb("prob", [BH, CHUNK])
        pT = sb("d_pT", [P, RUN, NB * (BH + HEADS)])
        m_old = sb("m_old", [BH, 1])
        m_new = sb("m_new", [BH, 1])
        neg_m = sb("neg_m", [BH, 1])
        shrink = sb("shrink", [BH, 1])
        den = sb("den", [BH, 1])
        den_c = sb("den_c", [BH, 1])
        rden = sb("rden", [BH, 1])
        o = sb("o_d", [BH, P])

        tr = [ctx.enter_context(nc.psum_tensor(f"d_tr{b}", [P, 512], F32)) for b in range(2)]
        S = [ctx.enter_context(nc.psum_tensor(f"d_S{b}", [P, 512], F32)) for b in range(2)]
        pw = ctx.enter_context(nc.psum_tensor("d_pw", [P, 512], F32))
        pt = ctx.enter_context(nc.psum_tensor("d_pt", [P, 512], F32))
        po = ctx.enter_context(nc.psum_tensor("d_po", [P, 512], F32))

        in_dma = sem("d_in_dma")
        pages_here = sem("d_pages")
        zeroed = sem("d_zeroed")
        prep = sem("d_prep")
        topk_step = sem("d_topk_step")

        def own(q, b_cols):
            return q.rearrange("p (b x) -> p b x", x=BH + HEADS)[:, :, b_cols]

        with nc.Block() as block:
            @block.sync
            def _(sp):
                sp.dma_start(after[:], CONST[3]).then_inc(in_dma, 16)
                sp.dma_start(expand[:], EXPAND).then_inc(in_dma, 16)
                sp.dma_start(pmod[:], PMOD).then_inc(in_dma, 16)
                sp.dma_start(same[:], SEQS[0]).then_inc(in_dma, 16)
                sp.dma_start(sooner[:], SEQS[1]).then_inc(in_dma, 16)
                with nc.allow_non_contiguous_dma(reason="the page table once per partition"):
                    for q in range(P // UNITS):
                        sp.dma_start(pages[q * UNITS:(q + 1) * UNITS].rearrange("p b c -> p (b c)"),
                                     PAGE_TABLE.rearrange("b (c q) -> q (b c)", q=RUN)[q:q + 1, :].to_broadcast([UNITS, NB * CHUNKS]))\
                            .then_inc(pages_here, 16)
                wait_alone(sp, zeroed, 5)
                rows = PN[SROW:SROW + NB, :]
                with nc.allow_non_contiguous_dma(reason="a few thousand elements"):
                    for g in range(2):
                        half = slice(g * HD, (g + 1) * HD)
                        for b in range(NB):
                            row = PN[SROW + b:SROW + b + 1, :]
                            sp.dma_start(own(q_b[half], slice(4 * g, 4 * g + 4))[:, b, :],
                                         row[:, QB + g * 256:QB + (g + 1) * 256].rearrange("o (h d) -> d (o h)", d=HD)).then_inc(in_dma, 16)
                            if g == 0:
                                sp.dma_start(own(q_a[half], slice(0, HEADS))[:, b, :],
                                             row[:, QA:QA + 512].rearrange("o (h d) -> d (o h)", d=HD)).then_inc(in_dma, 16)
                            at = b * (P + HEADS) + g * HD
                            sp.dma_start(q_i[half, at:at + HEADS],
                                         row[:, QI:QI + 512].rearrange("o (h d) -> d (o h)", d=HD)).then_inc(in_dma, 16)
                    sp.dma_start(kn_b[:], rows[:, KB:KB + P].rearrange("b n -> n b")).then_inc(in_dma, 16)
                    sp.dma_start(kn_a[:], rows[:, KA:KA + HD].rearrange("b n -> n b")).then_inc(in_dma, 16)
                    sp.dma_start(kn_i[:], rows[:, KI:KI + HD].rearrange("b n -> n b")).then_inc(in_dma, 16)
                    for b in range(NB):
                        for g in range(2):
                            at = g * BH + b * HEADS
                            sp.dma_start(w_sel[at:at + HEADS, g, b:b + 1],
                                         rows[b:b + 1, WI:WI + HEADS].rearrange("o h -> h o")).then_inc(in_dma, 16)
                        sp.dma_start(lf_later[0:1, b * HEADS:(b + 1) * HEADS], rows[b:b + 1, FL:FL + HEADS]).then_inc(in_dma, 16)
                wait_alone(sp, in_dma, 16 * (5 + 5 * NB + 3 + 3 * NB))

            @block.gpsimd
            def _(pool):
                pool.memset(q_b[:], 0.0).then_inc(zeroed, 1)
                pool.memset(q_a[:], 0.0).then_inc(zeroed, 1)
                pool.memset(q_i[:], 0.0).then_inc(zeroed, 1)
                pool.memset(w_sel[:], 0.0).then_inc(zeroed, 1)
                pool.memset(lf_later[:], 0.0).then_inc(zeroed, 1)
                pool.memset(pT[:], 0.0)
                pool.memset(work[:], 0.0)
                pool.memset(scores[:], NEG)
                pool.memset(lf_r[:], 0.0)

            @block.vector
            def _(v):
                v.wait_ge(pages_here, 16 * (P // UNITS))
                v.wait_ge(in_dma, 16 * (5 + 5 * NB + 3 + 3 * NB))
                v.tensor_scalar(runs[:], pages[:], float(UNITS), pmod[:], ALU.mult, ALU.add).then_inc(prep, 1)
                for q in (q_b, q_a):
                    v.tensor_scalar(q[:], q[:], HD ** -0.5, None, ALU.mult).then_inc(prep, 1)

        def heads_of(q, rows, b, width=BH):
            return q[rows, b * width:b * width + BH]

        def walk(kind):
            width = {"i": HD, "a": 2 * HD, "b": 4 * HD}[kind]
            pool_rows = {"i": CACHE_I, "a": CACHE_A, "b": CACHE_B}[kind]
            vcol, vw = {"i": (0, 0), "a": (HD, HD), "b": (P, P)}[kind]
            q = {"i": q_i, "a": q_a, "b": q_b}[kind]
            knew = {"i": kn_i, "a": kn_a, "b": kn_b}[kind]
            kd = P if kind == "b" else HD
            nblk = RUN // 2 if kind == "i" else RUN
            with ExitStack() as sub:
                def ksem(name):
                    return sub.enter_context(nc.semaphore(f"{kind}_{name}"))

                kv_here = [ksem(f"kv_here{p}") for p in range(2)]
                v0_here = ksem("v0_here")
                idx_done = ksem("idx_done")
                turned = ksem("turned")
                kt_copied = ksem("kt_copied")
                qk = ksem("qk")
                s_full = ksem("s_full")
                s_read = ksem("s_read")
                lf_step = ksem("lf_step")
                w_ps = ksem("w_ps")
                w_read = ksem("w_read")
                mx = ksem("mx")
                shrunk = ksem("shrunk")
                pt_ps = ksem("pt_ps")
                pt_copied = ksem("pt_copied")
                pv_ps = ksem("pv_ps")
                upd = ksem("upd")
                stored = ksem("stored")
                def reach(eng, semaphore, value):
                    wait_alone(eng, semaphore, value + 1)

                PER = dict(seq=NB, chunk=1, mx=4, upd=2, lf=5)

                def run(eng, body):
                    n = {k: Tally() for k in PER}
                    with eng.Fori(0, CHUNKS // 2) as i:
                        for k, per in PER.items():
                            n[k].enter(i, 2 * per)
                        for p in range(2):
                            body(i * -2 + (CHUNKS - 1 - p), p, i, n)
                            for k, per in PER.items():
                                n[k].add(per)
                        for k, per in PER.items():
                            n[k].leave(CHUNKS // 2, 2 * per)
                    return n

                attn = kind != "i"
                block = sub.enter_context(nc.Block())

                @block.sync
                def _(sp):
                    if not attn:
                        return
                    base = {"a": VA, "b": VB}[kind]
                    for b in range(NB):
                        sp.dma_start(o[b * HEADS:(b + 1) * HEADS, 0:vw],
                                     PN[SROW + b:SROW + b + 1, base:base + vw].to_broadcast([HEADS, vw])).then_inc(v0_here, 16)
                    reach(sp, upd, 2 * CHUNKS + 2)
                    out = OS[kind == "b"]
                    sp.dma_start(out[:, 0:vw], o[:, 0:vw]).then_inc(stored, 16)
                    wait_alone(sp, stored, 16)
                    tile0 = (TILES - 1) * P
                    with nc.allow_non_contiguous_dma(reason="a few thousand elements"):
                        for h in range(HEADS):
                            c = h // 2 + (4 if kind == "b" else 0)
                            v0 = (h // 4) * HD if kind == "b" else 0
                            row = tile0 + (h % 2) * HD
                            sp.dma_start(MT[row:row + HD, c * P + N_META:c * P + N_META + NB],
                                         out.rearrange("(b h) n -> h n b", h=HEADS)[h, v0:v0 + HD, :]).then_inc(stored, 16)
                    wait_alone(sp, stored, 16 * (1 + HEADS))

                @block.gpsimd
                def _(pool):
                    def chunk(c, p, i, n):
                        if attn:
                            reach(pool, pv_ps, n["chunk"].at())
                        else:
                            reach(pool, turned, n["seq"].at())
                        pool.tensor_copy(run_now[p][:], runs[:, :, ds(c, 1)].rearrange("p b o -> p (b o)")).then_inc(idx_done, 1)
                        wait_alone(pool, idx_done, n["chunk"].at(1))
                        for b in range(NB):
                            at = bass.IndirectOffsetOnAxis(ap=run_now[p][:, b:b + 1], axis=0)
                            pool.indirect_dma_start(kv[:, p, b, 0:RUN * width], None, pool_rows, at).then_inc(kv_here[p], 16)
                            if kind == "b":
                                pool.indirect_dma_start(lf[:, p, b, :], None, CACHE_LF, at).then_inc(kv_here[p], 16)

                    run(pool, chunk)

                @block.tensor
                def _(pe):
                    pe.sem_inc(turned, NB + 1)
                    for semaphore, first in ((qk, 1), (s_full, 1), (pt_ps, 1), (pv_ps, 2)):
                        pe.sem_inc(semaphore, first)
                    for b in range(NB):
                        ins = pe.matmul(S[1][0:BH, 0:1], heads_of(q, slice(0, kd), b, BH if attn else P), knew[0:kd, b:b + 1], start=(b == 0),
                                        stop=(b == NB - 1 and kind != "a"))
                    ins.then_inc(qk, 1)
                    if kind == "a":
                        pe.matmul(S[1][0:BH, 0:1], expand[:], work[:, NEW:NEW + 1], start=False, stop=True).then_inc(s_full, 1)
                    if kind == "i":
                        reach(pe, s_read, 1)
                        pe.matmul(pw[0:NB, 0:1], w_sel[0:BH, 0], relu[0:BH, 0:1], start=True, stop=True).then_inc(w_ps, 1)

                    def turn_keys(p, b, n):
                        reach(pe, kt_copied, n["seq"].at(b))
                        keys = kv[:, p, b, 0:RUN * width]
                        for r in range(nblk):
                            at = r * max(width, P)
                            ins = pe.transpose(tr[b % 2][:, r * P:(r + 1) * P], keys[:, at:at + P], ident[:])
                        ins.then_inc(turned, 1)

                    def products(p, b, n):
                        reach(pe, kt_copied, n["seq"].at(b + 2))
                        out = S[p][0:BH, :]
                        if attn:
                            ins = pe.matmul(out, heads_of(q, slice(0, P), b), kT[:, b % 2, :], start=(b == 0), stop=False)
                        else:
                            ins = pe.matmul(S[p][:, 0:2 * P], q_i[:, b * P:(b + 1) * P], kT[:, b % 2, 0:2 * P], start=(b == 0),
                                            stop=(b == NB - 1))
                        ins.then_inc(qk, 1)

                    def chunk(c, p, i, n):
                        out = S[p][0:BH, :]
                        wait_alone(pe, kv_here[p], (i + 1) * (16 * NB * (2 if kind == "b" else 1)))
                        turn_keys(p, 0, n)
                        for b in range(NB):
                            if b + 1 < NB:
                                turn_keys(p, b + 1, n)
                            if b == 0:
                                reach(pe, s_read, n["chunk"].at())
                            products(p, b, n)
                        if kind == "b":
                            reach(pe, lf_step, n["lf"].at(5))
                            for r in range(RUN - 1):
                                pe.matmul(out[:, r * P:(r + 1) * P], lf_r[:, r, :], ident[:], start=False, stop=False)
                            pe.matmul(out, lf_r[:, RUN - 1, :], after[:].unsqueeze(1).to_broadcast([P, RUN, P]), start=False, stop=False)
                            pe.matmul(out, lf_later[:], ones[:].unsqueeze(1).to_broadcast([P, RUN, P]), start=False, stop=True).then_inc(s_full, 1)
                        elif kind == "a":
                            pe.matmul(out, expand[:], work[:, ds(c * CHUNK_W, CHUNK)].rearrange("p (n r) -> p r n", r=RUN),
                                      start=False, stop=True).then_inc(s_full, 1)
                        else:
                            reach(pe, s_read, n["chunk"].at(2))
                            wait_alone(pe, w_read, n["chunk"].at(1))
                            for g in range(2):
                                ins = pe.matmul(pw[0:NB, g * 2 * P:(g + 1) * 2 * P], w_sel[:, g], relu[:], start=True, stop=True)
                            ins.then_inc(w_ps, 1)
                        if attn:
                            reach(pe, s_read, n["chunk"].at(2))
                            reach(pe, pt_copied, n["chunk"].at())
                            for r in range(RUN):
                                ins = pe.transpose(pt[:, r * BH:(r + 1) * BH], prob[:, r * P:(r + 1) * P], ident[0:BH, 0:BH])
                            ins.then_inc(pt_ps, 1)
                            reach(pe, pt_copied, n["chunk"].at(1))
                            reach(pe, upd, n["upd"].at())
                            for b in range(NB):
                                for r in range(RUN):
                                    at = r * width + vcol
                                    ins = pe.matmul(po[0:BH, 0:vw], heads_of(pT[:, r, :], slice(0, P), b), kv[:, p, b, at:at + vw],
                                                    start=(b == 0 and r == 0), stop=(b == NB - 1 and r == RUN - 1))
                            ins.then_inc(pv_ps, 1)

                    run(pe, chunk)

                @block.scalar
                def _(act):
                    act.sem_inc(kt_copied, 2)
                    act.sem_inc(pt_copied, 1)
                    if not attn:
                        act.sem_inc(s_read, 1)
                    if kind == "i":
                        reach(act, qk, 1)
                        act.activation(relu[0:BH, 0:1], S[1][0:BH, 0:1], ACT.Relu, scale=HD ** -0.5 * HEADS ** -0.5).then_inc(s_read, 1)

                    def chunk(c, p, i, n):
                        for b in range(NB):
                            reach(act, turned, n["seq"].at(b + 1 + NB))
                            reach(act, qk, n["seq"].at(b))
                            act.activation(kT[:, b % 2, 0:nblk * P], tr[b % 2][:, 0:nblk * P], ACT.Copy).then_inc(kt_copied, 1)
                        if kind == "i":
                            reach(act, qk, n["seq"].at(NB + 1))
                            act.wait_ge(w_ps, n["chunk"].at(1))
                            act.activation(relu[:], S[p][:, 0:2 * P], ACT.Relu, scale=HD ** -0.5 * HEADS ** -0.5).then_inc(s_read, 1)
                            return
                        act.wait_ge(mx, n["mx"].at(3 + 1))
                        reach(act, upd, n["upd"].at())
                        act.activation(shrink[:], m_old[:], ACT.Exp, bias=neg_m[:]).then_inc(shrunk, 1)
                        reach(act, pt_ps, n["chunk"].at())
                        act.activation(prob[:], S[p][0:BH, :], ACT.Exp, bias=neg_m[:], accum_out=den_c[:]).then_inc(s_read, 1)
                        reach(act, pt_ps, n["chunk"].at(1))
                        reach(act, pv_ps, n["chunk"].at(1))
                        act.activation(pT[:].rearrange("p r (b x) -> p r b x", x=BH + HEADS)[:, :, :, 0:HEADS],
                                       pt[:, 0:RUN * BH].rearrange("p (r b h) -> p r b h", r=RUN, b=NB), ACT.Copy).then_inc(pt_copied, 1)

                    run(act, chunk)

                @block.vector
                def _(v):
                    v.sem_inc(lf_step, 1)
                    v.sem_inc(upd, 1)
                    if attn:
                        v.sem_inc(s_read, 1)
                    if kind == "i":
                        v.wait_ge(w_ps, 1)
                        v.tensor_copy(scores[:, NEW:NEW + 1], pw[0:NB, 0:1]).then_inc(w_read, 1)
                    else:
                        v.memset(den[:], 1.0).then_inc(mx, 1)
                        reach(v, s_full if kind == "a" else qk, 1)
                        v.tensor_copy(m_old[:], S[1][0:BH, 0:1]).then_inc(s_read, 1)
                        v.wait_ge(v0_here, 16 * NB)

                    full = {"a": 2, "b": 1, "i": 0}[kind]

                    def chunk(c, p, i, n):
                        if kind == "i":
                            v.wait_ge(w_ps, n["chunk"].at(2))
                            v.tensor_copy(scores[:, ds(c * CHUNK_W, CHUNK)].rearrange("p (n j g) -> p g j n", j=2, g=2),
                                          pw[0:NB, :].rearrange("p (g j n) -> p g j n", g=2, j=2)).then_inc(w_read, 1)
                            return
                        if kind == "b":
                            v.wait_ge(kv_here[p], (i + 1) * (32 * NB))
                            reach(v, s_full, n["chunk"].at())
                            reach(v, lf_step, n["lf"].at())
                            v.tensor_tensor(lf_later[:], lf_later[:], lf_r[:, RUN - 1, :], ALU.add).then_inc(lf_step, 1)
                            mine = lf[:, p].rearrange("p b (r h) -> p r b h", r=RUN)
                            sums = lf_r[:].rearrange("p r (b h) -> p r b h", b=NB)
                            reach(v, lf_step, n["lf"].at(1))
                            v.tensor_copy(sums[:, 2], mine[:, 3]).then_inc(lf_step, 1)
                            for k, (to, frm) in enumerate(((1, 2), (0, 1), (3, 0))):
                                reach(v, lf_step, n["lf"].at(2 + k))
                                v.tensor_tensor(sums[:, to], sums[:, frm], mine[:, frm], ALU.add).then_inc(lf_step, 1)
                        reach(v, s_full, n["chunk"].at(full))
                        v.reduce_max(m_new[:], S[p][0:BH, :], AX.X).then_inc(mx, 1)
                        reach(v, s_read, n["chunk"].at(1))
                        v.wait_ge(mx, n["mx"].at(2))
                        v.tensor_tensor(m_new[:], m_new[:], m_old[:], ALU.max).then_inc(mx, 1)
                        v.wait_ge(mx, n["mx"].at(3))
                        v.tensor_scalar(neg_m[:], m_new[:], -1.0, None, ALU.mult).then_inc(mx, 1)
                        v.wait_ge(shrunk, n["chunk"].at(1))
                        v.tensor_copy(m_old[:], m_new[:]).then_inc(mx, 1)
                        reach(v, s_read, n["chunk"].at(2))
                        reach(v, upd, n["upd"].at())
                        v.wait_ge(mx, n["mx"].at(5))
                        v.scalar_tensor_tensor(out=den[:], in0=den[:], scalar=shrink[:], in1=den_c[:], op0=ALU.mult, op1=ALU.add)\
                            .then_inc(upd, 1)
                        reach(v, pv_ps, n["chunk"].at(2))
                        v.scalar_tensor_tensor(out=o[:, 0:vw], in0=o[:, 0:vw], scalar=shrink[:], in1=po[0:BH, 0:vw],
                                               op0=ALU.mult, op1=ALU.add).then_inc(upd, 1)

                    run(v, chunk)
                    if attn:
                        reach(v, upd, 2 * CHUNKS)
                        v.reciprocal(rden[:], den[:]).then_inc(upd, 1)
                        reach(v, upd, 2 * CHUNKS + 1)
                        v.tensor_scalar(o[:, 0:vw], o[:, 0:vw], rden[:], None, ALU.mult).then_inc(upd, 1)

        walk("i")

        with nc.Block() as block, nc.semaphore("d_moved") as moved, nc.semaphore("d_total_ps") as total_ps:
            total = pw[:, 0:1]

            @block.sync
            def _(sp):
                sp.dma_start(SC, scores[:]).then_inc(moved, 16)
                sp.wait_ge(moved, 16)
                sp.dma_start(spread[:], SC.rearrange("b (c n) -> (b c) n", n=CHUNK_W)).then_inc(moved, 16)
                sp.wait_ge(topk_step, 3 * BITS + 8)
                sp.dma_start(SC.rearrange("b (c n) -> (b c) n", n=CHUNK_W), chosen[:]).then_inc(moved, 16)
                sp.wait_ge(moved, 48)
                sp.dma_start(work[0:NB, :], SC).then_inc(moved, 16)
                sp.wait_ge(moved, 64)

            @block.tensor
            def _(pe):
                def add_up(k, who, counted):
                    pe.wait_ge(topk_step, counted)
                    pe.matmul(total, who[:], count[:], start=True, stop=True).then_inc(total_ps, 1)

                for k in range(BITS):
                    add_up(k, same, 3 * k + 2)
                add_up(BITS, same, 3 * BITS + 2)
                add_up(BITS + 1, sooner, 3 * BITS + 4)

            @block.vector
            def _(v):
                least = cand[:].bitcast(F32)
                v.memset(cand[:], 0).then_inc(topk_step, 1)
                v.wait_ge(moved, 32)
                for k in range(BITS):
                    v.wait_ge(topk_step, 3 * k + 1)
                    count_at_least(v, chosen[:], spread[:], cand[:], count[:]).then_inc(topk_step, 1)
                    v.wait_ge(total_ps, k + 1)
                    judge(v, k, total, miss[:]).then_inc(topk_step, 1)
                    v.wait_ge(topk_step, 3 * k + 3)
                    next_candidate(v, k, miss[:], cand[:]).then_inc(topk_step, 1)
                done = 3 * BITS + 1
                v.wait_ge(topk_step, done)
                v.tensor_scalar(chosen[:], spread[:], least, 0.0, ALU.is_gt, ALU.add, accum_out=count[:]).then_inc(topk_step, 1)
                v.wait_ge(total_ps, BITS + 1)
                v.tensor_scalar(left[:], total, -1.0, float(TOPK), ALU.mult, ALU.add).then_inc(topk_step, 1)
                v.wait_ge(topk_step, done + 2)
                v.tensor_scalar(chosen[:], spread[:], least, 0.0, ALU.is_equal, ALU.add, accum_out=count[:]).then_inc(topk_step, 1)
                v.wait_ge(topk_step, done + 3)
                v.wait_ge(total_ps, BITS + 2)
                v.tensor_tensor_scan(ties[:], chosen[:], chosen[:], total, ALU.add, ALU.max).then_inc(topk_step, 1)
                v.wait_ge(topk_step, done + 4)
                v.scalar_tensor_tensor(out=ties[:], in0=ties[:], scalar=left[:], in1=chosen[:], op0=ALU.is_gt, op1=ALU.mult)\
                    .then_inc(topk_step, 1)
                v.wait_ge(topk_step, done + 5)
                v.scalar_tensor_tensor(out=chosen[:], in0=spread[:], scalar=least, in1=ties[:], op0=ALU.is_lt, op1=ALU.add)\
                    .then_inc(topk_step, 1)
                v.wait_ge(topk_step, done + 6)
                v.tensor_scalar(chosen[:], chosen[:], FAR, None, ALU.mult).then_inc(topk_step, 1)

        walk("a")
        walk("b")


def build_program(nc, a, o):
    def scratch(name, shape):
        return nc.dram_tensor(f"dram_{name}", shape, F32, kind="Internal").ap()

    QTA = scratch("QTA", [ROWS, 8 * P])
    QTB = scratch("QTB", [TILES * AUG, 8 * P])
    HN = scratch("HN", [ROWS, D])
    MT = scratch("MT", [ROWS, D])
    H1T = scratch("H1T", [D, ROWS])
    OS = [scratch(f"OS{k}", [BH, P]) for k in range(2)]
    SC = scratch("SC", [NB, CHUNKS * CHUNK_W])
    PN, Y = o["PN"], o["Y"]
    with ExitStack() as consts:
        ident = consts.enter_context(nc.sbuf_tensor("ident", [P, P], F32))
        ones = consts.enter_context(nc.sbuf_tensor("ones", [P, P], F32))
        with ExitStack() as prompt:
            def sb(name, shape):
                return prompt.enter_context(nc.sbuf_tensor(name, shape, F32))

            split = {n: prompt.enter_context(nc.sbuf_tensor(n, [P, ROWS], F32R)) for n in ("ka_high", "ka_low", "ki_high", "ki_low")}
            keep = dict(split, ident=ident, ones=ones, tri=sb("tri", [P, P]),
                        kbT=sb("kbT", [P, 2, ROWS]), va1=sb("va1", [P, TILES, P]), vb1=sb("vb1", [P, TILES, 2, P]))
            project(nc, a["x_rows"], a["rope"], a["w_in"], a["ln_emb_g"], a["ln_emb_b"], a["b_forget"], a["matrices"],
                    PN, QTA, QTB, HN, keep)
            attend(nc, PN, QTA, QTB, a["mask"], MT, keep)
        keep = dict(ident=ident, ones=ones)
        decode(nc, PN, a["page_table"], a["cache_a"], a["cache_i"], a["cache_b"], a["cache_lf"], a["matrices"], a["pmod"],
               a["expand"], a["sequences"], SC, OS, MT, keep)
        mix_out(nc, MT, HN, a["w_o"], a["ln1_g"], a["ln1_b"], H1T, keep)
        feed_forward(nc, H1T, a["w_gate"], a["w_up"], a["w_down"], a["ln2_g"], a["ln2_b"], Y, keep)


def shape_constants():
    pos = np.zeros(ROWS, np.float32)
    pos[:TOTAL] = np.arange(TOTAL)
    pos[TOTAL:ALL] = PAST
    half = ROPE // 2
    inv = (np.float32(500000.0) ** (-np.arange(half, dtype=np.float32) / np.float32(half))).astype(np.float32)
    angle = (pos[:, None] * inv).astype(np.float32).astype(np.float64)
    cos, sin = np.cos(angle).astype(np.float32), np.sin(angle).astype(np.float32)
    square = np.ones((P, P), np.float32)
    expand = np.zeros((P, BH), np.float32)
    for b in range(NB):
        expand[b, b * HEADS:(b + 1) * HEADS] = 1.0
    seq, chunk = np.arange(P) // CHUNKS, np.arange(P) % CHUNKS
    same = seq[:, None] == seq[None, :]
    behind = np.arange(2 * ROWS)[None, :] - ROWS > np.arange(P)[:, None]
    return dict(
        rope=np.concatenate([cos, cos, -sin, sin], 1),
        matrices=np.stack([np.eye(P, dtype=np.float32), np.triu(square), square, np.tril(square, -1)]),
        mask=np.where(behind, np.float32(NEG), np.float32(0.0)).astype(np.float32),
        pmod=(np.arange(P) % UNITS).astype(np.float32)[:, None].copy(),
        expand=expand,
        sequences=np.stack([same, same & (chunk[:, None] < chunk[None, :])]).astype(np.float32),
    )


def kernel(x_prompt, x_sample, cache_a_kv, cache_idx_k, cache_b_kv, cache_b_logf, page_table, meta, ln_emb_g, ln_emb_b,
           w_in, b_forget, w_o, ln1_g, ln1_b, w_gate, w_up, w_down, ln2_g, ln2_b):
    import concourse.bacc as bacc
    from concourse.bass_utils import run_bass_kernel_spmd

    def arr(x):
        return np.ascontiguousarray(x)

    pad = np.zeros((ROWS - ALL, D), np.float32)
    arrays = dict(
        x_rows=np.concatenate([arr(meta), arr(x_prompt)[0], arr(x_sample)[:, 0], pad], 0),
        cache_a=arr(cache_a_kv).reshape(-1, RUN * 2 * HD), cache_i=arr(cache_idx_k).reshape(-1, RUN * HD),
        cache_b=arr(cache_b_kv).reshape(-1, RUN * 4 * HD), cache_lf=arr(cache_b_logf).reshape(-1, RUN * HEADS),
        page_table=arr(page_table), ln_emb_g=arr(ln_emb_g), ln_emb_b=arr(ln_emb_b), w_in=arr(w_in)[0], b_forget=arr(b_forget),
        w_o=arr(w_o)[0], ln1_g=arr(ln1_g)[0], ln1_b=arr(ln1_b)[0], w_gate=arr(w_gate)[0], w_up=arr(w_up)[0],
        w_down=arr(w_down)[0], ln2_g=arr(ln2_g)[0], ln2_b=arr(ln2_b)[0], **shape_constants())

    nc = bacc.Bacc("TRN2", target_bir_lowering=False, num_devices=1)
    arrays = {f"in_{n}": x for n, x in arrays.items()}
    ins = {n[3:]: nc.dram_tensor(n, x.shape, mybir.dt.from_np(x.dtype), kind="ExternalInput").ap() for n, x in arrays.items()}
    outs = {n: nc.dram_tensor(f"out_{n}", shape, F32, kind="ExternalOutput").ap() for n, shape in (("PN", (ROWS, N_IN)), ("Y", (ROWS, D)))}
    build_program(nc, ins, outs)
    got = run_bass_kernel_spmd(nc, [arrays], core_ids=[0]).results[0]
    pn, y = got["out_PN"], got["out_Y"]

    def rows(first, last, c0, c1, *shape):
        return np.ascontiguousarray(pn[first:last, c0:c1]).reshape(shape)

    n = N_SAMPLE
    return (y[N_META:TOTAL][None], y[TOTAL:ALL][:, None],
            rows(0, TOTAL, KA, KA + 2 * HD, 1, 1, TOTAL, 2, 1, HD), rows(0, TOTAL, KI, KI + HD, 1, 1, TOTAL, HD),
            rows(0, TOTAL, KB, KB + 4 * HD, 1, 1, TOTAL, 2, 2, HD), rows(0, TOTAL, FL, FL + HEADS, 1, 1, TOTAL, HEADS),
            rows(TOTAL, ALL, KA, KA + 2 * HD, 1, n, 1, 2, 1, HD), rows(TOTAL, ALL, KI, KI + HD, 1, n, 1, HD),
            rows(TOTAL, ALL, KB, KB + 4 * HD, 1, n, 1, 2, 2, HD), rows(TOTAL, ALL, FL, FL + HEADS, 1, n, 1, HEADS))
```

```python
from contextlib import ExitStack

import numpy as np

import concourse.bass as bass
from concourse import mybir

F32 = mybir.dt.float32
F32R = mybir.dt.float32r
I32 = mybir.dt.int32
ALU = mybir.AluOpType
ACT = mybir.ActivationFunctionType
AX = mybir.AxisListType
ds = bass.ds

P = 128
D = 1024
KD = D // P
N_META, SEQ, N_SAMPLE = 16, 2048, 8
TOTAL = N_META + SEQ
ALL = TOTAL + N_SAMPLE
TILES = -(-ALL // P)
ROWS = TILES * P
HD = 64
HEADS = 8
PAST, PAGE = 8192, 128
PAGES = PAST // PAGE
TOPK = 256
ROPE = 16
D_FF = 2816
EPS = 1e-5
ALPHA = 2.0 ** 0.25
QA, KA, VA, QI, KI, WI, QB, KB, VB, FL = 0, 512, 576, 640, 1152, 1216, 1224, 1736, 1864, 1992
N_IN = 2000
PROJ_CHUNKS = 4
PROJ_W = N_IN // PROJ_CHUNKS
AUG = HD + HEADS + 1
NEG = float(np.float32(-3.0e38))


def wait_alone(eng, semaphore, value):
    eng.wait_ge(semaphore, value)
    if not isinstance(value, int):
        eng.nop(nofuse=True)


class Chain:

    def __init__(self, eng, sem):
        self.eng, self.sem, self.n, self.base = eng, sem, 0, 0

    def step(self, ins):
        ins.then_inc(self.sem, 1)
        self.n += 1

    def wait(self):
        self.eng.wait_ge(self.sem, self.base + self.n)

    def wait_alone(self):
        wait_alone(self.eng, self.sem, self.base + self.n)

    def start_loop(self, i, first, per):
        self.outer = self.n
        self.base = (i - first) * per
        self.n0 = self.n

    def end_loop(self, turns, per):
        assert self.n - self.n0 == per, (self.n - self.n0, per)
        self.base = 0
        self.n = self.n0 + turns * per


def layer_norm_stats(chain, x, stats, mv):
    v = chain.eng
    for c in range(D // 512):
        chain.step(v.bn_stats(stats[:, 6 * c:6 * c + 6], x[:, 512 * c:512 * c + 512]))
    chain.wait_alone()
    chain.step(v.bn_aggr(mv, stats))
    chain.wait()


def project(nc, X, RT, W_IN, LN_G, LN_B, BF, CONST, PN, QTA, QTB, HN, keep):
    ka_high, ka_low, ki_high, ki_low = (keep[k] for k in ("ka_high", "ka_low", "ki_high", "ki_low"))
    kbT, va, vb, ident, tri, ones = (keep[k] for k in ("kbT", "va", "vb", "ident", "tri", "ones"))
    with ExitStack() as ctx:
        def sb(name, shape, dt=F32):
            return ctx.enter_context(nc.sbuf_tensor(name, shape, dt))

        def sem(name):
            return ctx.enter_context(nc.semaphore(name))

        w_in = sb("w_in", [P, KD, N_IN])
        g_emb = sb("g_emb", [P, D])
        b_emb = sb("b_emb", [P, D])
        bf = sb("bf", [P, HEADS])
        x_in = [sb(f"x_in{p}", [P, D]) for p in range(2)]
        rt = [sb(f"rt{p}", [P, 2 * ROPE]) for p in range(2)]
        hT = [sb(f"hT{p}", [P, KD, P]) for p in range(2)]
        pn = [sb(f"pn{p}", [P, N_IN]) for p in range(2)]
        rope_a = sb("rope_a", [P, 2, 9, ROPE])
        rope_b = sb("rope_b", [P, 2, 9, ROPE])
        kdup = sb("kdup", [P, 2, 2, HD])
        q_aug = sb("q_aug", [P, HEADS, AUG])
        k_aug = sb("k_aug", [P, 2, AUG])
        qaiT = sb("qaiT", [P, 2, 4, P])
        qbT = sb("qbT", [AUG, 2, 4, P])
        lf_sum = sb("lf_sum", [P, HEADS])
        stats = sb("stats", [P, 12])
        mv = sb("mv", [P, 2])
        sd = sb("sd", [P, 1])
        rs = sb("rs", [P, 1])
        eps = sb("eps", [P, 1])
        z = sb("z", [P, HEADS])
        az = sb("az", [P, HEADS])
        sp_e = sb("sp_e", [P, HEADS])
        sp_l = sb("sp_l", [P, HEADS])
        pT = ctx.enter_context(nc.psum_tensor("pT", [P, 2, 512], F32))
        pP = ctx.enter_context(nc.psum_tensor("pP", [P, 4, 512], F32))
        pQ = ctx.enter_context(nc.psum_tensor("pQ", [P, 2, 512], F32))
        c_ps = pT[:, 0, 0:HEADS]

        w_here = sem("w_here")
        consts_here = sem("consts_here")
        x_here = [sem(f"x_here{p}") for p in range(2)]
        x_free = sem("x_free")
        var_done = sem("var_done")
        sd_done = sem("sd_done")
        h_done = sem("h_done")
        hT_ps = sem("hT_ps")
        hT_done = sem("hT_done")
        proj_ps = sem("proj_ps")
        pn_done = sem("pn_done")
        az_done = sem("az_done")
        spl_done = sem("spl_done")
        act_own = sem("act_own")
        lf_done = sem("lf_done")
        lf_sum_done = sem("lf_sum_done")
        c_sum_ps = sem("c_sum_ps")
        aug_done = sem("aug_done")
        q_ps = sem("q_ps")
        q_evac = sem("q_evac")
        pn_stored = [sem(f"pn_stored{p}") for p in range(2)]
        h_stored = [sem(f"h_stored{p}") for p in range(2)]
        q_stored = sem("q_stored")
        kdup_done = sem("kdup_done")
        pool_init = sem("pool_init")
        dve = sem("dve1")

        LAST = TILES - 1

        def tiles(eng, body, chain=None, per=0):
            body(0, 0, 0)
            body(1, 1, 0)
            with eng.Fori(1, TILES // 2) as i:
                if chain:
                    chain.start_loop(i, 1, per)
                body(2 * i, 0, i)
                body(2 * i + 1, 1, i)
                if chain:
                    chain.end_loop(TILES // 2 - 1, per)
            body(LAST, 0, TILES // 2)

        def is_first(t):
            return isinstance(t, int) and t == 0

        def is_last(t):
            return isinstance(t, int) and t == LAST

        block = ctx.enter_context(nc.Block())

        @block.sync
        def _(sp):
            sp.dma_start(g_emb[:], LN_G.unsqueeze(0).to_broadcast([P, D])).then_inc(consts_here, 16)
            sp.dma_start(b_emb[:], LN_B.unsqueeze(0).to_broadcast([P, D])).then_inc(consts_here, 16)
            sp.dma_start(bf[:], BF.to_broadcast([P, HEADS])).then_inc(consts_here, 16)
            sp.dma_start(ident[:], CONST[0]).then_inc(consts_here, 16)
            sp.dma_start(tri[:], CONST[1]).then_inc(consts_here, 16)
            sp.dma_start(ones[:], CONST[2]).then_inc(consts_here, 16)

            def load(t, p, i):
                if not (isinstance(t, int) and t < 2):
                    wait_alone(sp, x_free, t - 1)
                    wait_alone(sp, h_stored[p], 16 * i)
                sp.dma_start(x_in[p][:], X[ds(t * P, P), :]).then_inc(x_here[p], 16)
                sp.dma_start(rt[p][:], RT[ds(t * P, P), :]).then_inc(x_here[p], 16)
                if is_first(t):
                    for k in range(KD):
                        sp.dma_start(w_in[:, k, :], W_IN[k * P:(k + 1) * P, :]).then_inc(w_here, 16)

            tiles(sp, load)

        @block.gpsimd
        def _(pool):
            pool.memset(eps[:], EPS)
            pool.memset(lf_sum[:], 0.0)
            pool.memset(k_aug[:, :, AUG - 1:AUG], 1.0)
            pool.memset(q_aug[:, :, HD:AUG], 0.0).then_inc(pool_init, 1)
            pool.wait_ge(pool_init, 1)
            for h in range(HEADS):
                pool.memset(q_aug[:, h, HD + h:HD + h + 1], 1.0).then_inc(pool_init, 1)

            def stage(t, p, i):
                wait_alone(pool, h_done, t + 1)
                pool.dma_start(HN[ds(t * P, P), :], x_in[p][:]).then_inc(h_stored[p], 16)
                wait_alone(pool, lf_done, t + 1)
                pool.dma_start(PN[ds(t * P, P), :], pn[p][:]).then_inc(pn_stored[p], 16)
                if not is_first(t):
                    wait_alone(pool, q_ps, t * 5)
                for c in range(2):
                    pool.tensor_copy(kdup[:, 0, c, :], pn[p][:, KA:KA + HD])
                    pool.tensor_copy(kdup[:, 1, c, :], pn[p][:, KI:KI + HD])
                pool.tensor_copy(va[:, ds(t, 1), 0:HD].squeeze(1), pn[p][:, VA:VA + HD])
                for g in range(2):
                    pool.tensor_copy(vb[:, ds(t, 1), g, 0:HD].squeeze(1), pn[p][:, VB + g * HD:VB + (g + 1) * HD])
                pool.tensor_copy(q_aug[:, :, 0:HD], pn[p][:, QB:QB + 512].rearrange("p (h d) -> p h d", d=HD))
                pool.tensor_copy(k_aug[:, :, 0:HD],
                                 pn[p][:, KB:KB + 128].rearrange("p (h d) -> p h d", d=HD)).then_inc(kdup_done, 1)
                if not is_first(t):
                    store_q(t - 1)

            def store_q(t):
                wait_alone(pool, q_evac, 5 * (t + 1))
                pool.dma_start(QTA[ds(t * P, P), :], qaiT[:].rearrange("p a b c -> p (a b c)")).then_inc(q_stored, 16)
                pool.dma_start(QTB[ds(t * AUG, AUG), :], qbT[:].rearrange("p a b c -> p (a b c)")).then_inc(q_stored, 16)

            tiles(pool, stage)
            store_q(LAST)
            pool.wait_ge(q_stored, 32 * TILES)
            for p in range(2):
                pool.wait_ge(h_stored[p], 16 * (TILES // 2 + 1 - p))
                pool.wait_ge(pn_stored[p], 16 * (TILES // 2 + 1 - p))

        @block.tensor
        def _(pe):
            def turn_h(t, p):
                pe.wait_ge(h_done, t + 1)
                if not is_first(t):
                    pe.wait_ge(hT_done, t)
                if not (isinstance(t, int) and t < 2):
                    pe.wait_ge(aug_done, t - 1)
                for k in range(KD):
                    ins = pe.transpose(pT[:, k // 4, (k % 4) * P:(k % 4 + 1) * P], x_in[p][:, k * P:(k + 1) * P], ident[:])
                ins.then_inc(hT_ps, 1)

            def turn_q(t, p):
                pe.wait_ge(kdup_done, t + 1)
                pe.wait_ge(aug_done, t + 1)
                for b in range(5):
                    if is_first(t) and b < 2:
                        pass
                    else:
                        pe.wait_ge(q_evac, t * 5 + max(b - 1, 0))
                    out = pQ[:, b % 2, :].rearrange("p (c n) -> p c n", c=4)
                    for c in range(4):
                        if b == 0:
                            ins = pe.transpose(out[:, c, :], pn[p][:, QA + c * P:QA + (c + 1) * P], ident[:])
                        elif b == 1:
                            ins = pe.transpose(out[:, c, :], pn[p][:, QI + c * P:QI + (c + 1) * P], ident[:])
                        elif b == 2 and c < 2:
                            ins = pe.transpose(out[:, c, :], kdup[:, c, :, :].rearrange("p a b -> p (a b)"), ident[:])
                        elif b == 2:
                            ins = pe.transpose(out[0:AUG, c, :], k_aug[:, c - 2, :], ident[:])
                        else:
                            ins = pe.transpose(out[0:AUG, c, :], q_aug[:, (b - 3) * 4 + c, :], ident[:])
                    ins.then_inc(q_ps, 1)

            def forget_sum(t, p):
                pe.wait_ge(lf_done, t + 1)
                pe.wait_ge(hT_done, TILES if is_last(t) else t + 2)
                pe.matmul(c_ps, tri[:], pn[p][:, FL:FL + HEADS], start=True, stop=False)
                pe.matmul(c_ps, ones[:], lf_sum[:], start=False, stop=True).then_inc(c_sum_ps, 1)

            def tile(t, p, i):
                pe.wait_ge(hT_done, t + 1)
                for j in range(PROJ_CHUNKS):
                    if not is_first(t):
                        pe.wait_ge(pn_done, (t - 1) * PROJ_CHUNKS + j + 1)
                    for k in range(KD):
                        if is_first(t) and j == 0:
                            pe.wait_ge(w_here, 16 * KD)
                        ins = pe.matmul(pP[:, j, 0:PROJ_W], hT[p][:, k, :], w_in[:, k, j * PROJ_W:(j + 1) * PROJ_W],
                                        start=(k == 0), stop=(k == KD - 1))
                    ins.then_inc(proj_ps, 1)
                    if j == 1 and not is_first(t):
                        forget_sum(t - 1, 1 - p)
                    if j == 2 and not is_first(t):
                        turn_q(t - 1, 1 - p)
                if not is_last(t):
                    turn_h(t + 1, 1 - p)

            pe.wait_ge(consts_here, 96)
            pe.wait_ge(pool_init, 1 + HEADS)
            turn_h(0, 0)
            tiles(pe, tile)
            forget_sum(LAST, 0)
            turn_q(LAST, 0)

        @block.scalar
        def _(act):
            def tile(t, p, i):
                if not is_last(t):
                    root(t + 1)
                if not (isinstance(t, int) and t < 2):
                    act.wait_ge(pn_stored[p], 16 * i)
                    act.wait_ge(q_ps, 5 * (t - 1))
                    act.wait_ge(kdup_done, t - 1)
                for j in range(PROJ_CHUNKS):
                    act.wait_ge(proj_ps, t * PROJ_CHUNKS + j + 1)
                    act.activation(pn[p][:, j * PROJ_W:(j + 1) * PROJ_W], pP[:, j, 0:PROJ_W], ACT.Copy).then_inc(pn_done, 1)
                    if j == 2 and not is_first(t):
                        copy_q(t - 1)
                if not is_last(t):
                    copy_h(t + 1, 1 - p)
                act.wait_ge(az_done, t + 1)
                act.activation(sp_e[:], az[:], ACT.Exp, scale=-1.0).then_inc(act_own, 1)
                act.wait_ge(act_own, t + 1)
                act.activation(sp_l[:], sp_e[:], ACT.Ln, bias=ones[:, 0:1]).then_inc(spl_done, 1)

            def root(t):
                act.wait_ge(var_done, t + 1)
                act.activation(sd[:], mv[:, 1:2], ACT.Sqrt, bias=eps[:]).then_inc(sd_done, 1)

            def copy_h(t, p):
                act.wait_ge(hT_ps, t + 1)
                if not (isinstance(t, int) and t < 2):
                    act.wait_ge(proj_ps, (t - 1) * PROJ_CHUNKS)
                act.activation(hT[p][:].rearrange("p a b -> p (a b)"), pT[:].rearrange("p a b -> p (a b)"),
                               ACT.Copy).then_inc(hT_done, 1)

            def copy_q(t):
                if not is_first(t):
                    act.wait_ge(q_stored, 32 * t)
                for b in (0, 1, 3, 4):
                    act.wait_ge(q_ps, t * 5 + b + 1)
                    out, rows = (qaiT[:, b], P) if b < 2 else (qbT[:, b - 3], AUG)
                    if b == 3:
                        act.wait_ge(q_evac, t * 5 + 3)
                    act.activation(out.rearrange("p a b -> p (a b)"), pQ[0:rows, b % 2, :], ACT.Copy).then_inc(q_evac, 1)

            act.wait_ge(consts_here, 96)
            act.wait_ge(pool_init, 1 + HEADS)
            root(0)
            copy_h(0, 0)
            tiles(act, tile)
            copy_q(LAST)

        @block.vector
        def _(v):
            ch = Chain(v, dve)

            def norm(t, p, turn):
                v.wait_ge(x_here[p], 32 * (turn + 1))
                layer_norm_stats(ch, x_in[p], stats[:], mv[:])
                v.sem_inc(var_done, 1)
                v.wait_ge(sd_done, t + 1)
                ch.step(v.reciprocal(rs[:], sd[:]))
                ch.wait()
                ch.step(v.tensor_scalar(x_in[p][:], x_in[p][:], mv[:, 0:1], rs[:], ALU.subtract, ALU.mult))
                ch.wait()
                ch.step(v.tensor_tensor(x_in[p][:], x_in[p][:], g_emb[:], ALU.mult))
                ch.wait()
                ch.step(v.tensor_tensor(x_in[p][:], x_in[p][:], b_emb[:], ALU.add))
                ch.wait()
                v.sem_inc(h_done, 1)

            def augment(t):
                v.wait_ge(c_sum_ps, t + 1)
                v.wait_ge(kdup_done, t + 1)
                for g in range(2):
                    ch.step(v.tensor_scalar(k_aug[:, g, HD:HD + HEADS], c_ps, -8.0, None, ALU.mult))
                ch.step(v.tensor_scalar(q_aug[:, :, AUG - 1], c_ps, 8.0, None, ALU.mult))
                ch.step(v.tensor_tensor(lf_sum[:], lf_sum[:], lf_of[t_par[0]], ALU.add))
                ch.wait()
                v.sem_inc(aug_done, 1)

            t_par = [0]
            lf_of = [pn[p][:, FL:FL + HEADS] for p in range(2)]

            def tile(t, p, i):
                if not is_last(t):
                    norm(t + 1, 1 - p, (i if p == 0 else i + 1))
                if not is_first(t):
                    t_par[0] = 1 - p
                    augment(t - 1)
                    copy_k(t - 1)
                v.wait_ge(pn_done, PROJ_CHUNKS * (t + 1))
                ch.step(v.tensor_tensor(z[:], pn[p][:, FL:FL + HEADS], bf[:], ALU.add))
                ch.wait()
                ch.step(v.scalar_tensor_tensor(out=az[:], in0=z[:], scalar=-1.0, in1=z[:], op0=ALU.mult, op1=ALU.max))
                ch.wait()
                v.sem_inc(az_done, 1)
                x4 = [pn[p][:, s:s + 9 * HD].rearrange("p (h d) -> p h d", d=HD) for s in (QA, QI)]
                cos = rt[p][:, 0:ROPE].unsqueeze(1).to_broadcast([P, 9, ROPE])
                sin = rt[p][:, ROPE:2 * ROPE].unsqueeze(1).to_broadcast([P, 9, ROPE])
                for s in range(2):
                    ch.step(v.tensor_tensor(rope_a[:, s], x4[s][:, :, 0:ROPE], cos, ALU.mult))
                    ch.step(v.tensor_tensor(rope_b[:, s, :, 0:8], x4[s][:, :, 8:16], sin[:, :, 0:8], ALU.mult))
                    ch.step(v.tensor_tensor(rope_b[:, s, :, 8:16], x4[s][:, :, 0:8], sin[:, :, 8:16], ALU.mult))
                ch.wait()
                for s in range(2):
                    ch.step(v.tensor_tensor(x4[s][:, :, 0:ROPE], rope_a[:, s], rope_b[:, s], ALU.add))
                v.wait_ge(spl_done, t + 1)
                ch.step(v.scalar_tensor_tensor(out=pn[p][:, FL:FL + HEADS], in0=z[:], scalar=0.0, in1=sp_l[:],
                                               op0=ALU.min, op1=ALU.subtract))
                ch.wait()
                v.sem_inc(x_free, 1)
                v.sem_inc(lf_done, 1)

            def copy_k(t):
                v.wait_ge(q_ps, t * 5 + 3)
                v.wait_ge(q_evac, t * 5 + 2)
                for k, (high, low) in enumerate(((ka_high, ka_low), (ki_high, ki_low))):
                    ch.step(v.tensor_copy(high[:, ds(t * P, P)], pQ[:, 0, k * P:(k + 1) * P]))
                ch.wait()
                for k, (high, low) in enumerate(((ka_high, ka_low), (ki_high, ki_low))):
                    ch.step(v.tensor_tensor(low[:, ds(t * P, P)], pQ[:, 0, k * P:(k + 1) * P],
                                            high[:, ds(t * P, P)].bitcast(F32), ALU.subtract))
                for g in range(2):
                    ch.step(v.tensor_copy(kbT[0:AUG, g, ds(t * P, P)], pQ[0:AUG, 0, (2 + g) * P:(3 + g) * P]))
                ch.wait()
                v.sem_inc(q_evac, 1)

            v.wait_ge(consts_here, 96)
            v.wait_ge(pool_init, 1 + HEADS)
            norm(0, 0, 0)
            per = 2 * (2 + 1 + 4 + 4 + 1 + 1 + 6 + 2 + 1 + 6)
            tiles(v, tile, ch, per)
            augment_last = LAST
            t_par[0] = 0
            augment(augment_last)
            copy_k(LAST)


BITS = 32


def count_at_least(v, out, x, cand, cnt):
    return v.tensor_scalar(out, x, cand.bitcast(F32), 0.0, ALU.is_ge, ALU.add, accum_out=cnt)


def judge(v, step, cnt, miss):
    if step == 0:
        return v.tensor_scalar(miss, cnt, float(TOPK), -1.0, ALU.is_lt, ALU.mult)
    return v.tensor_scalar(miss, cnt, float(TOPK), float(1 << (BITS - 1 - step)), ALU.is_lt, ALU.mult)


def next_candidate(v, step, miss, cand):
    if step == 0:
        return v.tensor_scalar(cand, miss, 1 << (BITS - 2), None, ALU.bitwise_xor)
    if step == BITS - 1:
        return v.tensor_tensor(cand, miss, cand, ALU.bitwise_xor)
    return v.scalar_tensor_tensor(out=cand, in0=miss, scalar=1 << (BITS - 2 - step), in1=cand, op0=ALU.bitwise_or, op1=ALU.bitwise_xor)


CHOOSE_STEPS = 8


def choose(v, x, ties, cand, cnt, low):
    least = cand.bitcast(F32)
    yield v.tensor_scalar(ties, x, least, 0.0, ALU.is_gt, ALU.add, accum_out=cnt)
    yield v.tensor_scalar(cnt, cnt, -1.0, float(TOPK), ALU.mult, ALU.add)
    yield v.tensor_scalar(ties, x, least, None, ALU.is_equal)
    yield v.tensor_tensor_scan(ties, ties, ties, 0.0, ALU.add, ALU.max)
    yield v.tensor_scalar(ties, ties, cnt, None, ALU.is_gt)
    yield v.scalar_tensor_tensor(out=ties, in0=x, scalar=least, in1=ties, op0=ALU.is_le, op1=ALU.mult)
    yield v.scalar_tensor_tensor(out=x, in0=x, scalar=least, in1=ties, op0=ALU.is_lt, op1=ALU.max)
    yield v.tensor_scalar(x, x, low, None, ALU.mult)


SPAN = 1024


class Tally:

    def __init__(self, first=0):
        self.n, self.base, self.outer = first, 0, []

    def at(self, more=0):
        return self.base + (self.n + more)

    def add(self, k=1):
        self.n += k

    def enter(self, turn, per):
        self.outer.append((self.n, self.base))
        self.base = self.base + turn * per

    def leave(self, turns, per):
        mark, self.base = self.outer.pop()
        assert self.n - mark == per, (self.n - mark, per)
        self.n = mark + turns * per


def wait(eng, semaphore, value):
    if not isinstance(value, int) or value > 0:
        wait_alone(eng, semaphore, value)


def spans(width):
    return [(c, min(SPAN, width - c)) for c in range(0, width, SPAN)]


def width(t):
    return (t + 1) * P


def attend(nc, PN, QTA, QTB, MASK, MT, keep):
    ka_high, ka_low, ki_high, ki_low = (keep[k] for k in ("ka_high", "ka_low", "ki_high", "ki_low"))
    kbT, va, vb, ident = (keep[k] for k in ("kbT", "va", "vb", "ident"))
    with ExitStack() as ctx:
        def sb(name, shape, dt=F32):
            return ctx.enter_context(nc.sbuf_tensor("at_" + name, shape, dt))

        def sem(name):
            return ctx.enter_context(nc.semaphore(name))

        q_raw = sb("q_raw", [P, HEADS, P])
        q_a = sb("q_a", [P, HEADS, P], F32R)
        q_i = sb("q_i", [P, HEADS, P], F32R)
        qbT = sb("queries_b", [AUG, 2, 4, P])
        wi = [sb(f"wi{p}", [P, HEADS]) for p in range(2)]
        mask = sb("mask", [P, ROWS])
        scores = [sb(f"scores{p}", [P, ROWS]) for p in range(2)]
        cand = sb("cand", [P, 1], I32)
        miss = sb("miss", [P, 1], I32)
        count = sb("count", [P, 1])
        relu = sb("relu", [P, 2, ROWS // 2])
        ties = relu[:].rearrange("p a b -> p (a b)")
        probs = sb("probs", [P, 2, 4, ROWS])
        nmax = sb("nmax", [P, 2 * HEADS])
        pT = sb("pT_sb", [P, 2, 4 * P])
        den = sb("den", [P, 2 * HEADS])
        rden = sb("rden", [P, 2 * HEADS])
        rsum = sb("rsum", [HD, 4, P])
        mixT = sb("mixT", [P, 8, P])
        S = [ctx.enter_context(nc.psum_tensor(f"S{b}", [P, SPAN], F32)) for b in range(2)]
        tr = [ctx.enter_context(nc.psum_tensor(f"tr{b}", [P, 4, P], F32)) for b in range(2)]
        pv = [ctx.enter_context(nc.psum_tensor(f"pv{b}", [P, 4, P], F32)) for b in range(2)]

        raw_here = sem("raw_here")
        q_split = sem("q_split")
        qb_here = sem("qb_here")
        wi_here = sem("wi_here")
        mask_here = sem("mask_here")
        s_full = sem("s_full")
        relu_done = sem("relu_done")
        acc_done = sem("acc_done")
        topk_step = sem("topk_step")
        ttr_done = sem("ttr_done")
        exp_done = sem("exp_done")
        tr_full = sem("tr_full")
        tr_copied = sem("tr_copied")
        pv_step = sem("pv_step")
        norm_step = sem("norm_step")
        rden_done = sem("rden_done")
        mix_stored = sem("mix_stored")

        COUNTS = ("full", "relu", "acc", "topk", "ttr", "exp", "tr", "pvs", "norm")
        FIRST_TOPK = TOPK // P

        def units(t):
            return len(spans(width(t)))

        def weighed(t, g):
            t, g = t + g // 4, g % 4
            return 4 * sum(range(1, t + 1)) + (g + 1) * (t + 1)

        def turned(t, g):
            return weighed(t, g) + max(0, 4 * t + g + 1)

        def has_next_scores(t):
            return FIRST_TOPK <= t + 1 < TILES

        def searched(t):
            return (3 * BITS + 1 + CHOOSE_STEPS) * max(0, t + 1 - FIRST_TOPK)

        def before(t):
            b = sum(units(u) for u in range(t))
            i = sum(HEADS * units(u + 1) for u in range(t) if has_next_scores(u))
            return dict(full=16 * b + i, ttr=16 * b, acc=i)

        def share(nb, j, parts):
            return range(nb * j // parts, nb * (j + 1) // parts)

        block = ctx.enter_context(nc.Block())

        @block.sync
        def _(sp):
            def load_raw(t, a):
                for half in range(2):
                    for e in range(2):
                        to = q_raw[half * HD:(half + 1) * HD].rearrange("p (c e) n -> p e c n", e=2)[:, e]
                        sp.dma_start(to, QTA[ds(t * P + e * HD, HD), a * 512:(a + 1) * 512].rearrange("p (c n) -> p c n", c=4))\
                            .then_inc(raw_here, 16)

            def load_b(t):
                sp.dma_start(qbT[:].rearrange("p a b c -> p (a b c)"), QTB[ds(t * AUG, AUG), :]).then_inc(qb_here, 16)

            def load_wi(t, p):
                sp.dma_start(wi[p][:], PN[ds(t * P, P), WI:WI + HEADS]).then_inc(wi_here, 16)

            def load_mask(t, W):
                sp.dma_start(mask[:, 0:W], MASK[:, ds(ROWS - t * P, W)]).then_inc(mask_here, 16)

            def store_mix(t):
                sp.dma_start(MT[ds(t * P, P), :], mixT[:].rearrange("p a b -> p (a b)")).then_inc(mix_stored, 16)

            def tile(t):
                now = before(t)
                if t + 1 < TILES:
                    wait(sp, q_split, t * 4 + 2)
                    load_raw(t + 1, 1)
                    wait(sp, acc_done, now["acc"])
                    load_wi(t + 1, (t + 1) % 2)
                    wait(sp, q_split, t * 4 + 4)
                    load_raw(t + 1, 0)
                if t > 0:
                    wait(sp, norm_step, 8 * t)
                    store_mix(t - 1)
                if t + 1 < TILES:
                    wait(sp, s_full, now["full"] + 8 * units(t))
                    load_b(t + 1)
                    wait(sp, ttr_done, now["ttr"] + (8 if t >= FIRST_TOPK else 16) * units(t))
                    load_mask(t + 1, width(t + 1))

            load_raw(0, 0)
            load_b(0)
            load_wi(0, 0)
            load_mask(0, width(0))
            for t in range(TILES):
                tile(t)
            wait(sp, norm_step, 8 * TILES)
            store_mix(TILES - 1)
            sp.wait_ge(mix_stored, 16 * TILES)

        @block.gpsimd
        def _(pool):
            def split(q, turn):
                wait(pool, raw_here, turn * 64 + 64)
                pool.tensor_copy(q[:], q_raw[:]).then_inc(q_split, 1)
                wait(pool, q_split, turn * 2 + 1)
                low = slice(HD, P)
                pool.tensor_tensor(q[low], q_raw[low], q[low].bitcast(F32), ALU.subtract).then_inc(q_split, 1)

            split(q_a, 0)
            for t in range(TILES - 1):
                wait(pool, s_full, before(t)["full"])
                split(q_i, t * 2 + 1)
                wait(pool, s_full, before(t + 1)["full"])
                split(q_a, t * 2 + 2)

        @block.tensor
        def _(pe):
            state = dict(kind="ttr", run=0, group=0, tb=0, block=0)
            n = {k: Tally() for k in COUNTS}

            def unit(kind, n, matmuls):
                if state["kind"] != kind:
                    state["before"], state["kind"], state["run"] = state["kind"], kind, 0
                sems = {"ttr": ttr_done, "relu": relu_done}
                if state["run"] < 2 and "before" in state:
                    wait(pe, sems[state["before"]], n[state["before"]].at(state["run"] - 1))
                else:
                    wait(pe, sems[kind], n[kind].at(-1))
                out = S[n["full"].n % 2]
                for lo, w, passes in matmuls:
                    for k, (lhsT, rhs) in enumerate(passes):
                        ins = pe.matmul(out[:, lo:lo + w], lhsT, rhs, start=(k == 0), stop=(k == len(passes) - 1))
                ins.then_inc(s_full, 1)
                n["full"].add()
                n[kind].add()
                state["run"] += 1

            def logits_b(g, h, W, n):
                for c, w in spans(W):
                    unit("ttr", n, [(lo, min(512, w - lo), [(qbT[:, g, h, :], kbT[0:AUG, g, c + lo:c + min(w, lo + 512)])])
                                    for lo in range(0, w, 512)])

            def split_products(kind, q, high, low, W, n):
                for c, w in spans(W):
                    unit(kind, n, [(lo, min(512, w - lo), [(q, keys[:, c + lo:c + min(w, lo + 512)]) for keys in (high, low)])
                                   for lo in range(0, w, 512)])

            def turn(n, into, of):
                wait(pe, tr_copied, n["tr"].at(-1))
                for h in range(4):
                    ins = pe.transpose(tr[state["tb"] % 2][0:into, h, :], of(h), ident[:])
                ins.then_inc(tr_full, 1)
                n["tr"].add()
                state["tb"] += 1

            def weigh(blocks, W, n, values):
                nb = W // P
                grp, bank = state["group"] % 2, state["group"] % 2
                for kb in blocks:
                    if kb == 0:
                        n["exp"].add(4)
                        wait(pe, exp_done, n["exp"].at())
                        wait(pe, norm_step, n["norm"].at(-2))
                    turn(n, P, lambda h: probs[:, grp, h, kb * P:(kb + 1) * P])
                    state["block"] += 1
                    copied = n["tr"].at()
                    if kb == nb - 1:
                        wait(pe, rden_done, state["group"] + 1)
                        slot = 4 * (state["group"] % 4)
                        turn(n, HD, lambda h: rden[:, slot + h:slot + h + 1].to_broadcast([P, HD]))
                    for late in ([kb - 1] if kb > 0 else []) + ([kb] if kb == nb - 1 else []):
                        wait(pe, tr_copied, copied + late - kb)
                        pe.matmul(pv[bank][0:HD].rearrange("p a b -> p (a b)"), values(late), pT[:, (state["block"] - 1 + late - kb) % 2, :],
                                  start=(late == 0), stop=(late == nb - 1)).then_inc(pv_step, 1)
                    if kb == nb - 1:
                        n["norm"].add(2)
                        state["group"] += 1

            def values(g):
                return (lambda kb: vb[:, kb, g, :]) if g < 2 else (lambda kb: va[:, kb, :])

            def indexer(t):
                if has_next_scores(t):
                    wait(pe, q_split, t * 4 + 4)
                    for h in range(HEADS):
                        split_products("relu", q_i[:, h, :], ki_high, ki_low, width(t + 1), n)

            def tile(t):
                W = width(t)
                wait(pe, qb_here, t * 16 + 16)
                for g in range(4):
                    if g == 2:
                        if t >= FIRST_TOPK:
                            indexer(t)
                        wait(pe, q_split, t * 4 + 2)
                    for h in range(4):
                        if g < 2:
                            logits_b(g, h, W, n)
                        else:
                            split_products("ttr", q_a[:, 4 * (g - 2) + h, :], ka_high, ka_low, W, n)
                        if g > 0:
                            weigh(share(t + 1, h, 4), W, n, values(g - 1))
                        elif t > 0:
                            weigh(share(t, h, 4), W - P, n, values(3))
                if t < FIRST_TOPK:
                    indexer(t)

            for t in range(TILES):
                tile(t)
            weigh(range(TILES), ROWS, n, values(3))

        @block.scalar
        def _(act):
            state = dict(group=0, tb=0)
            n = {k: Tally() for k in COUNTS}

            def softmax(W, n, h):
                k = len(spans(W))
                n["ttr"].add(k)
                n["full"].add(k)
                wait(act, ttr_done, n["ttr"].at())
                slot = 4 * (state["group"] % 4) + h
                row = probs[:, state["group"] % 2, h, 0:W]
                act.activation(row, row, ACT.Exp, bias=nmax[:, slot:slot + 1], scale=-1.0,
                               accum_out=den[:, slot:slot + 1]).then_inc(exp_done, 1)
                n["exp"].add()
                if h == 3:
                    state["group"] += 1

            def copies(blocks, nb, n):
                for kb in blocks:
                    n["tr"].add()
                    wait(act, tr_full, n["tr"].at())
                    wait(act, pv_step, n["pvs"].at(-1))
                    act.activation(pT[:, n["pvs"].n % 2, :], tr[state["tb"] % 2][:].rearrange("p a b -> p (a b)"), ACT.Copy)\
                        .then_inc(tr_copied, 1)
                    n["pvs"].add()
                    state["tb"] += 1
                    if kb == nb - 1:
                        n["tr"].add()
                        wait(act, tr_full, n["tr"].at())
                        wait(act, norm_step, n["norm"].at())
                        act.activation(rsum[:], tr[state["tb"] % 2][0:HD], ACT.Copy).then_inc(tr_copied, 1)
                        n["norm"].add(2)
                        state["tb"] += 1

            def relus(W, n):
                for c, w in spans(W):
                    b = n["full"].n % 2
                    n["full"].add()
                    wait(act, s_full, n["full"].at())
                    wait(act, acc_done, n["acc"].at(-1))
                    act.activation(relu[:, b, 0:w], S[b][:, 0:w], ACT.Relu, scale=HD ** -0.5 * HEADS ** -0.5).then_inc(relu_done, 1)
                    n["relu"].add()
                    n["acc"].add()

            def indexer(t):
                if has_next_scores(t):
                    wait(act, topk_step, searched(t))
                    for h in range(HEADS):
                        relus(width(t + 1), n)

            def tile(t):
                for g in range(4):
                    if g == 2 and t >= FIRST_TOPK:
                        indexer(t)
                    for h in range(4):
                        if g > 0:
                            copies(share(t + 1, h, 4), t + 1, n)
                        elif t > 0:
                            copies(share(t, h, 4), t, n)
                        softmax(width(t), n, h)
                if t < FIRST_TOPK:
                    indexer(t)

            for t in range(TILES):
                tile(t)
            copies(range(TILES), TILES, n)

        @block.vector
        def _(v):
            state = dict(group=0, out=0)
            n = {k: Tally() for k in COUNTS}

            def logits(W, n, bias, h, read):
                grp = state["group"] % 2
                if h == 0:
                    wait(v, tr_full, read)
                slot = 4 * (state["group"] % 4) + h
                for k, (c, w) in enumerate(spans(W)):
                    b = n["full"].n % 2
                    n["full"].add()
                    wait(v, s_full, n["full"].at())
                    if k:
                        wait(v, ttr_done, n["ttr"].at())
                    v.tensor_tensor_reduce(probs[:, grp, h, c:c + w], S[b][:, 0:w], bias[:, c:c + w], -HD ** -0.5,
                                           nmax[:, slot:slot + 1] if k else 3.4e38, ALU.add, ALU.min,
                                           nmax[:, slot:slot + 1]).then_inc(ttr_done, 1)
                    n["ttr"].add()
                if h == 3:
                    state["group"] += 1

            def invert_sums(k):
                wait(v, exp_done, 4 * (k + 1))
                slots = slice(4 * (k % 4), 4 * (k % 4) + 4)
                v.reciprocal(rden[:, slots], den[:, slots]).then_inc(rden_done, 1)

            def normalise(first, n, t, g):
                wait(v, pv_step, weighed(t, g))
                wait(v, tr_copied, turned(t, g))
                o = pv[state["out"] % 2]
                for k in range(2):
                    v.tensor_tensor(mixT[k * HD:(k + 1) * HD, first:first + 2, :], o[0:HD, k::2, :], rsum[:, k::2, :],
                                    ALU.mult).then_inc(norm_step, 1)
                    n["norm"].add()
                state["out"] += 1

            def index_scores(t):
                wait(v, mask_here, t * 16 + 16)
                wait(v, wi_here, t * 16 + 16)
                for h in range(HEADS):
                    for c, w in spans(width(t)):
                        b = n["full"].n % 2
                        n["full"].add()
                        n["relu"].add()
                        wait(v, relu_done, n["relu"].at())
                        if h:
                            wait(v, acc_done, n["acc"].at(1 - units(t)))
                        v.scalar_tensor_tensor(out=scores[t % 2][:, c:c + w], in0=relu[:, b, 0:w], scalar=wi[t % 2][:, h:h + 1],
                                               in1=(scores[t % 2] if h else mask)[:, c:c + w], op0=ALU.mult, op1=ALU.add)\
                            .then_inc(acc_done, 1)
                        n["acc"].add()
                wait(v, acc_done, n["acc"].at())

            def chained(n, ins):
                ins.then_inc(topk_step, 1)
                n["topk"].add()
                wait(v, topk_step, n["topk"].at())

            def search(t, steps):
                W = width(t)
                for step in steps:
                    if step == 0:
                        chained(n, v.memset(cand[:], 0))
                    chained(n, count_at_least(v, ties[:, 0:W], scores[t % 2][:, 0:W], cand[:], count[:]))
                    chained(n, judge(v, step, count[:], miss[:]))
                    chained(n, next_candidate(v, step, miss[:], cand[:]))

            def steps_beside(t, g, h):
                half = BITS // 2
                if g >= 2:
                    first = (4 * (g - 2) + h) * half // 8
                    return t + 1, range(first, first + half // 8) if FIRST_TOPK < t + 1 < TILES else ()
                if t == FIRST_TOPK:
                    first = (4 * g + h) * BITS // 8
                    return t, range(first, first + BITS // 8)
                first = half + (4 * g + h) * half // 8
                return t, range(first, first + half // 8) if t > FIRST_TOPK else ()

            def tile(t):
                W = width(t)
                wait(v, mask_here, t * 16 + 16)
                bias = mask
                for g in range(4):
                    if g == 2 and t >= FIRST_TOPK:
                        bias = scores[t % 2]
                        for ins in choose(v, bias[:, 0:W], ties[:, 0:W], cand[:], count[:], NEG):
                            chained(n, ins)
                        if has_next_scores(t):
                            index_scores(t + 1)
                    for h in range(4):
                        search(*steps_beside(t, g, h))
                        if h == 1 and t + g > 0:
                            invert_sums(4 * t + g - 1)
                        if h == 2 and (t > 0 or g >= 2):
                            if g == 2 and t > 0:
                                wait(v, mix_stored, t * 16)
                            normalise((0, 2, 4, 6)[g], n, t, g - 2)
                        logits(W, n, bias, h, turned(t, g - 2) if t > 0 or g >= 2 else 0)
                if t < FIRST_TOPK and has_next_scores(t):
                    index_scores(t + 1)

            for t in range(TILES):
                tile(t)
            invert_sums(4 * TILES - 1)
            for g in range(2):
                normalise(2 * g, n, TILES - 1, 2 + g)


GROUPS = 5
GCOLS = -(-ALL // (2 * GROUPS)) * 2
FC = D_FF // P
BLOCKS = -(-GCOLS // P)


def mix_out(nc, MT, HN, W_O, LN_G, LN_B, H1T, keep):
    ident = keep["ident"]
    with ExitStack() as ctx:
        def sb(name, shape, dt=F32):
            return ctx.enter_context(nc.sbuf_tensor(name, shape, dt))

        def sem(name):
            return ctx.enter_context(nc.semaphore(name))

        w_o = sb("w_o", [P, KD, D])
        g1 = sb("g1", [P, D])
        b1 = sb("b1", [P, D])
        mixT = [sb(f"mo_mixT{p}", [P, KD, P]) for p in range(2)]
        hn = [sb(f"mo_h{p}", [P, D]) for p in range(2)]
        z = [sb(f"mo_z{p}", [P, D]) for p in range(2)]
        h1T = [sb(f"mo_h1T{p}", [P, KD, P]) for p in range(2)]
        stats = sb("mo_stats", [P, 12])
        mv = sb("mo_mv", [P, 2])
        sd = sb("mo_sd", [P, 1])
        rs = sb("mo_rs", [P, 1])
        eps = sb("mo_eps", [P, 1])
        po = [ctx.enter_context(nc.psum_tensor(f"mo_po{p}", [P, D], F32)) for p in range(2)]
        pt = [ctx.enter_context(nc.psum_tensor(f"mo_pt{p}", [P, D], F32)) for p in range(2)]

        w_here = sem("mo_w_here")
        in_here = [sem(f"mo_in_here{p}") for p in range(2)]
        eps_set = sem("mo_eps_set")
        o_ps = sem("mo_o_ps")
        z_done = sem("mo_z_done")
        var_done = sem("mo_var_done")
        sd_done = sem("mo_sd_done")
        ln_step = sem("mo_ln_step")
        h1_done = sem("mo_h1_done")
        t_ps = sem("mo_t_ps")
        t_copied = sem("mo_t_copied")
        stored = [sem(f"mo_stored{p}") for p in range(2)]

        LN_STEPS = 5

        def run(eng, body):
            ln = Tally()
            for t in range(3):
                body(t, t % 2, t // 2, ln)
                ln.add(LN_STEPS)
            turns = (TILES - 3) // 2
            with eng.Fori(0, turns) as i:
                ln.enter(i, 2 * LN_STEPS)
                for t in (3, 4):
                    body(2 * i + t, t % 2, i + t // 2, ln)
                    ln.add(LN_STEPS)
                ln.leave(turns, 2 * LN_STEPS)

        block = ctx.enter_context(nc.Block())

        @block.sync
        def _(sp):
            for k in range(KD):
                sp.dma_start(w_o[:, k, :], W_O[k * P:(k + 1) * P, :]).then_inc(w_here, 16)
            sp.dma_start(g1[:], LN_G.unsqueeze(0).to_broadcast([P, D])).then_inc(w_here, 16)
            sp.dma_start(b1[:], LN_B.unsqueeze(0).to_broadcast([P, D])).then_inc(w_here, 16)

            def tile(t, p, i, ln):
                if not (isinstance(t, int) and t < 2):
                    wait_alone(sp, o_ps, t - 1)
                    wait_alone(sp, z_done, 2 * t - 2)
                sp.dma_start(mixT[p][:].rearrange("p a b -> p (a b)"), MT[ds(t * P, P), :]).then_inc(in_here[p], 16)
                sp.dma_start(hn[p][:], HN[ds(t * P, P), :]).then_inc(in_here[p], 16)

            run(sp, tile)

        @block.gpsimd
        def _(pool):
            pool.memset(eps[:], EPS).then_inc(eps_set, 1)

            def tile(t, p, i, ln):
                wait_alone(pool, t_copied, t + 1)
                pool.dma_start(H1T.rearrange("(k p) n -> p k n", p=P)[:, :, ds(t * P, P)], h1T[p][:]).then_inc(stored[p], 16)

            run(pool, tile)
            for p in range(2):
                wait_alone(pool, stored[p], 16 * (TILES // 2 + 1 - p))

        @block.tensor
        def _(pe):
            def turn(t, p):
                wait_alone(pe, h1_done, t + 1)
                if not (isinstance(t, int) and t < 2):
                    wait_alone(pe, t_copied, t - 1)
                for k in range(KD):
                    ins = pe.transpose(pt[p][:, k * P:(k + 1) * P], z[p][:, k * P:(k + 1) * P], ident[:])
                ins.then_inc(t_ps, 1)

            def tile(t, p, i, ln):
                wait_alone(pe, in_here[p], 32 * (i + 1))
                if not (isinstance(t, int) and t < 2):
                    wait_alone(pe, z_done, 2 * t - 2)
                for j in range(2):
                    for k in range(KD):
                        ins = pe.matmul(po[p][:, j * 512:(j + 1) * 512], mixT[p][:, k, :], w_o[:, k, j * 512:(j + 1) * 512],
                                        start=(k == 0), stop=(k == KD - 1))
                ins.then_inc(o_ps, 1)
                if not (isinstance(t, int) and t == 0):
                    turn(t - 1, 1 - p)

            wait_alone(pe, w_here, 16 * (KD + 2))
            run(pe, tile)
            turn(TILES - 1, 0)

        @block.scalar
        def _(act):
            def copy(t, p, i):
                act.wait_ge(t_ps, t + 1)
                if not (isinstance(t, int) and t < 2):
                    act.wait_ge(stored[p], 16 * i)
                act.activation(h1T[p][:].rearrange("p a b -> p (a b)"), pt[p][:], ACT.Copy).then_inc(t_copied, 1)

            def tile(t, p, i, ln):
                act.wait_ge(var_done, t + 1)
                act.activation(sd[:], mv[:, 1:2], ACT.Sqrt, bias=eps[:]).then_inc(sd_done, 1)
                if not (isinstance(t, int) and t == 0):
                    copy(t - 1, 1 - p, i if p else i - 1)

            act.wait_ge(eps_set, 1)
            run(act, tile)
            copy(TILES - 1, 0, TILES // 2)

        @block.vector
        def _(v):
            def tile(t, p, i, ln):
                v.wait_ge(in_here[p], 32 * (i + 1))
                v.wait_ge(o_ps, t + 1)
                if not (isinstance(t, int) and t < 2):
                    v.wait_ge(t_ps, t - 1)
                for j in range(2):
                    c = slice(j * 512, (j + 1) * 512)
                    v.scalar_tensor_tensor(out=z[p][:, c], in0=hn[p][:, c], scalar=ALPHA, in1=po[p][:, c],
                                           op0=ALU.mult, op1=ALU.add).then_inc(z_done, 1)
                v.wait_ge(z_done, 2 * t + 2)
                for j in range(2):
                    v.bn_stats(stats[:, 6 * j:6 * j + 6], z[p][:, j * 512:(j + 1) * 512]).then_inc(ln_step, 1)
                wait_alone(v, ln_step, ln.at(2))
                v.bn_aggr(mv[:], stats[:]).then_inc(var_done, 1)
                v.wait_ge(sd_done, t + 1)
                v.wait_ge(var_done, t + 1)
                v.reciprocal(rs[:], sd[:]).then_inc(ln_step, 1)
                v.wait_ge(ln_step, ln.at(3))
                v.tensor_scalar(z[p][:], z[p][:], mv[:, 0:1], rs[:], ALU.subtract, ALU.mult).then_inc(ln_step, 1)
                v.wait_ge(ln_step, ln.at(4))
                v.tensor_tensor(z[p][:], z[p][:], g1[:], ALU.mult).then_inc(ln_step, 1)
                v.wait_ge(ln_step, ln.at(5))
                v.tensor_tensor(z[p][:], z[p][:], b1[:], ALU.add).then_inc(h1_done, 1)

            v.wait_ge(w_here, 16 * (KD + 2))
            run(v, tile)


def feed_forward(nc, H1T, W_GATE, W_UP, W_DOWN, LN_G, LN_B, Y, keep):
    ident = keep["ident"]
    with ExitStack() as ctx:
        def sb(name, shape, dt=F32):
            return ctx.enter_context(nc.sbuf_tensor("ff_" + name, shape, dt))

        def sem(name):
            return ctx.enter_context(nc.semaphore("ff_" + name))

        zT = sb("zT", [P, KD, GCOLS])
        h_high = sb("h_high", [P, KD, GCOLS], F32R)
        h_low = sb("h_low", [P, KD, GCOLS], F32R)
        silu = sb("silu", [P, 2, GCOLS])
        hid = sb("hid", [P, 2, GCOLS])
        hid_high = sb("hid_high", [P, FC, GCOLS], F32R)
        hid_low = sb("hid_low", [P, FC, GCOLS], F32R)
        w_raw = [sb(f"w_raw{p}", [P, FC * P]) for p in range(2)]
        w_high = [sb(f"w_high{p}", [P, FC * P], F32R) for p in range(2)]
        w_low = [sb(f"w_low{p}", [P, FC * P], F32R) for p in range(2)]
        g2 = sb("g2", [P, D])
        b2 = sb("b2", [P, D])
        y = [sb(f"y{p}", [P, D]) for p in range(2)]
        stats = sb("stats", [P, 12])
        mv = sb("mv", [P, 2])
        sd = sb("sd", [P, 1])
        rs = sb("rs", [P, 1])
        eps = sb("eps", [P, 1])
        ps = [ctx.enter_context(nc.psum_tensor(f"ff_ps{p}", [P, 4, 512], F32)) for p in range(2)]

        consts = sem("consts")
        eps_set = sem("eps_set")
        h_here = sem("h_here")
        h_high_done = sem("h_high_done")
        h_low_done = sem("h_low_done")
        w_here = [sem(f"w_here{p}") for p in range(2)]
        w_high_done = sem("w_high_done")
        w_low_done = sem("w_low_done")
        products = sem("products")
        silu_done = sem("silu_done")
        hid_done = sem("hid_done")
        hid_high_done = sem("hid_high_done")
        hid_low_done = sem("hid_low_done")
        z_done = sem("z_done")
        t_ps = sem("t_ps")
        ln_step = sem("ln_step")
        var_done = sem("var_done")
        sd_done = sem("sd_done")
        y_done = sem("y_done")
        y_free = sem("y_free")
        y_stored = [sem(f"y_stored{p}") for p in range(2)]

        HIDDEN = dict(w=2, hid=2)
        DOWN = dict(w=2, z=2)
        AHEAD = dict(w=2, hid=2, z=2, y=1, t=1)
        BLOCK = dict(t=1, ln=5, var=1, y=1)
        hidden_cols, down_cols = 2 * KD * P, FC * P

        def run(eng, start, hidden, down, rows):
            n = {k: Tally(AHEAD.get(k, 0)) for k in (*HIDDEN, *DOWN, *BLOCK)}
            group = {k: (HIDDEN.get(k, 0) * FC + DOWN.get(k, 0) * KD) // 2 + BLOCK.get(k, 0) * BLOCKS for k in n}

            def pairs(g, part, grows, count, cols, last_cols):
                def pair(at, cols_behind):
                    for p in range(2):
                        if part:
                            part(g, at + p, p, n, cols_behind if p else cols)
                        for k, per in grows.items():
                            n[k].add(per // 2)

                with eng.Fori(0, count // 2 - 1) as i:
                    for k, per in grows.items():
                        n[k].enter(i, per)
                    pair(2 * i, cols)
                    for k, per in grows.items():
                        n[k].leave(count // 2 - 1, per)
                pair(count - 2, last_cols)

            with eng.Fori(0, GROUPS) as g:
                for k in n:
                    n[k].enter(g, group[k])
                start(g, n)
                pairs(g, hidden, HIDDEN, FC, hidden_cols, down_cols)
                pairs(g, down, DOWN, KD, down_cols, 0)
                for r in range(BLOCKS):
                    if rows:
                        rows(g, r, min(P, GCOLS - r * P), n)
                    for k, per in BLOCK.items():
                        n[k].add(per)
                for k in n:
                    n[k].leave(GROUPS, group[k])

        def block_bank(r):
            first = 2 if r < 2 else 0
            return ps[r % 2][:, first:first + 2, :].rearrange("p a b -> p (a b)")

        block = ctx.enter_context(nc.Block())

        @block.sync
        def _(sp):
            sp.dma_start(g2[:], LN_G.unsqueeze(0).to_broadcast([P, D])).then_inc(consts, 16)
            sp.dma_start(b2[:], LN_B.unsqueeze(0).to_broadcast([P, D])).then_inc(consts, 16)

            def start(g, n):
                wait_alone(sp, t_ps, n["t"].at())
                sp.dma_start(zT[:], H1T.rearrange("(k p) n -> p k n", p=P)[:, :, ds(g * GCOLS, GCOLS)]).then_inc(h_here, 16)

            def hidden(g, f, p, n, cols_next):
                wait_alone(sp, w_low_done, n["w"].at(-1))
                for m, src in enumerate((W_GATE, W_UP)):
                    to = w_raw[p][:, m * KD * P:(m + 1) * KD * P].rearrange("p (k n) -> p k n", n=P)
                    sp.dma_start(to, src.rearrange("(k p) n -> p k n", p=P)[:, :, ds(f * P, P)]).then_inc(w_here[p], 16)

            def down(g, d, p, n, cols_next):
                wait_alone(sp, w_low_done, n["w"].at(-1))
                for m in range(2):
                    part = slice(m * FC // 2, (m + 1) * FC // 2)
                    sp.dma_start(w_raw[p][:].rearrange("p (f n) -> p f n", n=P)[:, part],
                                 W_DOWN.rearrange("(f p) n -> p f n", p=P)[:, part, ds(d * P, P)]).then_inc(w_here[p], 16)

            run(sp, start, hidden, down, None)

        @block.gpsimd
        def _(pool):
            pool.memset(eps[:], EPS).then_inc(eps_set, 1)

            def rows(g, r, m, n):
                wait_alone(pool, y_done, n["y"].at(1))
                pool.dma_start(Y[ds(g * GCOLS + r * P, m), :], y[r % 2][0:m, :]).then_inc(y_stored[r % 2], 16)
                if r == BLOCKS - 1:
                    for p in range(2):
                        wait_alone(pool, y_stored[p], (g + 1) * (16 * BLOCKS // 2))
                    pool.sem_inc(y_free, 1)

            pool.sem_inc(y_free, 1)
            run(pool, lambda g, n: None, None, None, rows)

        @block.tensor
        def _(pe):
            def three(out, at, high, low, p, first, last):
                w = slice(at * P, (at + 1) * P)
                pe.matmul(out, w_high[p][:, w], high, start=first, stop=False)
                pe.matmul(out, w_high[p][:, w], low, start=False, stop=False)
                return pe.matmul(out, w_low[p][:, w], high, start=False, stop=last)

            def start(g, n):
                wait_alone(pe, h_low_done, g + 1)
                wait_alone(pe, y_done, n["y"].at())

            def hidden(g, f, p, n, cols_next):
                wait_alone(pe, w_low_done, n["w"].at(1))
                wait_alone(pe, hid_done, n["hid"].at(-1))
                for m in range(2):
                    for k in range(KD):
                        ins = three(ps[p][:, m, 0:GCOLS], m * KD + k, h_high[:, k, :], h_low[:, k, :], p, k == 0, k == KD - 1)
                ins.then_inc(products, 1)

            def down(g, d, p, n, cols_next):
                wait_alone(pe, w_low_done, n["w"].at(1))
                wait_alone(pe, hid_low_done, n["hid"].at())
                wait_alone(pe, z_done, n["z"].at(-1))
                for f in range(FC):
                    ins = three(ps[p][:, 0, 0:GCOLS], f, hid_high[:, f, :], hid_low[:, f, :], p, f == 0, f == FC - 1)
                ins.then_inc(products, 1)

            def rows(g, r, m, n):
                if r == 0:
                    wait_alone(pe, z_done, n["z"].at())
                for k in range(KD):
                    ins = pe.transpose(block_bank(r)[0:m, k * P:(k + 1) * P], zT[:, k, r * P:r * P + m], ident[:])
                ins.then_inc(t_ps, 1)

            pe.sem_inc(products, AHEAD["w"])
            pe.sem_inc(t_ps, AHEAD["t"])
            run(pe, start, hidden, down, rows)

        @block.scalar
        def _(act):
            def split(p, n, more, cols):
                act.wait_ge(w_here[p], (n["w"].at(more - AHEAD["w"]) - p) * 16 + 32)
                act.wait_ge(products, n["w"].at(more - 1))
                act.activation(w_high[p][:, 0:cols], w_raw[p][:, 0:cols], ACT.Copy).then_inc(w_high_done, 1)

            def start(g, n):
                act.wait_ge(h_here, g * 16 + 16)
                act.wait_ge(products, n["w"].at())
                act.activation(h_high[:], zT[:], ACT.Copy).then_inc(h_high_done, 1)
                split(0, n, 0, hidden_cols)

            def hidden(g, f, p, n, cols_next):
                split(1 - p, n, 1, cols_next)
                act.wait_ge(products, n["w"].at(1))
                act.wait_ge(hid_done, n["hid"].at(-1))
                act.activation(silu[:, p], ps[p][:, 0, 0:GCOLS], ACT.Silu).then_inc(silu_done, 1)
                act.wait_ge(hid_done, n["hid"].at(1))
                act.activation(hid_high[:, ds(f, 1), :].squeeze(1), hid[:, p], ACT.Copy).then_inc(hid_high_done, 1)

            def down(g, d, p, n, cols_next):
                if cols_next:
                    split(1 - p, n, 1, cols_next)

            def rows(g, r, m, n):
                act.wait_ge(var_done, n["var"].at(1))
                act.activation(sd[0:m], mv[0:m, 1:2], ACT.Sqrt, bias=eps[0:m]).then_inc(sd_done, 1)

            act.wait_ge(eps_set, 1)
            act.sem_inc(w_high_done, AHEAD["w"])
            act.sem_inc(hid_high_done, AHEAD["hid"])
            act.sem_inc(silu_done, AHEAD["hid"])
            run(act, start, hidden, down, rows)

        @block.vector
        def _(v):
            def split(p, n, more, cols):
                v.wait_ge(w_high_done, n["w"].at(more + 1))
                v.tensor_tensor(w_low[p][:, 0:cols], w_raw[p][:, 0:cols], w_high[p][:, 0:cols].bitcast(F32),
                                ALU.subtract).then_inc(w_low_done, 1)

            def start(g, n):
                v.wait_ge(h_high_done, g + 1)
                v.tensor_tensor(h_low[:], zT[:], h_high[:].bitcast(F32), ALU.subtract).then_inc(h_low_done, 1)
                split(0, n, 0, hidden_cols)

            def hidden(g, f, p, n, cols_next):
                split(1 - p, n, 1, cols_next)
                v.wait_ge(silu_done, n["hid"].at(1))
                v.wait_ge(hid_low_done, n["hid"].at(-1))
                v.tensor_tensor(hid[:, p], silu[:, p], ps[p][:, 1, 0:GCOLS], ALU.mult).then_inc(hid_done, 1)
                v.wait_ge(hid_high_done, n["hid"].at(1))
                v.tensor_tensor(hid_low[:, ds(f, 1), :].squeeze(1), hid[:, p], hid_high[:, ds(f, 1), :].squeeze(1).bitcast(F32),
                                ALU.subtract).then_inc(hid_low_done, 1)

            def down(g, d, p, n, cols_next):
                if cols_next:
                    split(1 - p, n, 1, cols_next)
                v.wait_ge(products, n["w"].at(1))
                v.scalar_tensor_tensor(out=zT[:, ds(d, 1), :].squeeze(1), in0=zT[:, ds(d, 1), :].squeeze(1), scalar=ALPHA,
                                       in1=ps[p][:, 0, 0:GCOLS], op0=ALU.mult, op1=ALU.add).then_inc(z_done, 1)

            def rows(g, r, m, n):
                x = block_bank(r)[0:m]
                out = y[r % 2][0:m, :]
                ln = n["ln"].at
                v.wait_ge(t_ps, n["t"].at(1))
                for j in range(2):
                    v.bn_stats(stats[0:m, 6 * j:6 * j + 6], x[:, j * 512:(j + 1) * 512]).then_inc(ln_step, 1)
                wait_alone(v, ln_step, ln(2))
                v.bn_aggr(mv[0:m], stats[0:m]).then_inc(var_done, 1)
                v.wait_ge(sd_done, n["var"].at(1))
                v.wait_ge(var_done, n["var"].at(1))
                v.reciprocal(rs[0:m], sd[0:m]).then_inc(ln_step, 1)
                v.wait_ge(ln_step, ln(3))
                if r < 2:
                    v.wait_ge(y_free, g + 1)
                else:
                    v.wait_ge(y_stored[r % 2], (g * (BLOCKS // 2) + r // 2) * 16)
                v.tensor_scalar(out, x, mv[0:m, 0:1], rs[0:m], ALU.subtract, ALU.mult).then_inc(ln_step, 1)
                v.wait_ge(ln_step, ln(4))
                v.tensor_tensor(out, out, g2[0:m], ALU.mult).then_inc(ln_step, 1)
                v.wait_ge(ln_step, ln(5))
                v.tensor_tensor(out, out, b2[0:m], ALU.add).then_inc(y_done, 1)

            for semaphore, first in ((w_low_done, "w"), (hid_done, "hid"), (hid_low_done, "hid"), (z_done, "z"), (y_done, "y")):
                v.sem_inc(semaphore, AHEAD[first])
            v.wait_ge(consts, 32)
            run(v, start, hidden, down, rows)


NB = N_SAMPLE
BH = NB * HEADS
RUN = 4
CHUNK = P * RUN
CHUNKS = PAST // CHUNK
UNITS = PAGE // RUN
SROW = TOTAL
FAR = -1.0e30
CHUNK_W = CHUNK + 1
NEW = CHUNKS * CHUNK_W - 1


def decode(nc, PN, PAGE_TABLE, CACHE_A, CACHE_I, CACHE_B, CACHE_LF, CONST, PMOD, EXPAND, SEQS, SC, OS, MT, keep):
    ident, ones = keep["ident"], keep["ones"]
    with ExitStack() as ctx:
        def sb(name, shape, dt=F32):
            return ctx.enter_context(nc.sbuf_tensor("de_" + name, shape, dt))

        def sem(name):
            return ctx.enter_context(nc.semaphore(name))

        after = sb("after", [P, P])
        expand = sb("expand", [P, BH])
        pmod = sb("pmod", [P, 1])
        pages = sb("pages", [P, NB, CHUNKS], I32)
        runs = sb("runs", [P, NB, CHUNKS], I32)
        run_now = [sb(f"run_now{p}", [P, NB], I32) for p in range(2)]
        q_b = sb("q_b", [P, NB * (BH + HEADS)])
        q_a = sb("q_a", [P, NB * (BH + HEADS)])
        q_i = sb("q_i", [P, NB * (P + HEADS)])
        kn_b = sb("kn_b", [P, NB])
        kn_a = sb("kn_a", [HD, NB])
        kn_i = sb("kn_i", [HD, NB])
        w_sel = sb("w_sel", [P, 2, NB])
        scores = sb("d_scores", [NB, CHUNKS * CHUNK_W])
        work = sb("d_work", [P, CHUNKS * CHUNK_W])
        spread = sb("spread", [P, CHUNK_W])
        chosen = sb("chosen", [P, CHUNK_W])
        ties = sb("d_ties", [P, CHUNK_W])
        same = sb("same", [P, P])
        sooner = sb("sooner", [P, P])
        cand = sb("d_cand", [P, 1], I32)
        miss = sb("d_miss", [P, 1], I32)
        count = sb("d_count", [P, 1])
        left = sb("d_left", [P, 1])
        kv = sb("kv", [P, 2, NB, RUN * 256])
        lf = sb("d_lf", [P, 2, NB, RUN * HEADS])
        lf_r = sb("lf_r", [P, RUN, BH])
        lf_later = sb("lf_later", [P, BH])
        kT = sb("kT_d", [P, 2, CHUNK])
        relu = sb("d_relu", [P, CHUNK // 2])
        prob = sb("prob", [BH, CHUNK])
        pT = sb("d_pT", [P, RUN, NB * (BH + HEADS)])
        m_old = sb("m_old", [BH, 1])
        m_new = sb("m_new", [BH, 1])
        neg_m = sb("neg_m", [BH, 1])
        shrink = sb("shrink", [BH, 1])
        den = sb("den", [BH, 1])
        den_c = sb("den_c", [BH, 1])
        rden = sb("rden", [BH, 1])
        o = sb("o_d", [BH, P])

        tr = [ctx.enter_context(nc.psum_tensor(f"d_tr{b}", [P, 512], F32)) for b in range(2)]
        S = [ctx.enter_context(nc.psum_tensor(f"d_S{b}", [P, 512], F32)) for b in range(2)]
        pw = ctx.enter_context(nc.psum_tensor("d_pw", [P, 512], F32))
        pt = ctx.enter_context(nc.psum_tensor("d_pt", [P, 512], F32))
        po = ctx.enter_context(nc.psum_tensor("d_po", [P, 512], F32))

        in_dma = sem("d_in_dma")
        pages_here = sem("d_pages")
        zeroed = sem("d_zeroed")
        prep = sem("d_prep")
        topk_step = sem("d_topk_step")

        def own(q, b_cols):
            return q.rearrange("p (b x) -> p b x", x=BH + HEADS)[:, :, b_cols]

        with nc.Block() as block:
            @block.sync
            def _(sp):
                sp.dma_start(after[:], CONST[3]).then_inc(in_dma, 16)
                sp.dma_start(expand[:], EXPAND).then_inc(in_dma, 16)
                sp.dma_start(pmod[:], PMOD).then_inc(in_dma, 16)
                sp.dma_start(same[:], SEQS[0]).then_inc(in_dma, 16)
                sp.dma_start(sooner[:], SEQS[1]).then_inc(in_dma, 16)
                with nc.allow_non_contiguous_dma(reason="the page table once per partition"):
                    for q in range(P // UNITS):
                        sp.dma_start(pages[q * UNITS:(q + 1) * UNITS].rearrange("p b c -> p (b c)"),
                                     PAGE_TABLE.rearrange("b (c q) -> q (b c)", q=RUN)[q:q + 1, :].to_broadcast([UNITS, NB * CHUNKS]))\
                            .then_inc(pages_here, 16)
                wait_alone(sp, zeroed, 5)
                rows = PN[SROW:SROW + NB, :]
                with nc.allow_non_contiguous_dma(reason="a few thousand elements"):
                    for g in range(2):
                        half = slice(g * HD, (g + 1) * HD)
                        for b in range(NB):
                            row = PN[SROW + b:SROW + b + 1, :]
                            sp.dma_start(own(q_b[half], slice(4 * g, 4 * g + 4))[:, b, :],
                                         row[:, QB + g * 256:QB + (g + 1) * 256].rearrange("o (h d) -> d (o h)", d=HD)).then_inc(in_dma, 16)
                            if g == 0:
                                sp.dma_start(own(q_a[half], slice(0, HEADS))[:, b, :],
                                             row[:, QA:QA + 512].rearrange("o (h d) -> d (o h)", d=HD)).then_inc(in_dma, 16)
                            at = b * (P + HEADS) + g * HD
                            sp.dma_start(q_i[half, at:at + HEADS],
                                         row[:, QI:QI + 512].rearrange("o (h d) -> d (o h)", d=HD)).then_inc(in_dma, 16)
                    sp.dma_start(kn_b[:], rows[:, KB:KB + P].rearrange("b n -> n b")).then_inc(in_dma, 16)
                    sp.dma_start(kn_a[:], rows[:, KA:KA + HD].rearrange("b n -> n b")).then_inc(in_dma, 16)
                    sp.dma_start(kn_i[:], rows[:, KI:KI + HD].rearrange("b n -> n b")).then_inc(in_dma, 16)
                    for b in range(NB):
                        for g in range(2):
                            at = g * BH + b * HEADS
                            sp.dma_start(w_sel[at:at + HEADS, g, b:b + 1],
                                         rows[b:b + 1, WI:WI + HEADS].rearrange("o h -> h o")).then_inc(in_dma, 16)
                        sp.dma_start(lf_later[0:1, b * HEADS:(b + 1) * HEADS], rows[b:b + 1, FL:FL + HEADS]).then_inc(in_dma, 16)
                wait_alone(sp, in_dma, 16 * (5 + 5 * NB + 3 + 3 * NB))

            @block.gpsimd
            def _(pool):
                pool.memset(q_b[:], 0.0).then_inc(zeroed, 1)
                pool.memset(q_a[:], 0.0).then_inc(zeroed, 1)
                pool.memset(q_i[:], 0.0).then_inc(zeroed, 1)
                pool.memset(w_sel[:], 0.0).then_inc(zeroed, 1)
                pool.memset(lf_later[:], 0.0).then_inc(zeroed, 1)
                pool.memset(pT[:], 0.0)
                pool.memset(work[:], 0.0)
                pool.memset(scores[:], NEG)
                pool.memset(lf_r[:], 0.0)

            @block.vector
            def _(v):
                v.wait_ge(pages_here, 16 * (P // UNITS))
                v.wait_ge(in_dma, 16 * (5 + 5 * NB + 3 + 3 * NB))
                v.tensor_scalar(runs[:], pages[:], float(UNITS), pmod[:], ALU.mult, ALU.add).then_inc(prep, 1)
                for q in (q_b, q_a):
                    v.tensor_scalar(q[:], q[:], HD ** -0.5, None, ALU.mult).then_inc(prep, 1)

        def heads_of(q, rows, b, width=BH):
            return q[rows, b * width:b * width + BH]

        def walk(kind):
            width = {"i": HD, "a": 2 * HD, "b": 4 * HD}[kind]
            pool_rows = {"i": CACHE_I, "a": CACHE_A, "b": CACHE_B}[kind]
            vcol, vw = {"i": (0, 0), "a": (HD, HD), "b": (P, P)}[kind]
            q = {"i": q_i, "a": q_a, "b": q_b}[kind]
            knew = {"i": kn_i, "a": kn_a, "b": kn_b}[kind]
            kd = P if kind == "b" else HD
            nblk = RUN // 2 if kind == "i" else RUN
            with ExitStack() as sub:
                def ksem(name):
                    return sub.enter_context(nc.semaphore(f"{kind}_{name}"))

                kv_here = [ksem(f"kv_here{p}") for p in range(2)]
                v0_here = ksem("v0_here")
                idx_done = ksem("idx_done")
                turned = ksem("turned")
                kt_copied = ksem("kt_copied")
                qk = ksem("qk")
                s_full = ksem("s_full")
                s_read = ksem("s_read")
                lf_step = ksem("lf_step")
                w_ps = ksem("w_ps")
                w_read = ksem("w_read")
                mx = ksem("mx")
                shrunk = ksem("shrunk")
                pt_ps = ksem("pt_ps")
                pt_copied = ksem("pt_copied")
                pv_ps = ksem("pv_ps")
                upd = ksem("upd")
                stored = ksem("stored")
                def reach(eng, semaphore, value):
                    wait_alone(eng, semaphore, value + 1)

                PER = dict(seq=NB, chunk=1, mx=4, upd=2, lf=5)

                def run(eng, body):
                    n = {k: Tally() for k in PER}
                    with eng.Fori(0, CHUNKS // 2) as i:
                        for k, per in PER.items():
                            n[k].enter(i, 2 * per)
                        for p in range(2):
                            body(i * -2 + (CHUNKS - 1 - p), p, i, n)
                            for k, per in PER.items():
                                n[k].add(per)
                        for k, per in PER.items():
                            n[k].leave(CHUNKS // 2, 2 * per)
                    return n

                attn = kind != "i"
                block = sub.enter_context(nc.Block())

                @block.sync
                def _(sp):
                    if not attn:
                        return
                    base = {"a": VA, "b": VB}[kind]
                    for b in range(NB):
                        sp.dma_start(o[b * HEADS:(b + 1) * HEADS, 0:vw],
                                     PN[SROW + b:SROW + b + 1, base:base + vw].to_broadcast([HEADS, vw])).then_inc(v0_here, 16)
                    reach(sp, upd, 2 * CHUNKS + 2)
                    out = OS[kind == "b"]
                    sp.dma_start(out[:, 0:vw], o[:, 0:vw]).then_inc(stored, 16)
                    wait_alone(sp, stored, 16)
                    tile0 = (TILES - 1) * P
                    with nc.allow_non_contiguous_dma(reason="a few thousand elements"):
                        for h in range(HEADS):
                            c = h // 2 + (4 if kind == "b" else 0)
                            v0 = (h // 4) * HD if kind == "b" else 0
                            row = tile0 + (h % 2) * HD
                            sp.dma_start(MT[row:row + HD, c * P + N_META:c * P + N_META + NB],
                                         out.rearrange("(b h) n -> h n b", h=HEADS)[h, v0:v0 + HD, :]).then_inc(stored, 16)
                    wait_alone(sp, stored, 16 * (1 + HEADS))

                @block.gpsimd
                def _(pool):
                    def chunk(c, p, i, n):
                        if attn:
                            reach(pool, pv_ps, n["chunk"].at())
                        else:
                            reach(pool, turned, n["seq"].at())
                        pool.tensor_copy(run_now[p][:], runs[:, :, ds(c, 1)].rearrange("p b o -> p (b o)")).then_inc(idx_done, 1)
                        wait_alone(pool, idx_done, n["chunk"].at(1))
                        for b in range(NB):
                            at = bass.IndirectOffsetOnAxis(ap=run_now[p][:, b:b + 1], axis=0)
                            pool.indirect_dma_start(kv[:, p, b, 0:RUN * width], None, pool_rows, at).then_inc(kv_here[p], 16)
                            if kind == "b":
                                pool.indirect_dma_start(lf[:, p, b, :], None, CACHE_LF, at).then_inc(kv_here[p], 16)

                    run(pool, chunk)

                @block.tensor
                def _(pe):
                    pe.sem_inc(turned, NB + 1)
                    for semaphore, first in ((qk, 1), (s_full, 1), (pt_ps, 1), (pv_ps, 2)):
                        pe.sem_inc(semaphore, first)
                    for b in range(NB):
                        ins = pe.matmul(S[1][0:BH, 0:1], heads_of(q, slice(0, kd), b, BH if attn else P), knew[0:kd, b:b + 1], start=(b == 0),
                                        stop=(b == NB - 1 and kind != "a"))
                    ins.then_inc(qk, 1)
                    if kind == "a":
                        pe.matmul(S[1][0:BH, 0:1], expand[:], work[:, NEW:NEW + 1], start=False, stop=True).then_inc(s_full, 1)
                    if kind == "i":
                        reach(pe, s_read, 1)
                        pe.matmul(pw[0:NB, 0:1], w_sel[0:BH, 0], relu[0:BH, 0:1], start=True, stop=True).then_inc(w_ps, 1)

                    def turn_keys(p, b, n):
                        reach(pe, kt_copied, n["seq"].at(b))
                        keys = kv[:, p, b, 0:RUN * width]
                        for r in range(nblk):
                            at = r * max(width, P)
                            ins = pe.transpose(tr[b % 2][:, r * P:(r + 1) * P], keys[:, at:at + P], ident[:])
                        ins.then_inc(turned, 1)

                    def products(p, b, n):
                        reach(pe, kt_copied, n["seq"].at(b + 2))
                        out = S[p][0:BH, :]
                        if attn:
                            ins = pe.matmul(out, heads_of(q, slice(0, P), b), kT[:, b % 2, :], start=(b == 0), stop=False)
                        else:
                            ins = pe.matmul(S[p][:, 0:2 * P], q_i[:, b * P:(b + 1) * P], kT[:, b % 2, 0:2 * P], start=(b == 0),
                                            stop=(b == NB - 1))
                        ins.then_inc(qk, 1)

                    def chunk(c, p, i, n):
                        out = S[p][0:BH, :]
                        wait_alone(pe, kv_here[p], (i + 1) * (16 * NB * (2 if kind == "b" else 1)))
                        turn_keys(p, 0, n)
                        for b in range(NB):
                            if b + 1 < NB:
                                turn_keys(p, b + 1, n)
                            if b == 0:
                                reach(pe, s_read, n["chunk"].at())
                            products(p, b, n)
                        if kind == "b":
                            reach(pe, lf_step, n["lf"].at(5))
                            for r in range(RUN - 1):
                                pe.matmul(out[:, r * P:(r + 1) * P], lf_r[:, r, :], ident[:], start=False, stop=False)
                            pe.matmul(out, lf_r[:, RUN - 1, :], after[:].unsqueeze(1).to_broadcast([P, RUN, P]), start=False, stop=False)
                            pe.matmul(out, lf_later[:], ones[:].unsqueeze(1).to_broadcast([P, RUN, P]), start=False, stop=True).then_inc(s_full, 1)
                        elif kind == "a":
                            pe.matmul(out, expand[:], work[:, ds(c * CHUNK_W, CHUNK)].rearrange("p (n r) -> p r n", r=RUN),
                                      start=False, stop=True).then_inc(s_full, 1)
                        else:
                            reach(pe, s_read, n["chunk"].at(2))
                            wait_alone(pe, w_read, n["chunk"].at(1))
                            for g in range(2):
                                ins = pe.matmul(pw[0:NB, g * 2 * P:(g + 1) * 2 * P], w_sel[:, g], relu[:], start=True, stop=True)
                            ins.then_inc(w_ps, 1)
                        if attn:
                            reach(pe, s_read, n["chunk"].at(2))
                            reach(pe, pt_copied, n["chunk"].at())
                            for r in range(RUN):
                                ins = pe.transpose(pt[:, r * BH:(r + 1) * BH], prob[:, r * P:(r + 1) * P], ident[0:BH, 0:BH])
                            ins.then_inc(pt_ps, 1)
                            reach(pe, pt_copied, n["chunk"].at(1))
                            reach(pe, upd, n["upd"].at())
                            for b in range(NB):
                                for r in range(RUN):
                                    at = r * width + vcol
                                    ins = pe.matmul(po[0:BH, 0:vw], heads_of(pT[:, r, :], slice(0, P), b), kv[:, p, b, at:at + vw],
                                                    start=(b == 0 and r == 0), stop=(b == NB - 1 and r == RUN - 1))
                            ins.then_inc(pv_ps, 1)

                    run(pe, chunk)

                @block.scalar
                def _(act):
                    act.sem_inc(kt_copied, 2)
                    act.sem_inc(pt_copied, 1)
                    if not attn:
                        act.sem_inc(s_read, 1)
                    if kind == "i":
                        reach(act, qk, 1)
                        act.activation(relu[0:BH, 0:1], S[1][0:BH, 0:1], ACT.Relu, scale=HD ** -0.5 * HEADS ** -0.5).then_inc(s_read, 1)

                    def chunk(c, p, i, n):
                        for b in range(NB):
                            reach(act, turned, n["seq"].at(b + 1 + NB))
                            reach(act, qk, n["seq"].at(b))
                            act.activation(kT[:, b % 2, 0:nblk * P], tr[b % 2][:, 0:nblk * P], ACT.Copy).then_inc(kt_copied, 1)
                        if kind == "i":
                            reach(act, qk, n["seq"].at(NB + 1))
                            act.wait_ge(w_ps, n["chunk"].at(1))
                            act.activation(relu[:], S[p][:, 0:2 * P], ACT.Relu, scale=HD ** -0.5 * HEADS ** -0.5).then_inc(s_read, 1)
                            return
                        act.wait_ge(mx, n["mx"].at(3 + 1))
                        reach(act, upd, n["upd"].at())
                        act.activation(shrink[:], m_old[:], ACT.Exp, bias=neg_m[:]).then_inc(shrunk, 1)
                        reach(act, pt_ps, n["chunk"].at())
                        act.activation(prob[:], S[p][0:BH, :], ACT.Exp, bias=neg_m[:], accum_out=den_c[:]).then_inc(s_read, 1)
                        reach(act, pt_ps, n["chunk"].at(1))
                        reach(act, pv_ps, n["chunk"].at(1))
                        act.activation(pT[:].rearrange("p r (b x) -> p r b x", x=BH + HEADS)[:, :, :, 0:HEADS],
                                       pt[:, 0:RUN * BH].rearrange("p (r b h) -> p r b h", r=RUN, b=NB), ACT.Copy).then_inc(pt_copied, 1)

                    run(act, chunk)

                @block.vector
                def _(v):
                    v.sem_inc(lf_step, 1)
                    v.sem_inc(upd, 1)
                    if attn:
                        v.sem_inc(s_read, 1)
                    if kind == "i":
                        v.wait_ge(w_ps, 1)
                        v.tensor_copy(scores[:, NEW:NEW + 1], pw[0:NB, 0:1]).then_inc(w_read, 1)
                    else:
                        v.memset(den[:], 1.0).then_inc(mx, 1)
                        reach(v, s_full if kind == "a" else qk, 1)
                        v.tensor_copy(m_old[:], S[1][0:BH, 0:1]).then_inc(s_read, 1)
                        v.wait_ge(v0_here, 16 * NB)

                    full = {"a": 2, "b": 1, "i": 0}[kind]

                    def chunk(c, p, i, n):
                        if kind == "i":
                            v.wait_ge(w_ps, n["chunk"].at(2))
                            v.tensor_copy(scores[:, ds(c * CHUNK_W, CHUNK)].rearrange("p (n j g) -> p g j n", j=2, g=2),
                                          pw[0:NB, :].rearrange("p (g j n) -> p g j n", g=2, j=2)).then_inc(w_read, 1)
                            return
                        if kind == "b":
                            v.wait_ge(kv_here[p], (i + 1) * (32 * NB))
                            reach(v, s_full, n["chunk"].at())
                            reach(v, lf_step, n["lf"].at())
                            v.tensor_tensor(lf_later[:], lf_later[:], lf_r[:, RUN - 1, :], ALU.add).then_inc(lf_step, 1)
                            mine = lf[:, p].rearrange("p b (r h) -> p r b h", r=RUN)
                            sums = lf_r[:].rearrange("p r (b h) -> p r b h", b=NB)
                            reach(v, lf_step, n["lf"].at(1))
                            v.tensor_copy(sums[:, 2], mine[:, 3]).then_inc(lf_step, 1)
                            for k, (to, frm) in enumerate(((1, 2), (0, 1), (3, 0))):
                                reach(v, lf_step, n["lf"].at(2 + k))
                                v.tensor_tensor(sums[:, to], sums[:, frm], mine[:, frm], ALU.add).then_inc(lf_step, 1)
                        reach(v, s_full, n["chunk"].at(full))
                        v.reduce_max(m_new[:], S[p][0:BH, :], AX.X).then_inc(mx, 1)
                        reach(v, s_read, n["chunk"].at(1))
                        v.wait_ge(mx, n["mx"].at(2))
                        v.tensor_tensor(m_new[:], m_new[:], m_old[:], ALU.max).then_inc(mx, 1)
                        v.wait_ge(mx, n["mx"].at(3))
                        v.tensor_scalar(neg_m[:], m_new[:], -1.0, None, ALU.mult).then_inc(mx, 1)
                        v.wait_ge(shrunk, n["chunk"].at(1))
                        v.tensor_copy(m_old[:], m_new[:]).then_inc(mx, 1)
                        reach(v, s_read, n["chunk"].at(2))
                        reach(v, upd, n["upd"].at())
                        v.wait_ge(mx, n["mx"].at(5))
                        v.scalar_tensor_tensor(out=den[:], in0=den[:], scalar=shrink[:], in1=den_c[:], op0=ALU.mult, op1=ALU.add)\
                            .then_inc(upd, 1)
                        reach(v, pv_ps, n["chunk"].at(2))
                        v.scalar_tensor_tensor(out=o[:, 0:vw], in0=o[:, 0:vw], scalar=shrink[:], in1=po[0:BH, 0:vw],
                                               op0=ALU.mult, op1=ALU.add).then_inc(upd, 1)

                    run(v, chunk)
                    if attn:
                        reach(v, upd, 2 * CHUNKS)
                        v.reciprocal(rden[:], den[:]).then_inc(upd, 1)
                        reach(v, upd, 2 * CHUNKS + 1)
                        v.tensor_scalar(o[:, 0:vw], o[:, 0:vw], rden[:], None, ALU.mult).then_inc(upd, 1)

        walk("i")

        with nc.Block() as block, nc.semaphore("d_moved") as moved, nc.semaphore("d_total_ps") as total_ps:
            total = pw[:, 0:1]

            @block.sync
            def _(sp):
                sp.dma_start(SC, scores[:]).then_inc(moved, 16)
                sp.wait_ge(moved, 16)
                sp.dma_start(spread[:], SC.rearrange("b (c n) -> (b c) n", n=CHUNK_W)).then_inc(moved, 16)
                sp.wait_ge(topk_step, 3 * BITS + 8)
                sp.dma_start(SC.rearrange("b (c n) -> (b c) n", n=CHUNK_W), chosen[:]).then_inc(moved, 16)
                sp.wait_ge(moved, 48)
                sp.dma_start(work[0:NB, :], SC).then_inc(moved, 16)
                sp.wait_ge(moved, 64)

            @block.tensor
            def _(pe):
                def add_up(k, who, counted):
                    pe.wait_ge(topk_step, counted)
                    pe.matmul(total, who[:], count[:], start=True, stop=True).then_inc(total_ps, 1)

                for k in range(BITS):
                    add_up(k, same, 3 * k + 2)
                add_up(BITS, same, 3 * BITS + 2)
                add_up(BITS + 1, sooner, 3 * BITS + 4)

            @block.vector
            def _(v):
                least = cand[:].bitcast(F32)
                v.memset(cand[:], 0).then_inc(topk_step, 1)
                v.wait_ge(moved, 32)
                for k in range(BITS):
                    v.wait_ge(topk_step, 3 * k + 1)
                    count_at_least(v, chosen[:], spread[:], cand[:], count[:]).then_inc(topk_step, 1)
                    v.wait_ge(total_ps, k + 1)
                    judge(v, k, total, miss[:]).then_inc(topk_step, 1)
                    v.wait_ge(topk_step, 3 * k + 3)
                    next_candidate(v, k, miss[:], cand[:]).then_inc(topk_step, 1)
                done = 3 * BITS + 1
                v.wait_ge(topk_step, done)
                v.tensor_scalar(chosen[:], spread[:], least, 0.0, ALU.is_gt, ALU.add, accum_out=count[:]).then_inc(topk_step, 1)
                v.wait_ge(total_ps, BITS + 1)
                v.tensor_scalar(left[:], total, -1.0, float(TOPK), ALU.mult, ALU.add).then_inc(topk_step, 1)
                v.wait_ge(topk_step, done + 2)
                v.tensor_scalar(chosen[:], spread[:], least, 0.0, ALU.is_equal, ALU.add, accum_out=count[:]).then_inc(topk_step, 1)
                v.wait_ge(topk_step, done + 3)
                v.wait_ge(total_ps, BITS + 2)
                v.tensor_tensor_scan(ties[:], chosen[:], chosen[:], total, ALU.add, ALU.max).then_inc(topk_step, 1)
                v.wait_ge(topk_step, done + 4)
                v.scalar_tensor_tensor(out=ties[:], in0=ties[:], scalar=left[:], in1=chosen[:], op0=ALU.is_gt, op1=ALU.mult)\
                    .then_inc(topk_step, 1)
                v.wait_ge(topk_step, done + 5)
                v.scalar_tensor_tensor(out=chosen[:], in0=spread[:], scalar=least, in1=ties[:], op0=ALU.is_lt, op1=ALU.add)\
                    .then_inc(topk_step, 1)
                v.wait_ge(topk_step, done + 6)
                v.tensor_scalar(chosen[:], chosen[:], FAR, None, ALU.mult).then_inc(topk_step, 1)

        walk("a")
        walk("b")


def build_program(nc, a, o):
    def scratch(name, shape):
        return nc.dram_tensor(f"dram_{name}", shape, F32, kind="Internal").ap()

    QTA = scratch("QTA", [ROWS, 8 * P])
    QTB = scratch("QTB", [TILES * AUG, 8 * P])
    HN = scratch("HN", [ROWS, D])
    MT = scratch("MT", [ROWS, D])
    H1T = scratch("H1T", [D, ROWS])
    OS = [scratch(f"OS{k}", [BH, P]) for k in range(2)]
    SC = scratch("SC", [NB, CHUNKS * CHUNK_W])
    PN, Y = o["PN"], o["Y"]
    with ExitStack() as consts:
        ident = consts.enter_context(nc.sbuf_tensor("ident", [P, P], F32))
        ones = consts.enter_context(nc.sbuf_tensor("ones", [P, P], F32))
        with ExitStack() as prompt:
            def sb(name, shape):
                return prompt.enter_context(nc.sbuf_tensor(name, shape, F32))

            split = {n: prompt.enter_context(nc.sbuf_tensor(n, [P, ROWS], F32R)) for n in ("ka_high", "ka_low", "ki_high", "ki_low")}
            keep = dict(split, ident=ident, ones=ones, tri=sb("tri", [P, P]),
                        kbT=sb("kbT", [P, 2, ROWS]), va=sb("va", [P, TILES, HD]), vb=sb("vb", [P, TILES, 2, HD]))
            project(nc, a["x_rows"], a["rope"], a["w_in"], a["ln_emb_g"], a["ln_emb_b"], a["b_forget"], a["matrices"],
                    PN, QTA, QTB, HN, keep)
            attend(nc, PN, QTA, QTB, a["mask"], MT, keep)
        keep = dict(ident=ident, ones=ones)
        decode(nc, PN, a["page_table"], a["cache_a"], a["cache_i"], a["cache_b"], a["cache_lf"], a["matrices"], a["pmod"],
               a["expand"], a["sequences"], SC, OS, MT, keep)
        mix_out(nc, MT, HN, a["w_o"], a["ln1_g"], a["ln1_b"], H1T, keep)
        feed_forward(nc, H1T, a["w_gate"], a["w_up"], a["w_down"], a["ln2_g"], a["ln2_b"], Y, keep)


def shape_constants():
    pos = np.zeros(ROWS, np.float32)
    pos[:TOTAL] = np.arange(TOTAL)
    pos[TOTAL:ALL] = PAST
    half = ROPE // 2
    inv = (np.float32(500000.0) ** (-np.arange(half, dtype=np.float32) / np.float32(half))).astype(np.float32)
    angle = (pos[:, None] * inv).astype(np.float32).astype(np.float64)
    cos, sin = np.cos(angle).astype(np.float32), np.sin(angle).astype(np.float32)
    square = np.ones((P, P), np.float32)
    expand = np.zeros((P, BH), np.float32)
    for b in range(NB):
        expand[b, b * HEADS:(b + 1) * HEADS] = 1.0
    seq, chunk = np.arange(P) // CHUNKS, np.arange(P) % CHUNKS
    same = seq[:, None] == seq[None, :]
    behind = np.arange(2 * ROWS)[None, :] - ROWS > np.arange(P)[:, None]
    return dict(
        rope=np.concatenate([cos, cos, -sin, sin], 1),
        matrices=np.stack([np.eye(P, dtype=np.float32), np.triu(square), square, np.tril(square, -1)]),
        mask=np.where(behind, np.float32(NEG), np.float32(0.0)).astype(np.float32),
        pmod=(np.arange(P) % UNITS).astype(np.float32)[:, None].copy(),
        expand=expand,
        sequences=np.stack([same, same & (chunk[:, None] < chunk[None, :])]).astype(np.float32),
    )


def kernel(x_prompt, x_sample, cache_a_kv, cache_idx_k, cache_b_kv, cache_b_logf, page_table, meta, ln_emb_g, ln_emb_b,
           w_in, b_forget, w_o, ln1_g, ln1_b, w_gate, w_up, w_down, ln2_g, ln2_b):
    import concourse.bacc as bacc
    from concourse.bass_utils import run_bass_kernel_spmd

    def arr(x):
        return np.ascontiguousarray(x)

    pad = np.zeros((ROWS - ALL, D), np.float32)
    arrays = dict(
        x_rows=np.concatenate([arr(meta), arr(x_prompt)[0], arr(x_sample)[:, 0], pad], 0),
        cache_a=arr(cache_a_kv).reshape(-1, RUN * 2 * HD), cache_i=arr(cache_idx_k).reshape(-1, RUN * HD),
        cache_b=arr(cache_b_kv).reshape(-1, RUN * 4 * HD), cache_lf=arr(cache_b_logf).reshape(-1, RUN * HEADS),
        page_table=arr(page_table), ln_emb_g=arr(ln_emb_g), ln_emb_b=arr(ln_emb_b), w_in=arr(w_in)[0], b_forget=arr(b_forget),
        w_o=arr(w_o)[0], ln1_g=arr(ln1_g)[0], ln1_b=arr(ln1_b)[0], w_gate=arr(w_gate)[0], w_up=arr(w_up)[0],
        w_down=arr(w_down)[0], ln2_g=arr(ln2_g)[0], ln2_b=arr(ln2_b)[0], **shape_constants())

    nc = bacc.Bacc("TRN2", target_bir_lowering=False, num_devices=1)
    arrays = {f"in_{n}": x for n, x in arrays.items()}
    ins = {n[3:]: nc.dram_tensor(n, x.shape, mybir.dt.from_np(x.dtype), kind="ExternalInput").ap() for n, x in arrays.items()}
    outs = {n: nc.dram_tensor(f"out_{n}", shape, F32, kind="ExternalOutput").ap() for n, shape in (("PN", (ROWS, N_IN)), ("Y", (ROWS, D)))}
    build_program(nc, ins, outs)
    got = run_bass_kernel_spmd(nc, [arrays], core_ids=[0]).results[0]
    pn, y = got["out_PN"], got["out_Y"]

    def rows(first, last, c0, c1, *shape):
        return np.ascontiguousarray(pn[first:last, c0:c1]).reshape(shape)

    n = N_SAMPLE
    return (y[N_META:TOTAL][None], y[TOTAL:ALL][:, None],
            rows(0, TOTAL, KA, KA + 2 * HD, 1, 1, TOTAL, 2, 1, HD), rows(0, TOTAL, KI, KI + HD, 1, 1, TOTAL, HD),
            rows(0, TOTAL, KB, KB + 4 * HD, 1, 1, TOTAL, 2, 2, HD), rows(0, TOTAL, FL, FL + HEADS, 1, 1, TOTAL, HEADS),
            rows(TOTAL, ALL, KA, KA + 2 * HD, 1, n, 1, 2, 1, HD), rows(TOTAL, ALL, KI, KI + HD, 1, n, 1, HD),
            rows(TOTAL, ALL, KB, KB + 4 * HD, 1, n, 1, 2, 2, HD), rows(TOTAL, ALL, FL, FL + HEADS, 1, n, 1, HEADS))
```
